# Optimizing a Trainium2 kernel written in Bass

```python
import math
import jax, jax.numpy as jnp
from jax import lax
import numpy as np

D_MODEL = 1024
BATCH = 1
SEQ = 512
DEPTH = 1

CHUNK = 64
N_META = 16

N_HEADS = 8
HEAD_DIM = 64
ATTN_WIDTH = N_HEADS * HEAD_DIM
Q_BLOCK = 128

POOL_WINDOWS = (2, 4, 8, 16)
POOL_GROUPS = len(POOL_WINDOWS)
POOL_WIDTH = D_MODEL // 2
POOL_GROUP_DIM = POOL_WIDTH // POOL_GROUPS

N_BRANCHES = 2

Q_OFF = 0
K_OFF = Q_OFF + ATTN_WIDTH
V_OFF = K_OFF + ATTN_WIDTH
F_OFF = V_OFF + ATTN_WIDTH
P_OFF = F_OFF + N_HEADS
G_OFF = P_OFF + POOL_WIDTH
IN_WIDTH = G_OFF + N_BRANCHES * D_MODEL

N_EXPERT_GROUPS = 4
EXPERTS_PER_GROUP = 8
EXPERT_HIDDEN = 256
TOP_K_EXPERTS = 2

RMS_EPS = 1e-6

kernel_name = "hybrid_fox_pool_hiermoe_block"

def rmsnorm(x, g):
    xf = x.astype(jnp.float32)
    y = xf * lax.rsqrt(jnp.mean(xf * xf, axis=-1, keepdims=True) + RMS_EPS)
    return (y * g.astype(jnp.float32)).astype(x.dtype)

def forgetting_attention(q, k, v, fcum):
    L = q.shape[2]
    n_blocks = -(-L // Q_BLOCK)
    pad = n_blocks * Q_BLOCK - L
    q = jnp.pad(q, ((0, 0), (0, 0), (0, pad), (0, 0)))
    k = jnp.pad(k, ((0, 0), (0, 0), (0, pad), (0, 0)))
    v = jnp.pad(v, ((0, 0), (0, 0), (0, pad), (0, 0)))
    fcum = jnp.pad(fcum, ((0, 0), (0, 0), (0, pad)))
    scale = 1.0 / math.sqrt(HEAD_DIM)
    outs = []
    for i in range(n_blocks):
        lo, hi = i * Q_BLOCK, (i + 1) * Q_BLOCK
        qb, kb, vb = q[:, :, lo:hi], k[:, :, :hi], v[:, :, :hi]
        s = jnp.einsum('bhqd,bhkd->bhqk', qb, kb).astype(jnp.float32) * scale
        s = s + (fcum[:, :, lo:hi, None] - fcum[:, :, None, :hi])
        mask = jnp.arange(hi)[None, :] <= (lo + jnp.arange(Q_BLOCK))[:, None]
        s = jnp.where(mask[None, None], s, -jnp.inf)
        p = jax.nn.softmax(s, axis=-1).astype(vb.dtype)
        outs.append(jnp.einsum('bhqk,bhkd->bhqd', p, vb))
    return jnp.concatenate(outs, axis=2)[:, :, :L]

def multiscale_pool(u, w_pool, pool_scale):
    B, L, C = u.shape
    ug = u.reshape(B, L, POOL_GROUPS, POOL_GROUP_DIM)
    cs = jnp.cumsum(ug.astype(jnp.float32), axis=1)
    cs = jnp.concatenate([jnp.zeros_like(cs[:, :1]), cs], axis=1)
    hi = jnp.arange(1, L + 1)
    windows = jnp.array(POOL_WINDOWS, dtype=jnp.int32)
    lo = jnp.maximum(hi[:, None] - windows[None, :], 0)
    grp = jnp.arange(POOL_GROUPS)[None, :]
    count = (hi[:, None] - lo).astype(jnp.float32)[None, :, :, None]
    mean = (cs[:, 1:] - cs[:, lo, grp]) / count
    mixed = (mean - ug.astype(jnp.float32)).astype(u.dtype)
    y = jnp.einsum('blgc,gcd->blgd', mixed, w_pool).reshape(B, L, C)
    return y * pool_scale

def hierarchical_moe(x2, w_group, b_group, w_router, b_router, w1, w3, w2):
    T = x2.shape[0]
    g_logits = (x2 @ w_group).astype(jnp.float32) + b_group.astype(jnp.float32)
    g_prob = jax.nn.softmax(g_logits, axis=-1)
    g_top, g_idx = lax.top_k(g_prob, 1)
    e_logits = ((x2 @ w_router).astype(jnp.float32) + b_router.astype(jnp.float32)
                ).reshape(T, N_EXPERT_GROUPS, EXPERTS_PER_GROUP)
    e_sel = jnp.take_along_axis(e_logits, g_idx[:, :, None], axis=1)[:, 0]
    e_prob = jax.nn.softmax(e_sel, axis=-1)
    e_top, e_idx = lax.top_k(e_prob, TOP_K_EXPERTS)
    e_w = e_top / jnp.sum(e_top, axis=-1, keepdims=True) * g_top
    w_within = jnp.sum(jax.nn.one_hot(e_idx, EXPERTS_PER_GROUP, dtype=jnp.float32)
                       * e_w[..., None], axis=1)
    combine = (jax.nn.one_hot(g_idx[:, 0], N_EXPERT_GROUPS, dtype=jnp.float32)[:, :, None]
               * w_within[:, None, :]).astype(x2.dtype)
    y = jnp.zeros_like(x2)
    for g in range(N_EXPERT_GROUPS):
        h1 = jnp.einsum('td,edf->tef', x2, w1[g])
        h3 = jnp.einsum('td,edf->tef', x2, w3[g])
        hh = jax.nn.silu(h1) * h3 * combine[:, g, :, None]
        y = y + jnp.einsum('tef,efd->td', hh, w2[g])
    return y

def setup_inputs(seed: int = 0) -> dict:
    key = jax.random.key(seed)
    ks = jax.random.split(key, 20)
    f32 = jnp.float32
    D, G, E, F = D_MODEL, N_EXPERT_GROUPS, EXPERTS_PER_GROUP, EXPERT_HIDDEN
    nrm = lambda k, shape, fan_in: jax.random.normal(k, shape, f32) * (fan_in ** -0.5)
    return {
        "x": jax.random.normal(ks[0], (BATCH, SEQ, D), f32),
        "meta_tokens": jax.random.normal(ks[1], (N_META, D), f32),
        "norm_mix_g": 1.0 + 0.05 * jax.random.normal(ks[2], (DEPTH, D), f32),
        "w_in": nrm(ks[3], (DEPTH, D, IN_WIDTH), D),
        "b_forget": jax.random.uniform(ks[4], (DEPTH, N_HEADS), f32, 3.0, 6.0),
        "q_norm_g": 1.0 + 0.05 * jax.random.normal(ks[5], (DEPTH, HEAD_DIM), f32),
        "k_norm_g": 1.0 + 0.05 * jax.random.normal(ks[6], (DEPTH, HEAD_DIM), f32),
        "w_up_attn": nrm(ks[7], (DEPTH, ATTN_WIDTH, D), ATTN_WIDTH),
        "w_pool": nrm(ks[8], (DEPTH, POOL_GROUPS, POOL_GROUP_DIM, POOL_GROUP_DIM), POOL_GROUP_DIM),
        "pool_scale": 1.0 + 0.1 * jax.random.normal(ks[9], (DEPTH, POOL_WIDTH), f32),
        "w_up_pool": nrm(ks[10], (DEPTH, POOL_WIDTH, D), POOL_WIDTH),
        "w_out": nrm(ks[11], (DEPTH, D, D), D),
        "norm_ffn_g": 1.0 + 0.05 * jax.random.normal(ks[12], (DEPTH, D), f32),
        "w_group": nrm(ks[13], (DEPTH, D, G), D),
        "b_group": 0.01 * jax.random.normal(ks[14], (DEPTH, G), f32),
        "w_router": nrm(ks[15], (DEPTH, D, G * E), D),
        "b_router": 0.01 * jax.random.normal(ks[16], (DEPTH, G * E), f32),
        "w1": nrm(ks[17], (DEPTH, G, E, D, F), D),
        "w3": nrm(ks[18], (DEPTH, G, E, D, F), D),
        "w2": nrm(ks[19], (DEPTH, G, E, F, D), F),
    }

def reference(x, meta_tokens, norm_mix_g, w_in, b_forget, q_norm_g, k_norm_g, w_up_attn,
              w_pool, pool_scale, w_up_pool, w_out, norm_ffn_g, w_group, b_group, w_router,
              b_router, w1, w3, w2):
    B = x.shape[0]
    meta = jnp.broadcast_to(meta_tokens.astype(x.dtype)[None], (B, N_META, D_MODEL))
    h = jnp.concatenate([meta, x], axis=1)
    L = h.shape[1]
    for l in range(DEPTH):
        hn = rmsnorm(h, norm_mix_g[l])
        proj = hn @ w_in[l]
        q = rmsnorm(proj[..., Q_OFF:K_OFF].reshape(B, L, N_HEADS, HEAD_DIM), q_norm_g[l])
        k = rmsnorm(proj[..., K_OFF:V_OFF].reshape(B, L, N_HEADS, HEAD_DIM), k_norm_g[l])
        v = proj[..., V_OFF:F_OFF].reshape(B, L, N_HEADS, HEAD_DIM)
        log_f = jax.nn.log_sigmoid(proj[..., F_OFF:P_OFF].astype(jnp.float32)
                                   + b_forget[l].astype(jnp.float32))
        fcum = jnp.cumsum(log_f, axis=1).transpose(0, 2, 1)
        o = forgetting_attention(q.transpose(0, 2, 1, 3), k.transpose(0, 2, 1, 3),
                                 v.transpose(0, 2, 1, 3), fcum)
        y_attn = o.transpose(0, 2, 1, 3).reshape(B, L, ATTN_WIDTH) @ w_up_attn[l]
        y_pool = multiscale_pool(proj[..., P_OFF:G_OFF], w_pool[l], pool_scale[l]) @ w_up_pool[l]
        gates = jax.nn.sigmoid(proj[..., G_OFF:].astype(jnp.float32)).astype(h.dtype)
        gates = gates.reshape(B, L, N_BRANCHES, D_MODEL)
        merged = gates[:, :, 0] * y_attn + gates[:, :, 1] * y_pool
        h = h + merged @ w_out[l]
        hn = rmsnorm(h, norm_ffn_g[l]).reshape(B * L, D_MODEL)
        y_ffn = hierarchical_moe(hn, w_group[l], b_group[l], w_router[l], b_router[l],
                                 w1[l], w3[l], w2[l])
        h = h + y_ffn.reshape(B, L, D_MODEL)
    return h[:, N_META:]


_drawn_inputs = setup_inputs


def setup_inputs(seed=0):
    import zlib

    import numpy as np

    out = dict(_drawn_inputs(seed))
    spreads = {}
    factors = {'q_norm_g': 3.275, 'k_norm_g': 3.395, 'b_group': 3.49, 'b_router': 4.338}
    for name, (base, spread) in spreads.items():
        noise = np.random.default_rng([zlib.crc32(name.encode()), seed]).standard_normal(out[name].shape)
        drawn = base * np.exp(spread * noise) if base else spread * noise
        out[name] = __import__('jax').numpy.asarray(drawn.astype(out[name].dtype))
    for name, factor in factors.items():
        out[name] = (out[name] * factor).astype(out[name].dtype)
    return out
```

```python
import concourse.bass as bass
from concourse import mybir

F32 = mybir.dt.float32
F32R = mybir.dt.float32r
I32 = mybir.dt.int32
U32 = mybir.dt.uint32
ALU = mybir.AluOpType
ACT = mybir.ActivationFunctionType
AX = mybir.AxisListType

P = 128
D = 1024
KD = D // P
SEQ = 512
NT = SEQ // P
META = 16
L = META + SEQ
HEADS, DH = 8, 64
PAIRS = HEADS // 2
AW = HEADS * DH
NG, NE = 4, 8
EXPERTS = NG * NE
F = 256
CAP = 64
BLOCKS = SEQ // CAP
WINDOWS = (2, 4, 8, 16)
EPS = 1e-6
SKIP = 65536.0
Q_OFF, K_OFF, V_OFF = 0, AW, 2 * AW
F_OFF = 3 * AW
P_OFF = F_OFF + HEADS
G_OFF = P_OFF + AW
CHUNKS = (P_OFF, V_OFF, K_OFF, Q_OFF)
CP, CV, CK, CQ = range(4)
SLOTS = 4
ROUNDS = EXPERTS // SLOTS

C_ID, C_TRI, C_TRS, C_ONE, C_MASK, C_SLOT = (P * i for i in range(6))
C_I8 = 6 * P
C_VA = C_I8 + NE
C_VB = C_VA + 2 * NT
C_HALF = C_VB + 2 * NT
C_END = C_HALF + 1
NB = len(WINDOWS)


def constants():
    import numpy as np

    i = np.arange(P)
    c = np.zeros((P, C_END), np.float32)
    c[:, C_ID:C_ID + P] = i[:, None] == i[None, :]
    c[:, C_TRI:C_TRI + P] = i[:, None] <= i[None, :]
    c[:, C_TRS:C_TRS + P] = i[:, None] < i[None, :]
    c[:, C_ONE:C_ONE + P] = 1
    c[:, C_MASK:C_MASK + P] = np.where(i[None, :] <= i[:, None], 0.0, -1e30)
    c[:, C_SLOT:C_SLOT + P] = i[None, :] % CAP
    c[:, C_I8:C_I8 + NE] = np.arange(NE)
    for t in range(NT):
        for k in range(2):
            c[:, C_VA + 2 * t + k] = 2 * (P * t + i) + 1
            c[:, C_VB + 2 * t + k] = 2 * (P * t + i + SEQ * k) + 1
    c[:, C_HALF] = np.where(i < CAP, -1, 0)
    b = np.zeros((P, 3, NB, P), np.float32)
    for g, w in enumerate(WINDOWS):
        ago = i[None, :] - i[:, None]
        b[:, 0, g] = ((ago >= 0) & (ago < w)) / w - (ago == 0)
        b[:, 1, g] = (ago + P < w) / w
        b[:META, 2, g] = (ago[:META] + META < w) / w
    return {"consts": c, "bands": b.reshape(P, 3 * NB * P)}


class Chain:

    def __init__(self, eng, sem):
        self.eng, self.sem, self.base, self.k = eng, sem, 0, 0

    def __call__(self, ins):
        ins.then_inc(self.sem, 1)
        self.k += 1
        self.eng.wait_ge(self.sem, self.base + self.k)

    def settle(self, base):
        self.base, self.k = base, 0


def program(nc, x, meta_tokens, norm_mix_g, w_in, b_forget, q_norm_g, k_norm_g, w_up_attn, w_pool,
            pool_scale, w_up_pool, w_out, norm_ffn_g, w_group, b_group, w_router, b_router, w1, w3, w2,
            consts, bands, out):
    frames = x[0].rearrange("(i p) d -> i p d", p=P)
    out_rows = out[0].rearrange("(i p) d -> i p d", p=P)
    win = w_in[0].rearrange("(k p) n -> p k n", p=P)
    wua = w_up_attn[0].rearrange("(k p) n -> p k n", p=P)
    wup = w_up_pool[0].rearrange("(k p) n -> p k n", p=P)
    wout = w_out[0].rearrange("(k p) n -> p k n", p=P)
    w1e = w1[0].rearrange("g e (h p c) f -> (g e) p h (c f)", h=2, c=4)
    w3e = w3[0].rearrange("g e (h p c) f -> (g e) p h (c f)", h=2, c=4)
    w2e = w2[0].rearrange("g e (j p) d -> (g e) p j d", p=P)
    hn2_rows = nc.dram_tensor("hn2_rows", [2 * SEQ, D // 2], F32).ap()
    y_rows = nc.dram_tensor("y_rows", [4 * SEQ, D // 2], F32).ap()
    nf_rows = nc.dram_tensor("nf_rows", [HEADS, L], F32).ap()
    nf_pairs = nf_rows.rearrange("(q a) s -> q (a s)", a=2)

    BASE = 16512
    KB = 1024

    def sb(name, shape, at, dt=F32):
        return nc.alloc_sbuf_tensor_at(name, shape, dt, offset=BASE + int(at * KB))

    cst = sb("cst", [P, C_END], 0)
    ident = cst[:, C_ID:C_ID + P]
    tri = cst[:, C_TRI:C_TRI + P]
    tri_strict = cst[:, C_TRS:C_TRS + P]
    ones = cst[:, C_ONE:C_ONE + P]
    small = [3.25]

    def keep(name, shape, dt=F32):
        n = 1
        for s in shape[1:]:
            n *= s
        t = sb(name, shape, small[0], dt)
        small[0] += -(-n * 4 // 32) * 32 / KB
        assert small[0] <= 11
        return t

    wf = keep("wf", [P, KD, HEADS])
    wf_hi = keep("wf_hi", [P, KD, HEADS], F32R)
    wf_lo = keep("wf_lo", [P, KD, HEADS], F32R)
    w_rt = keep("w_rt", [P, KD, NG + EXPERTS])
    bias_rt = keep("bias_rt", [P, NG + EXPERTS])
    bias_f = keep("bias_f", [P, HEADS])
    gain_q = keep("gain_q", [P, 1])
    gain_k = keep("gain_k", [P, 1])
    scale_pool = keep("scale_pool", [P, NB])
    ss = keep("ss", [P, NT + 1])
    rstd = keep("rstd", [P, NT + 1])
    nw1 = keep("nw1", [P, NT + 1])
    nw2 = keep("nw2", [P, NT + 1])
    nw3 = keep("nw3", [P, NT + 1])
    metaT = keep("metaT", [P, KD, META])
    ssh = keep("ssh", [P, 2, NT + 1, HEADS])
    rsh = keep("rsh", [P, 2, NT + 1, HEADS])
    nh1 = keep("nh1", [P, 2, NT + 1, HEADS])
    nh2 = keep("nh2", [P, 2, NT + 1, HEADS])
    fx = keep("fx", [P, NT + 1, HEADS])
    fa = keep("fa", [P, NT + 1, HEADS])
    fcum = keep("fcum", [P, NT, HEADS])
    mx = keep("mx", [P, 2])
    nmx = keep("nmx", [P, 2])
    rs = keep("rs", [P, 2, 2])
    rinv = keep("rinv", [P, 2])

    mov = [[sb(f"mov{b}{n}", [P, 2, 512], 11 + 8 * b + 4 * h, F32R) for h, n in enumerate(("hi", "lo"))]
           for b in range(2)]
    sta = [[sb(f"sta{b}{n}", [P, KD, P], 11 + 8 * b + 4 * h, F32R) for h, n in enumerate(("hi", "lo"))]
           for b in range(2)]
    xin = sb("xin", [P, NT, D], 27)
    gain_mix = sb("gain_mix", [P, D], 43)
    meta_in = sb("meta_in", [META, D], 116)
    junk = sb("junk", [P, D], 124)
    band = sb("band", [P, 3, NB, P], 27)
    mixT = sb("mixT", [P, NB, SEQ], 33)
    wpool = sb("wpool", [P, NB, P], 41)
    sq = sb("sq", [P, NT, 512], 154)
    sqm = sb("sqm", [META, 512], 162)
    nfT = sb("nfT", [HEADS, L], 43)
    qn = sb("qn", [P, NT, P], 27)
    kn = sb("kn", [P, NT, P], 29)
    knm = sb("knm", [META, P], 31)
    QT = sb("QT", [P, SEQ], 31.5)
    KT = sb("KT", [P, L], 33.5)
    sc = sb("sc", [P, 2, L], 35.75)
    pT = sb("pT", [P, 2, SEQ], 40)
    pTm = sb("pTm", [META, 2, P], 44)
    oN = sb("oN", [P, P], 45)
    smeta = sb("smeta", [P, 2, NT, META], 45.5)
    probs = sb("probs", [P, 2, 2, L], 194)
    nfb = sb("nfb", [P, 2, L], 202.5)
    land_b = [sb(f"land_b{c}", [P, KD, 512], at) for c, at in enumerate((50, 66, 162, 178))]
    land_s = [sb(f"land_s{b}", [P, KD, 256], 50 + 8 * b) for b in range(2)]
    land_e = [sb("land_e0", [P, KD, 512], 66), sb("land_e1", [P, KD, 512], 50)]
    hnT = [sb(f"hnT_{n}", [P, KD, L], 82 + 17 * h, F32R) for h, n in enumerate(("hi", "lo"))]
    brT = [sb(f"brT_{n}", [P, KD, SEQ], 82 + 16 * h, F32R) for h, n in enumerate(("hi", "lo"))]
    raw = sb("raw", [P, 4, NT, 512], 116)
    poolT = sb("poolT", [P, NB, SEQ], 116)
    rawm = sb("rawm", [META, 3, 512], 148)
    oT = sb("oT", [P, PAIRS, SEQ], 154)
    gates = sb("gates", [P, 2 * KD, SEQ], 162)
    mgT = [sb(f"mgT_{n}", [P, KD, SEQ], 124 + 16 * h, F32R) for h, n in enumerate(("hi", "lo"))]
    mg = [sb(f"mg{b}", [P, SEQ], 27 + 4 * b) for b in range(2)]
    mg2 = [sb(f"mg2{b}", [P, SEQ], 29 + 4 * b) for b in range(2)]
    h2 = sb("h2", [P, NT, D], 27)
    gain_ffn = sb("gain_ffn", [P, D], 11)
    hn2 = sb("hn2", [P, 2, D], 15)
    hn2T = sb("hn2T", [P, 2, KD, P], 106.5)
    rt = [114.5]

    def route(name, shape, dt=F32):
        n = 1
        for s in shape[1:]:
            n *= s
        t = sb(name, shape, rt[0], dt)
        rt[0] += -(-n * 4 // 32) * 32 / KB
        assert rt[0] <= 124
        return t

    lg = route("lg", [P, NT, NG + EXPERTS])
    gl8 = route("gl8", [P, NT, 8])
    top = route("top", [P, NT, 8])
    topi = route("topi", [P, NT, 8], U32)
    idf = route("idf", [P, NT, 2])
    gex = route("gex", [P, NT, NG])
    gtop = route("gtop", [P, NT])
    ohg = route("ohg", [P, NT, NG])
    esel = route("esel", [P, NT, NE])
    p2 = route("p2", [P, NT])
    r2 = route("r2", [P, NT])
    gate2 = route("gate2", [P, NT, 2])
    oh8 = route("oh8", [P, NT, 2, NE])
    chosen = route("chosen", [P, NT, EXPERTS])
    rank = route("rank", [P, 2 * NT])
    cmax = route("cmax", [P, 1])
    cmaxi = route("cmaxi", [P, 1], I32)
    skip = route("skip", [P, 2, EXPERTS])
    cand = route("cand", [P, NT * EXPERTS])
    idx = route("idx", [P, 2, EXPERTS], U32)
    gslot = route("gslot", [P, EXPERTS])
    pick = sb("pick", [P, 2 * NT, EXPERTS], 74)
    pickc = sb("pickc", [P, 2 * NT, EXPERTS], 75)
    vals = sb("vals", [P, 2 * NT, 3, EXPERTS], 76)
    rank1 = sb("rank1", [P, 2 * NT, P], 43)
    xg = [sb(f"xg{s}", [P, 512], 11 + 2 * s) for s in range(SLOTS)]
    xT = [sb(f"xT{b}", [P, 512], 19 + 2 * b) for b in range(2)]
    ye = [sb(f"ye{s}", [P, 512], 106.5 + 2 * s) for s in range(SLOTS)]
    hh = [sb(f"hh{b}", [P, P], 23 + b / 2) for b in range(2)]
    hhT = [sb(f"hhT{b}", [P, P], 24 + b / 2) for b in range(2)]
    ex = [sb(f"ex{b}", [P, P], 25 + b / 2) for b in range(2)]
    ixg = [sb(f"ixg{s}", [P, 1], 26 + s / 32, U32) for s in range(SLOTS)]
    ixs = [sb(f"ixs{s}", [P, 1], 26.125 + s / 32, U32) for s in range(SLOTS)]
    landed_flag = sb("landed_flag", [P, 1], 26.375)
    gcol = [sb(f"gcol{b}", [P, 1], 26.25 + b / 32) for b in range(2)]
    wslot_at = (82, 159.75, 183.75, 50)
    w13 = [sb(f"w13_{s}", [P, 2, 2, 4 * F], at) for s, at in enumerate(wslot_at)]
    w2s = [sb(f"w2s_{s}", [P, 2, D], at + 16) for s, at in enumerate(wslot_at)]
    yfin = sb("yfin", [P, 2, 2, D], 82)

    ps = [nc.alloc_psum_tensor(f"ps{b}", [P, 512], F32) for b in range(8)]

    def sem(name):
        return nc.alloc_semaphore(name)

    ld_x = [sem(f"ld_x{i}") for i in range(NT)]
    ld_first = sem("ld_first")
    ld_small = sem("ld_small")
    ld_b = [sem(f"ld_b{c}") for c in range(4)]
    ld_pool = sem("ld_pool")
    ld_s = [sem(f"ld_s{b}") for b in range(2)]
    ld_nf = sem("ld_nf")
    ld_nfb = sem("ld_nfb")
    ld_e = [sem(f"ld_e{b}") for b in range(2)]
    ld_h2 = sem("ld_h2")
    ld_gf = sem("ld_gf")
    ld_up = [sem(f"ld_up{s}") for s in range(SLOTS)]
    ld_dn = [sem(f"ld_dn{s}") for s in range(SLOTS)]
    ld_y = [sem(f"ld_y{b}") for b in range(2)]
    ld_half = sem("ld_half")
    st_hn2 = [sem(f"st_hn2{b}") for b in range(2)]
    st_out = sem("st_out")
    chain_v, chain_c, chain_e, chain_t = (sem(f"chain_{n}") for n in "vcet")
    chain_a, chain_g = sem("chain_a"), sem("chain_g")
    sq_sum = sem("sq_sum")
    var_ok = sem("var_ok")
    rs_est = sem("rs_est")
    hn_ok = sem("hn_ok")
    tp_done = sem("tp_done")
    hi_ok = sem("hi_ok")
    lo_ok = sem("lo_ok")
    wf_h, wf_l = sem("wf_h"), sem("wf_l")
    f_done, fx_ok, fe_ok, logf_ok = sem("f_done"), sem("fx_ok"), sem("fe_ok"), sem("logf_ok")
    mov_hi, mov_lo, mov_used = sem("mov_hi"), sem("mov_lo"), sem("mov_used")
    acc_done = sem("acc_done")
    acc_ev_a, acc_ev_v = sem("acc_ev_a"), sem("acc_ev_v")
    meta_done, meta_ev = sem("meta_done"), sem("meta_ev")
    fc_done, fc_ev = sem("fc_done"), sem("fc_ev")
    mix_done, mix_ev, pool_done, pool_ev = sem("mix_done"), sem("mix_ev"), sem("pool_done"), sem("pool_ev")
    qk_n = sem("qk_n")
    qk_t = sem("qk_t")
    q_ev, k_ev = sem("q_ev"), sem("k_ev")
    sm_done = sem("sm_done")
    s_done = sem("s_done")
    s_read = sem("s_read")
    e_done = sem("e_done")
    pt_done, pt_ev_a, pt_ev_v = sem("pt_done"), sem("pt_ev_a"), sem("pt_ev_v")
    pv_done, o_ev, ot_done, ot_ev = sem("pv_done"), sem("o_ev"), sem("ot_done"), sem("ot_ev")
    sta_hi, sta_lo = sem("sta_hi"), sem("sta_lo")
    g_done, g_ev, g_ok = sem("g_done"), sem("g_ev"), sem("g_ok")
    br_hi, br_lo = sem("br_hi"), sem("br_lo")
    up_done, up_read, mg_hi, mg_lo = sem("up_done"), sem("up_read"), sem("mg_hi"), sem("mg_lo")
    h2_ok = sem("h2_ok")
    hn2_ok, t2_done, t2_ev, lg_done = (sem(n) for n in ("hn2_ok", "t2_done", "t2_ev", "lg_done"))
    ge_in, ge_out, pe_in, pe_out = (sem(n) for n in ("ge_in", "ge_out", "pe_in", "pe_out"))
    ch_ok, cnt_done, cnt_ok = sem("ch_ok"), sem("cnt_done"), sem("cnt_ok")
    tab_in, tab_done, tab_ok = sem("tab_in"), sem("tab_done"), sem("tab_ok")
    xg_zero = sem("xg_zero")
    ga = [sem(f"ga{s}") for s in range(SLOTS)]
    sca = [sem(f"sca{s}") for s in range(SLOTS)]
    t_done, t_ev = sem("t_done"), sem("t_ev")
    up2_done, e2_done, hh_ok = sem("up2_done"), sem("e2_done"), sem("hh_ok")
    ht_done, ht_ev = sem("ht_done"), sem("ht_ev")
    dn_done, y_ev = sem("dn_done"), sem("y_ev")
    yf_ok = sem("yf_ok")
    passed = sem("passed")
    all_landed = sem("all_landed")

    def apart(eng):
        eng.sem_inc(passed, 1)

    def bc(ap, shape):
        return ap.to_broadcast(shape)

    N_SMALL = 11
    N_MOV_B = 4 * 4
    N_STA = 2 * KD + KD
    N_RT = NG + EXPERTS
    PAIR_STEPS = 1 + 3 * NT + NT
    EXPERT_STEPS = 2

    with nc.Block() as block:

        @block.sync
        def _(sp):
            sp.dma_start(cst[:, :], consts).then_inc(ld_first, 16)
            sp.dma_start(gain_mix[:, :], norm_mix_g.to_broadcast([P, D])).then_inc(ld_first, 16)
            sp.dma_start(meta_in[:, :], meta_tokens).then_inc(ld_first, 16)
            for i in range(NT):
                sp.dma_start(xin[:, i, :], frames[i]).then_inc(ld_x[i], 16)
            with nc.allow_non_contiguous_dma(reason="small weights, once"):
                small_loads = (
                    (wf[:, :, :], win[:, :, F_OFF:F_OFF + HEADS]),
                    (bias_f[:, :], b_forget.to_broadcast([P, HEADS])),
                    (gain_q[0:DH, :], q_norm_g.rearrange("a d -> d a")),
                    (gain_q[DH:P, :], q_norm_g.rearrange("a d -> d a")),
                    (gain_k[0:DH, :], k_norm_g.rearrange("a d -> d a")),
                    (gain_k[DH:P, :], k_norm_g.rearrange("a d -> d a")),
                    (scale_pool[:, :], pool_scale[0].rearrange("(g p) -> p g", p=P)),
                    (w_rt[:, :, 0:NG], w_group[0].rearrange("(k p) n -> p k n", p=P)),
                    (w_rt[:, :, NG:], w_router[0].rearrange("(k p) n -> p k n", p=P)),
                    (bias_rt[:, 0:NG], b_group.to_broadcast([P, NG])),
                    (bias_rt[:, NG:], b_router.to_broadcast([P, EXPERTS])),
                )
                assert len(small_loads) == N_SMALL
                for dst, src in small_loads:
                    sp.dma_start(dst, src).then_inc(ld_small, 16)
            for c, off in enumerate(CHUNKS):
                sp.dma_start(land_b[c][:, :, :], win[:, :, off:off + 512]).then_inc(ld_b[c], 16)
            sp.wait_ge(tp_done, 2 * NT + 1)
            sp.dma_start(band[:, :, :, :], bands.rearrange("p (a g t) -> p a g t", a=3, g=NB)).then_inc(ld_pool, 16)
            sp.dma_start(wpool[:, :, :], w_pool[0].rearrange("g c d -> c g d")).then_inc(ld_pool, 16)
            sp.wait_ge(mov_lo, N_MOV_B)
            sp.wait_ge(meta_done, 1)
            for b in range(2):
                sp.dma_start(land_s[b][:, :, :], win[:, :, G_OFF + 256 * b:G_OFF + 256 * (b + 1)]).then_inc(ld_s[b], 16)
            sp.wait_ge(fc_ev, 1)
            sp.dma_start(nf_rows, nfT[:, :]).then_inc(ld_nf, 16)
            sp.wait_ge(ld_nf, 16)
            nfb_flat = nfb[:, :, :].rearrange("p a s -> p (a s)")
            sp.dma_start(nfb_flat, nf_pairs[0:1, :].to_broadcast([P, 2 * L])).then_inc(ld_nfb, 16)
            with sp.Fori(1, PAIRS) as p:
                for b in range(2):
                    sp.wait_ge(sta_lo, p * 4 + (2 * b - 2))
                    sp.dma_start(land_s[b][:, :, :],
                                 win[:, :, bass.ds(p * 512 + (G_OFF + 256 * b), 256)]).then_inc(ld_s[b], 16)
                sp.wait_ge(s_read, p * NT)
                sp.dma_start(nfb_flat, nf_pairs[bass.ds(p, 1), :].to_broadcast([P, 2 * L])).then_inc(ld_nfb, 16)
            for q in range(4):
                b = q % 2
                sp.wait_ge(sta_lo, 2 * KD - 2 + 2 * q)
                sp.dma_start(land_s[b][:, 0:4, :], wua[:, :, 256 * q:256 * (q + 1)]).then_inc(ld_half, 16)
                sp.wait_ge(ld_half, 16 * (q + 1))
                sp.dma_start(land_s[b][:, 4:8, :], wup[:, :, 256 * q:256 * (q + 1)]).then_inc(ld_s[b], 16)
                if q == 0:
                    sp.dma_start(land_e[0][:, :, :], wout[:, :, 0:512]).then_inc(ld_e[0], 16)
            sp.wait_ge(sta_lo, N_STA)
            sp.dma_start(land_e[1][:, :, :], wout[:, :, 512:1024]).then_inc(ld_e[1], 16)
            sp.wait_ge(mg_lo, KD)
            for i in range(NT):
                sp.dma_start(h2[:, i, :], frames[i]).then_inc(ld_h2, 16)

            def load_expert(e, s, used=None):
                if used is not None:
                    sp.wait_ge(up2_done, used)
                sp.dma_start(w13[s][:, 0, :, :], w1e[bass.ds(e, 1)].rearrange("o p h f -> p (o h) f")).then_inc(ld_up[s], 16)
                sp.dma_start(w13[s][:, 1, :, :], w3e[bass.ds(e, 1)].rearrange("o p h f -> p (o h) f")).then_inc(ld_up[s], 16)
                if used is not None:
                    sp.wait_ge(dn_done, used)
                sp.dma_start(w2s[s][:, :, :], w2e[bass.ds(e, 1)].rearrange("o p j d -> p (o j) d")).then_inc(ld_dn[s], 16)

            sp.wait_ge(up_done, KD)
            for s in range(3):
                load_expert(s, s)
            sp.wait_ge(acc_done, 6 * NT)
            sp.dma_start(gain_ffn[:, :], norm_ffn_g.to_broadcast([P, D])).then_inc(ld_gf, 16)
            load_expert(3, 3)

            def load_round(r, e0):
                for s in range(SLOTS):
                    load_expert(sp.snap(r * SLOTS + s, min_val=0, max_val=EXPERTS - 1), s, e0 + (s - SLOTS + 1))

            with sp.Fori(1, ROUNDS) as r:
                load_round(r, r * SLOTS)
            sp.wait_ge(cnt_ok, 1)
            fullest = sp.value_load(cmaxi[0:1, 0:1], min_val=0, max_val=SEQ)
            with sp.Fori(1, BLOCKS) as blk:
                with sp.If(fullest > blk * CAP):
                    with sp.Fori(0, ROUNDS) as r:
                        load_round(r, blk * EXPERTS + r * SLOTS)
            sp.wait_ge(all_landed, 1)
            for i in range(NT):
                b = i % 2
                if i >= 2:
                    sp.wait_ge(yf_ok, i - 1)
                for k in range(2):
                    r0 = 2 * (SEQ * k + P * i)
                    sp.dma_start(yfin[:, b, k, :],
                                 y_rows[r0:r0 + 2 * P, :].rearrange("(p h) d -> p (h d)", h=2)).then_inc(ld_y[b], 16)
            for i in range(NT):
                sp.wait_ge(yf_ok, i + 1)
                sp.dma_start(out_rows[i], h2[:, i, :]).then_inc(st_out, 16)
            sp.wait_ge(st_out, 16 * NT)

        @block.gpsimd
        def _(pool):
            last_row, last_result = pool.to_reg(2 * SEQ - 1), pool.to_reg(4 * SEQ - 1)

            def gather(col, s, n, gathers=None, turned=None):
                if gathers is not None:
                    pool.wait_ge(ga[s], gathers)
                    pool.wait_ge(t_done, turned)
                    apart(pool)
                pool.tensor_copy(ixg[s][:, :], idx[:, 0, bass.ds(col, 1)]).then_inc(chain_g, 1)
                pool.wait_ge(chain_g, n)
                apart(pool)
                pool.indirect_dma_start(
                    out=xg[s][:, :], out_offset=None, in_=hn2_rows,
                    in_offset=bass.IndirectOffsetOnAxis(ap=ixg[s][:, 0:1], axis=0),
                    bounds_check=last_row, oob_is_err=False).then_inc(ga[s], 16)

            def scatter(e, col, s, n, scatters=None):
                pool.wait_ge(y_ev, e + 1)
                if scatters is not None:
                    pool.wait_ge(sca[s], scatters)
                apart(pool)
                pool.tensor_copy(ixs[s][:, :], idx[:, 1, bass.ds(col, 1)]).then_inc(chain_g, 1)
                pool.wait_ge(chain_g, n)
                apart(pool)
                pool.indirect_dma_start(
                    out=y_rows, out_offset=bass.IndirectOffsetOnAxis(ap=ixs[s][:, 0:1], axis=0),
                    in_=ye[s][:, :], in_offset=None,
                    bounds_check=last_result, oob_is_err=False).then_inc(sca[s], 16)

            def round_(r, e0, first=False, last=False):
                for s in range(SLOTS):
                    if not last:
                        gather(r * SLOTS + (SLOTS + s), s, e0 * 2 + (SLOTS + 2 * s + 1), e0 * 4 + 16, e0 + (s + 1))
                    scatter(e0 + s, r * SLOTS + s, s, e0 * 2 + (SLOTS + (s + 1 if last else 2 * s + 2)),
                            None if first else e0 * 4)

            pool.wait_ge(tab_ok, 1)
            pool.wait_ge(xg_zero, 1)
            for b in range(2):
                pool.wait_ge(st_hn2[b], 16 * (NT // 2))
            for s in range(SLOTS):
                gather(s, s, s + 1)
            round_(0, 0, first=True)
            with pool.Fori(1, ROUNDS - 1) as r:
                round_(r, r * SLOTS)
            round_(ROUNDS - 1, (ROUNDS - 1) * SLOTS, last=True)
            for s in range(SLOTS):
                pool.wait_ge(sca[s], 16 * ROUNDS)
            pool.wait_ge(cnt_ok, 1)
            fullest = pool.value_load(cmaxi[0:1, 0:1], min_val=0, max_val=SEQ)
            with pool.Fori(1, BLOCKS) as blk:
                with pool.If(fullest > blk * CAP):
                    e0 = blk * EXPERTS
                    pool.wait_ge(tab_ok, blk + 1)
                    for s in range(SLOTS):
                        gather(s, s, e0 * 2 + (s + 1), e0 * 4, e0)
                    with pool.Fori(0, ROUNDS - 1) as r:
                        round_(r, blk * EXPERTS + r * SLOTS)
                    round_(ROUNDS - 1, e0 + (ROUNDS - 1) * SLOTS, last=True)
                    for s in range(SLOTS):
                        pool.wait_ge(sca[s], e0 * 4 + 16 * ROUNDS)
            pool.memset(landed_flag[:, :], 0.0).then_inc(all_landed, 1)

        @block.scalar
        def _(act):
            link = Chain(act, chain_a)

            def estimate(dst, src, tmp):
                link(act.activation(tmp, src, ACT.Ln))
                act.activation(dst, tmp, ACT.Exp, scale=-0.5).then_inc(rs_est, 1)

            act.wait_ge(ld_first, 48)
            act.wait_ge(var_ok, 1)
            link(act.activation(junk[0:META, :], meta_in[:, :], ACT.Square, accum_out=ss[0:META, NT:NT + 1]))
            for i in range(NT):
                act.wait_ge(ld_x[i], 16)
                last = act.activation(junk[:, :], xin[:, i, :], ACT.Square, accum_out=ss[:, i:i + 1])
                if i < NT - 1:
                    link(last)
            last.then_inc(sq_sum, 1)
            act.wait_ge(var_ok, 2)
            estimate(rstd[:, :], nw1[:, :], nw2[:, :])
            act.wait_ge(ld_small, 16 * N_SMALL)
            act.activation(wf_hi[:, :, :], wf[:, :, :], ACT.Copy).then_inc(wf_h, 1)
            for n in range(2 * NT):
                i, half = n // 2, n % 2
                act.wait_ge(tp_done, n + 1)
                act.activation(hnT[0][:, 4 * half:4 * half + 4, META + P * i:META + P * (i + 1)],
                               ps[n % 4][:, :].rearrange("p (k t) -> p k t", k=4), ACT.Copy).then_inc(hi_ok, 1)
            act.wait_ge(tp_done, 2 * NT + 1)
            act.activation(hnT[0][:, :, 0:META], ps[4][:, 0:KD * META].rearrange("p (k t) -> p k t", k=KD),
                           ACT.Copy).then_inc(hi_ok, 1)

            def move_hi(n, src):
                if n >= 2:
                    c, kp = divmod(n - 2, 4)
                    if kp < 3:
                        act.wait_ge(mov_used, 3 * c + kp + 1)
                    else:
                        act.wait_ge(acc_done, NT * (c + 1))
                act.activation(mov[n % 2][0][:, :, :], src, ACT.Copy).then_inc(mov_hi, 1)

            def evacuate(c):
                for i in (0, 2):
                    act.wait_ge(acc_done, NT * c + i + 1)
                    act.activation(raw[:, c, i, :], ps[i][:, :], ACT.Copy).then_inc(acc_ev_a, 1)

            for c in range(4):
                act.wait_ge(ld_b[c], 16)
                for kp in range(4):
                    move_hi(4 * c + kp, land_b[c][:, 2 * kp:2 * kp + 2, :])
                    if kp == 0 and c > 0:
                        evacuate(c - 1)
                if c == 2:
                    act.wait_ge(fx_ok, 1)
                    link(act.activation(fa[:, :, :], fa[:, :, :], ACT.Exp))
                    act.activation(fa[:, :, :], fa[:, :, :], ACT.Ln, bias=1.0).then_inc(fe_ok, 1)
            evacuate(CQ)
            act.wait_ge(meta_done, 1)
            for j in range(3):
                last = act.activation(rawm[:, j, :], ps[6][32 * j:32 * j + META, :], ACT.Copy)
            last.then_inc(meta_ev, 1)
            act.wait_ge(acc_ev_v, 8)
            act.wait_ge(acc_ev_a, 8)
            act.wait_ge(meta_ev, 1)
            act.activation(sqm[:, :], rawm[:, CK, :], ACT.Square)
            act.activation(sq[:, :, :], raw[:, CK, :, :], ACT.Square).then_inc(sq_sum, 1)
            act.wait_ge(var_ok, 3)
            act.activation(sq[:, :, :], raw[:, CQ, :, :], ACT.Square).then_inc(sq_sum, 1)
            act.wait_ge(var_ok, 4)
            estimate(rsh[:, :, :, :], nh1[:, :, :, :], nh2[:, :, :, :])
            act.wait_ge(acc_done, 4 * NT)
            act.wait_ge(ld_s[0], 16)
            act.activation(sta[0][0][:, :, :], land_s[0][:, :, 0:P], ACT.Copy).then_inc(sta_hi, 1)

            def exps(n, i):
                w = META + P * (i + 1)
                act.wait_ge(s_read, n)
                for a in range(2):
                    last = act.activation(probs[:, i % 2, a, 0:w], sc[:, a, 0:w], ACT.Exp,
                                          bias=nmx[:, a:a + 1], accum_out=rs[:, i % 2, a:a + 1])
                last.then_inc(e_done, 1)

            with act.Fori(0, PAIRS) as p:
                act.wait_ge(qk_t, p + 1)
                act.activation(QT[:, :], ps[7][:, :], ACT.Copy, scale=gain_q[:, 0:1]).then_inc(q_ev, 1)
                exps(p * NT + 1, 0)
                for i in range(NT):
                    act.wait_ge(pt_done, p * NT + (i + 1))
                    act.activation(pT[:, 0, 0:P * (i + 1)], ps[1][:, 0:P * (i + 1)], ACT.Copy)
                    act.activation(pTm[:, :, :].rearrange("p a t -> p (a t)"), ps[6][0:META, 0:2 * P],
                                   ACT.Copy).then_inc(pt_ev_a, 1)
                    if i < NT - 1:
                        exps(p * NT + (i + 2), i + 1)
                    b, s = (i + 1) % 2, (i + 1) // 2 % 2
                    if b == 0:
                        act.wait_ge(ld_s[s], p * 16 + (32 if i == NT - 1 else 16))
                    act.activation(sta[b][0][:, :, :], land_s[s][:, :, P * b:P * (b + 1)], ACT.Copy).then_inc(sta_hi, 1)
                    act.wait_ge(g_done, p * NT + (i + 1))
                    act.activation(gates[:, bass.ds(p * NT + i, 1), :].rearrange("p o t -> p (o t)"), ps[0][:, :],
                                   ACT.Copy).then_inc(g_ev, 1)
            act.wait_ge(ot_ev, PAIRS)
            act.activation(brT[0][:, 0:4, :], oT[:, :, :], ACT.Copy)
            act.activation(brT[0][:, 4:8, :], poolT[:, :, :], ACT.Copy).then_inc(br_hi, 1)
            for c in range(KD):
                n = 2 * KD + c + 1
                b, s = n % 2, n // 2 % 2
                if n < N_STA:
                    if b == 0:
                        act.wait_ge(ld_s[s], 16 * (PAIRS + 1 + (n - 2 * KD) // 4))
                    if c >= 1:
                        act.wait_ge(up_done, c)
                    act.activation(sta[b][0][:, :, :], land_s[s][:, :, P * b:P * (b + 1)], ACT.Copy).then_inc(sta_hi, 1)
                act.activation(gates[:, c, :], gates[:, c, :], ACT.Sigmoid)
                act.activation(gates[:, KD + c, :], gates[:, KD + c, :], ACT.Sigmoid).then_inc(g_ok, 1)
                act.wait_ge(up_read, c + 1)
                act.activation(mgT[0][:, c, :], mg[c % 2][:, :], ACT.Copy).then_inc(mg_hi, 1)
            act.wait_ge(up_done, KD)
            for c in range(2):
                act.wait_ge(ld_e[c], 16)
                for kp in range(4):
                    move_hi(N_MOV_B + 4 * c + kp, land_e[c][:, 2 * kp:2 * kp + 2, :])
            for i in range(NT):
                act.wait_ge(h2_ok, NT + i + 1)
                last = act.activation(hn2[:, 0, :], h2[:, i, :], ACT.Square, accum_out=ss[:, i:i + 1])
                if i < NT - 1:
                    link(last)
            last.then_inc(sq_sum, 1)
            act.wait_ge(var_ok, 5)
            estimate(rstd[:, 0:NT], nw1[:, 0:NT], nw2[:, 0:NT])
            for n in range(2 * NT):
                i = n // 2
                if n % 2 == 0:
                    act.wait_ge(hn2_ok, i + 1)
                    act.dma_start(hn2_rows[2 * P * i:2 * P * (i + 1), :].rearrange("(p h) d -> p (h d)", h=2),
                                  hn2[:, i % 2, :]).then_inc(st_hn2[i % 2], 16)
                act.wait_ge(t2_done, n + 1)
                if i >= 2:
                    act.wait_ge(lg_done, i - 1)
                act.activation(hn2T[:, i % 2, 4 * (n % 2):4 * (n % 2) + 4, :].rearrange("p k t -> p (k t)"),
                               ps[n % 4][:, :], ACT.Copy).then_inc(t2_ev, 1)
            act.wait_ge(ge_in, 1)
            act.activation(gex[:, :, :], gex[:, :, :], ACT.Exp).then_inc(ge_out, 1)
            act.wait_ge(pe_in, 1)
            act.activation(p2[:, :], p2[:, :], ACT.Exp).then_inc(pe_out, 1)

            def x_ev(e, b):
                act.wait_ge(t_done, e + 1)
                act.activation(xT[b][:, :], ps[b][:, :], ACT.Copy).then_inc(t_ev, 1)

            def sigmoid(e, b):
                act.wait_ge(up2_done, e + 1)
                act.activation(ex[b][:, :], ps[2 + b][:, 0:P], ACT.Sigmoid).then_inc(e2_done, 1)

            def round_(e0, first=False, last=False):
                for s in range(SLOTS):
                    b = s % 2
                    if not (last and s == SLOTS - 1):
                        sigmoid(e0 + (s + 1), 1 - b)
                    if not (last and s >= SLOTS - 2):
                        x_ev(e0 + (s + 2), b)
                    act.wait_ge(dn_done, e0 + (s + 1))
                    if not first:
                        act.wait_ge(sca[s], e0 * 4)
                    act.activation(ye[s][:, :], ps[6 + b][:, :], ACT.Copy).then_inc(y_ev, 1)

            def first_two(e0):
                x_ev(e0, 0)
                sigmoid(e0, 0)
                x_ev(e0 + 1, 1)

            first_two(0)
            round_(0, first=True)
            with act.Fori(1, ROUNDS - 1) as r:
                round_(r * SLOTS)
            round_(SLOTS * (ROUNDS - 1), last=True)
            act.wait_ge(cnt_ok, 1)
            fullest = act.value_load(cmaxi[0:1, 0:1], min_val=0, max_val=SEQ)
            with act.Fori(1, BLOCKS) as blk:
                with act.If(fullest > blk * CAP):
                    first_two(blk * EXPERTS)
                    with act.Fori(0, ROUNDS - 1) as r:
                        round_(blk * EXPERTS + r * SLOTS)
                    round_(blk * EXPERTS + SLOTS * (ROUNDS - 1), last=True)

        @block.vector
        def _(dve):
            link = Chain(dve, chain_v)
            tt, ts, stt = dve.tensor_tensor, dve.tensor_scalar, dve.scalar_tensor_tensor

            def refine(y, v, t):
                link(tt(t, y, y, ALU.mult))
                link(tt(t, t, v, ALU.mult))
                link(ts(t, t, -0.5, 1.5, ALU.mult, ALU.add))
                link(tt(y, y, t, ALU.mult))

            dve.memset(ss[:, :], 1.0).then_inc(var_ok, 1)
            dve.memset(ssh[:, :, :, :], 1.0)
            link(dve.memset(fx[:, :, :], 0.0))
            dve.wait_ge(sq_sum, 1)
            ts(nw1[:, :], ss[:, :], 1.0 / D, EPS, ALU.mult, ALU.add).then_inc(var_ok, 1)
            dve.wait_ge(rs_est, 1)
            refine(rstd[:, :], nw1[:, :], nw3[:, :])
            for i in range(NT):
                stt(xin[:, i, :], xin[:, i, :], rstd[:, i:i + 1], gain_mix[:, :], ALU.mult, ALU.mult).then_inc(hn_ok, 1)
            stt(meta_in[:, :], meta_in[:, :], rstd[0:META, NT:NT + 1], gain_mix[0:META, :],
                ALU.mult, ALU.mult).then_inc(hn_ok, 1)
            dve.wait_ge(wf_h, 1)
            tt(wf_lo[:, :, :], wf[:, :, :], wf_hi[:, :, :].bitcast(F32), ALU.subtract).then_inc(wf_l, 1)
            for n in range(2 * NT):
                i, half = n // 2, n % 2
                at = (slice(None), slice(4 * half, 4 * half + 4), slice(META + P * i, META + P * (i + 1)))
                dve.wait_ge(hi_ok, n + 1)
                tt(hnT[1][at], ps[n % 4][:, :].rearrange("p (k t) -> p k t", k=4), hnT[0][at].bitcast(F32),
                   ALU.subtract).then_inc(lo_ok, 1)
            dve.wait_ge(hi_ok, 2 * NT + 1)
            mps = ps[4][:, 0:KD * META].rearrange("p (k t) -> p k t", k=KD)
            tt(hnT[1][:, :, 0:META], mps, hnT[0][:, :, 0:META].bitcast(F32), ALU.subtract)
            dve.tensor_copy(metaT[:, :, :], mps).then_inc(lo_ok, 1)

            def move_lo(n, src):
                dve.wait_ge(mov_hi, n + 1)
                tt(mov[n % 2][1][:, :, :], src, mov[n % 2][0][:, :, :].bitcast(F32), ALU.subtract).then_inc(mov_lo, 1)

            def evacuate(c):
                for i in (1, 3):
                    dve.wait_ge(acc_done, NT * c + i + 1)
                    dve.tensor_copy(raw[:, c, i, :], ps[i][:, :]).then_inc(acc_ev_v, 1)

            for c in range(4):
                for kp in range(4):
                    move_lo(4 * c + kp, land_b[c][:, 2 * kp:2 * kp + 2, :])
                    if kp == 0 and c > 0:
                        evacuate(c - 1)
                if c == 1:
                    dve.wait_ge(f_done, 1)
                    tt(fx[:, 0:NT, :], ps[5][:, 0:NT * HEADS].rearrange("p (i h) -> p i h", i=NT),
                       bc(bias_f[:, :].unsqueeze(1), [P, NT, HEADS]), ALU.add)
                    link(tt(fx[0:META, NT, :], ps[5][0:META, NT * HEADS:(NT + 1) * HEADS], bias_f[0:META, :], ALU.add))
                    link(ts(fa[:, :, :], fx[:, :, :], -1.0, None, ALU.mult))
                    tt(fa[:, :, :], fa[:, :, :], fx[:, :, :], ALU.min).then_inc(fx_ok, 1)
                    link(ts(fx[:, :, :], fx[:, :, :], 0.0, None, ALU.min))
                if c == 2:
                    dve.wait_ge(fe_ok, 1)
                    tt(fx[:, :, :], fx[:, :, :], fa[:, :, :], ALU.subtract).then_inc(logf_ok, 1)
            evacuate(CQ)
            dve.wait_ge(fc_done, 1)
            dve.tensor_copy(fcum[:, :, :].rearrange("p i h -> p (i h)"), ps[5][:, 0:NT * HEADS])
            ts(nfT[:, META:L], ps[7][0:HEADS, :], -1.0, None, ALU.mult)
            ts(nfT[:, 0:META], ps[4][0:HEADS, 0:META], -1.0, None, ALU.mult).then_inc(fc_ev, 1)
            ts(gain_q[:, :], gain_q[:, :], DH ** -0.5, None, ALU.mult)
            for g in range(NB):
                dve.wait_ge(mix_done, g + 1)
                dve.tensor_copy(mixT[:, g, :], ps[g][:, :]).then_inc(mix_ev, 1)
            dve.wait_ge(sq_sum, 2)
            dve.reduce_sum(ssh[0:META, 1, NT, :], sqm[:, :].rearrange("p (h d) -> p h d", h=HEADS), axis=AX.X)
            by_head = sq[:, :, :].rearrange("p i (h d) -> p (i h) d", d=DH)
            dve.reduce_sum(ssh[:, 1, 0:NT, :].rearrange("p i h -> p (i h)"), by_head, axis=AX.X).then_inc(var_ok, 1)
            dve.wait_ge(sq_sum, 3)
            link(dve.reduce_sum(ssh[:, 0, 0:NT, :].rearrange("p i h -> p (i h)"), by_head, axis=AX.X))
            ts(nh1[:, :, :, :], ssh[:, :, :, :], 1.0 / DH, EPS, ALU.mult, ALU.add).then_inc(var_ok, 1)
            for g in range(NB):
                dve.wait_ge(pool_done, g + 1)
                ts(poolT[:, g, :], ps[g][:, :], scale_pool[:, g:g + 1], None, ALU.mult).then_inc(pool_ev, 1)
            dve.wait_ge(rs_est, 2)
            refine(rsh[:, :, :, :], nh1[:, :, :, :], nh2[:, :, :, :])

            dve.wait_ge(sta_hi, 1)
            tt(sta[0][1][:, :, :], land_s[0][:, :, 0:P], sta[0][0][:, :, :].bitcast(F32), ALU.subtract).then_inc(sta_lo, 1)
            pair = Chain(dve, chain_c)

            def scores(p, n, i):
                w = P * (i + 1)
                dve.wait_ge(s_done, n)
                if i > 0:
                    dve.wait_ge(e_done, n - 1)
                for a in range(2):
                    fc = fcum[:, i, bass.ds(p * 2 + a, 1)]
                    stt(sc[:, a, META:META + w], ps[2 + a][:, 0:w], fc, nfb[:, a, META:META + w], ALU.add, ALU.add)
                    last = stt(sc[:, a, 0:META], smeta[:, a, i, :], fc, nfb[:, a, 0:META], ALU.add, ALU.add)
                pair(last)
                diag = sc[:, :, META + P * i:META + P * (i + 1)]
                pair(tt(diag, diag, bc(cst[:, C_MASK:C_MASK + P].unsqueeze(1), [P, 2, P]), ALU.add))
                pair(dve.reduce_max(mx[:, :], sc[:, :, 0:META + w], axis=AX.X))
                ts(nmx[:, :], mx[:, :], -1.0, None, ALU.mult).then_inc(s_read, 1)

            with dve.Fori(0, PAIRS) as p:
                pair.settle(p * PAIR_STEPS)
                cols = bass.ds(p * P, P)
                for dst, c, j in ((qn, CQ, 0), (kn, CK, 1)):
                    for a in range(2):
                        tt(dst[:, :, DH * a:DH * (a + 1)], raw[:, c, :, bass.ds(p * P + DH * a, DH)],
                           bc(rsh[:, j, 0:NT, bass.ds(p * 2 + a, 1)], [P, NT, DH]), ALU.mult)
                for a in range(2):
                    last = tt(knm[:, DH * a:DH * (a + 1)], rawm[:, CK, bass.ds(p * P + DH * a, DH)],
                              bc(rsh[0:META, 1, NT, bass.ds(p * 2 + a, 1)], [META, DH]), ALU.mult)
                last.then_inc(qk_n, 1)
                dve.wait_ge(qk_t, p + 1)
                ts(KT[:, META:L], ps[5][:, :], gain_k[:, 0:1], None, ALU.mult)
                ts(KT[:, 0:META], ps[4][:, 0:META], gain_k[:, 0:1], None, ALU.mult).then_inc(k_ev, 1)
                dve.wait_ge(sm_done, p + 1)
                dve.tensor_copy(smeta[:, 0, :, :].rearrange("p i s -> p (i s)"), ps[4][:, 0:NT * META])
                pair(dve.tensor_copy(smeta[:, 1, :, :].rearrange("p i s -> p (i s)"), ps[7][:, 0:NT * META]))
                dve.wait_ge(ld_nfb, p * 16 + 16)
                scores(p, p * NT + 1, 0)
                for i in range(NT):
                    dve.wait_ge(pt_done, p * NT + (i + 1))
                    dve.tensor_copy(pT[:, 1, 0:P * (i + 1)], ps[5][:, 0:P * (i + 1)]).then_inc(pt_ev_v, 1)
                    if i < NT - 1:
                        scores(p, p * NT + (i + 2), i + 1)
                    b = (i + 1) % 2
                    dve.wait_ge(sta_hi, p * NT + (i + 2))
                    tt(sta[b][1][:, :, :], land_s[(i + 1) // 2 % 2][:, :, P * b:P * (b + 1)],
                       sta[b][0][:, :, :].bitcast(F32), ALU.subtract).then_inc(sta_lo, 1)
                    pair(dve.reciprocal(rinv[:, :], rs[:, i % 2, :]))
                    dve.wait_ge(pv_done, p * NT + (i + 1))
                    tt(oN[:, :].rearrange("p (a d) -> p a d", a=2), ps[6][:, 2 * P:3 * P].rearrange("p (a d) -> p a d", a=2),
                       bc(rinv[:, :].unsqueeze(2), [P, 2, DH]), ALU.mult).then_inc(o_ev, 1)
                dve.wait_ge(ot_done, p * NT + NT)
                dve.tensor_copy(oT[:, bass.ds(p, 1), :].rearrange("p o t -> p (o t)"), ps[7][:, :]).then_inc(ot_ev, 1)
                assert pair.k == PAIR_STEPS, pair.k
            dve.wait_ge(br_hi, 1)
            tt(brT[1][:, 0:4, :], oT[:, :, :], brT[0][:, 0:4, :].bitcast(F32), ALU.subtract)
            tt(brT[1][:, 4:8, :], poolT[:, :, :], brT[0][:, 4:8, :].bitcast(F32), ALU.subtract).then_inc(br_lo, 1)
            for c in range(KD):
                n = 2 * KD + c + 1
                b = n % 2
                if n < N_STA:
                    dve.wait_ge(sta_hi, n + 1)
                    tt(sta[b][1][:, :, :], land_s[n // 2 % 2][:, :, P * b:P * (b + 1)],
                       sta[b][0][:, :, :].bitcast(F32), ALU.subtract).then_inc(sta_lo, 1)
                dve.wait_ge(up_done, c + 1)
                dve.wait_ge(g_ok, c + 1)
                tt(mg[c % 2][:, :], ps[c % 2][:, :], gates[:, c, :], ALU.mult)
                link(tt(mg2[c % 2][:, :], ps[2 + c % 2][:, :], gates[:, KD + c, :], ALU.mult))
                tt(mg[c % 2][:, :], mg[c % 2][:, :], mg2[c % 2][:, :], ALU.add).then_inc(up_read, 1)
                dve.wait_ge(mg_hi, c + 1)
                tt(mgT[1][:, c, :], mg[c % 2][:, :], mgT[0][:, c, :].bitcast(F32), ALU.subtract).then_inc(mg_lo, 1)
            def residual(c):
                for i in range(NT):
                    dve.wait_ge(acc_done, (4 + c) * NT + i + 1)
                    half = h2[:, i, 512 * c:512 * (c + 1)]
                    tt(half, half, ps[i][:, :], ALU.add).then_inc(h2_ok, 1)

            for c in range(2):
                for kp in range(4):
                    move_lo(N_MOV_B + 4 * c + kp, land_e[c][:, 2 * kp:2 * kp + 2, :])
                    if kp == 0 and c == 1:
                        dve.wait_ge(ld_h2, 16 * NT)
                        residual(0)
            residual(1)
            dve.wait_ge(sq_sum, 4)
            ts(nw1[:, 0:NT], ss[:, 0:NT], 1.0 / D, EPS, ALU.mult, ALU.add).then_inc(var_ok, 1)
            dve.wait_ge(rs_est, 3)
            refine(rstd[:, 0:NT], nw1[:, 0:NT], nw3[:, 0:NT])
            dve.wait_ge(ld_gf, 16)
            for i in range(NT):
                if i >= 2:
                    dve.wait_ge(st_hn2[i % 2], 16 * (i // 2))
                    dve.wait_ge(t2_done, 2 * (i - 1))
                stt(hn2[:, i % 2, :], h2[:, i, :], rstd[:, i:i + 1], gain_ffn[:, :], ALU.mult, ALU.mult).then_inc(hn2_ok, 1)
            link(dve.memset(gl8[:, :, :], -3e38))
            dve.wait_ge(lg_done, NT)
            link(tt(lg[:, :, :], ps[4][:, 0:NT * N_RT].rearrange("p (i n) -> p i n", i=NT),
                    bc(bias_rt[:, :].unsqueeze(1), [P, NT, N_RT]), ALU.add))
            link(dve.tensor_copy(gl8[:, :, 0:NG], lg[:, :, 0:NG]))

            def top8(src):
                for i in range(NT):
                    last = dve.max(top[:, i, :], src[:, i, :])
                link(last)
                for i in range(NT):
                    last = dve.max_index(topi[:, i, :], top[:, i, :], src[:, i, :])
                link(last)

            top8(gl8)
            tt(gex[:, :, :], lg[:, :, 0:NG], bc(top[:, :, 0:1], [P, NT, NG]), ALU.subtract).then_inc(ge_in, 1)
            link(dve.tensor_copy(idf[:, :, 0:1], topi[:, :, 0:1]))
            link(tt(ohg[:, :, :], bc(cst[:, C_I8:C_I8 + NG].unsqueeze(1), [P, NT, NG]), bc(idf[:, :, 0:1], [P, NT, NG]),
                    ALU.is_equal))
            link(tt(cand[:, :].rearrange("p (i g e) -> p i g e", i=NT, g=NG),
                    lg[:, :, NG:].rearrange("p i (g e) -> p i g e", g=NG),
                    bc(ohg[:, :, :].unsqueeze(3), [P, NT, NG, NE]), ALU.mult))
            link(dve.reduce_sum(esel[:, :, :], cand[:, :].rearrange("p (i g e) -> p i e g", i=NT, g=NG), axis=AX.X))
            top8(esel)
            tt(p2[:, :], top[:, :, 1], top[:, :, 0], ALU.subtract).then_inc(pe_in, 1)
            link(dve.tensor_copy(idf[:, :, :], topi[:, :, 0:2]))
            link(tt(oh8[:, :, :, :], bc(cst[:, C_I8:C_I8 + NE].unsqueeze(1).unsqueeze(1), [P, NT, 2, NE]),
                    bc(idf[:, :, :].unsqueeze(3), [P, NT, 2, NE]), ALU.is_equal))
            pk = pick[:, :, :].rearrange("p (i k) (g e) -> p i k g e", k=2, g=NG)
            for k in range(2):
                last = tt(pk[:, :, k, :, :], bc(ohg[:, :, :].unsqueeze(3), [P, NT, NG, NE]),
                          bc(oh8[:, :, k, :].unsqueeze(2), [P, NT, NG, NE]), ALU.mult)
            link(last)
            pki = pick[:, :, :].rearrange("p (i k) e -> p i k e", k=2)
            tt(chosen[:, :, :], pki[:, :, 0, :], pki[:, :, 1, :], ALU.add).then_inc(ch_ok, 1)
            dve.wait_ge(ge_out, 1)
            link(dve.reduce_sum(gtop[:, :], gex[:, :, :], axis=AX.X))
            dve.wait_ge(pe_out, 1)
            link(ts(r2[:, :], p2[:, :], 1.0, None, ALU.add))
            link(tt(r2[:, :], r2[:, :], gtop[:, :], ALU.mult))
            link(dve.reciprocal(gate2[:, :, 0], r2[:, :]))
            link(tt(gate2[:, :, 1], gate2[:, :, 0], p2[:, :], ALU.mult))
            for v, val in enumerate((cst[:, C_VA:C_VA + 2 * NT], cst[:, C_VB:C_VB + 2 * NT],
                                     gate2[:, :, :].rearrange("p i k -> p (i k)"))):
                last = tt(vals[:, :, v, :], pick[:, :, :], bc(val.unsqueeze(2), [P, 2 * NT, EXPERTS]), ALU.mult)
            link(last)
            dve.wait_ge(cnt_done, 1)
            link(dve.reduce_max(cmax[:, :], ps[6][:, 0:EXPERTS], axis=AX.X))
            before = ps[5][:, 0:NT * EXPERTS].rearrange("p (i e) -> p i e", i=NT)
            pci = pickc[:, :, :].rearrange("p (i k) e -> p i k e", k=2)
            for k in range(2):
                last = tt(pci[:, :, k, :], pki[:, :, k, :], before, ALU.mult)
            link(last)
            dve.tensor_copy(cmaxi[:, :], cmax[:, :]).then_inc(cnt_ok, 1)
            link(dve.reduce_sum(rank[:, :], pickc[:, :, :], axis=AX.X))
            for b in range(2):
                dve.wait_ge(st_hn2[b], 16 * (NT // 2))
            dve.wait_ge(t2_done, 2 * NT)
            for s in range(SLOTS):
                last = dve.memset(xg[s][:, :], 0.0)
            last.then_inc(xg_zero, 1)

            def make_tables(n, step):
                tt(rank1[:, :, :], bc(cst[:, C_SLOT:C_SLOT + P].unsqueeze(1), [P, 2 * NT, P]),
                   bc(rank[:, :].unsqueeze(2), [P, 2 * NT, P]), ALU.is_equal).then_inc(tab_in, 1)
                dve.wait_ge(tab_done, n)
                tab = ps[7][:, 0:2 * EXPERTS]
                flat = skip[:, :, :].rearrange("p v e -> p (v e)")
                step(ts(flat, tab, 0.0, SKIP, ALU.is_equal, ALU.mult))
                dve.tensor_copy(gslot[:, :], ps[7][:, 2 * EXPERTS:3 * EXPERTS])
                stt(idx[:, :, :].rearrange("p v e -> p (v e)"), tab, cst[:, C_HALF:C_HALF + 1], flat,
                    ALU.add, ALU.add).then_inc(tab_ok, 1)

            make_tables(1, link)
            dve.wait_ge(tab_ok, 1)

            turn = Chain(dve, chain_e)

            def round_(r, e0):
                turn.settle(e0 * EXPERT_STEPS)
                for s in range(SLOTS):
                    b = s % 2
                    turn(dve.tensor_copy(gcol[b][:, :], gslot[:, bass.ds(r * SLOTS + s, 1)]))
                    dve.wait_ge(e2_done, e0 + (s + 1))
                    turn(stt(hh[b][:, :], ps[2 + b][:, 0:P], gcol[b][:, 0:1], ex[b][:, :], ALU.mult, ALU.mult))
                    tt(hh[b][:, :], hh[b][:, :], ps[2 + b][:, P:2 * P], ALU.mult).then_inc(hh_ok, 1)
                    dve.wait_ge(ht_done, e0 + (s + 1))
                    dve.tensor_copy(hhT[b][:, :], ps[4 + b][:, 0:P]).then_inc(ht_ev, 1)
                assert turn.k == EXPERT_STEPS * SLOTS

            with dve.Fori(0, ROUNDS) as r:
                round_(r, r * SLOTS)
            fullest = dve.value_load(cmaxi[0:1, 0:1], min_val=0, max_val=SEQ)
            fill = Chain(dve, chain_t)
            with dve.Fori(1, BLOCKS) as blk:
                with dve.If(fullest > blk * CAP):
                    fill.settle(blk * 2 - 2)
                    fill(ts(rank[:, :], rank[:, :], float(-CAP), None, ALU.add))
                    for s in range(SLOTS):
                        dve.wait_ge(sca[s], blk * (16 * ROUNDS))
                    make_tables(blk + 1, fill)
                    dve.wait_ge(tab_ok, blk + 1)
                    apart(dve)
                    with dve.Fori(0, ROUNDS) as r:
                        round_(r, blk * EXPERTS + r * SLOTS)
            for i in range(NT):
                b = i % 2
                dve.wait_ge(ld_y[b], 32 * (i // 2 + 1))
                link(tt(h2[:, i, :], h2[:, i, :], yfin[:, b, 0, :], ALU.add))
                tt(h2[:, i, :], h2[:, i, :], yfin[:, b, 1, :], ALU.add).then_inc(yf_ok, 1)

        @block.tensor
        def _(pe):
            mm, tp = pe.matmul, pe.transpose

            def split_mm(dst, held, moved, first, final):
                for n, (u, v) in enumerate(((0, 0), (0, 1), (1, 0))):
                    last = mm(dst, held[u], moved[v], start=first and n == 0, stop=final and n == 2)
                return last

            pe.wait_ge(ld_first, 48)
            for n in range(2 * NT):
                i, half = n // 2, n % 2
                pe.wait_ge(hn_ok, i + 1)
                if n >= 4:
                    pe.wait_ge(lo_ok, n - 3)
                for j in range(4):
                    k = 4 * half + j
                    last = tp(ps[n % 4][:, P * j:P * (j + 1)], xin[:, i, P * k:P * (k + 1)], ident)
                last.then_inc(tp_done, 1)
            pe.wait_ge(hn_ok, NT + 1)
            for k in range(KD):
                last = tp(ps[4][:, META * k:META * (k + 1)], meta_in[:, P * k:P * (k + 1)], ident[0:META, 0:META])
            last.then_inc(tp_done, 1)
            pe.wait_ge(lo_ok, 2 * NT + 1)
            pe.wait_ge(wf_l, 1)
            for i in range(NT):
                cols = slice(META + P * i, META + P * (i + 1))
                for k in range(KD):
                    split_mm(ps[5][:, HEADS * i:HEADS * (i + 1)], (hnT[0][:, k, cols], hnT[1][:, k, cols]),
                             (wf_hi[:, k, :], wf_lo[:, k, :]), k == 0, k == KD - 1)
            for k in range(KD):
                last = mm(ps[5][0:META, HEADS * NT:HEADS * (NT + 1)], metaT[:, k, :], wf[:, k, :],
                          start=k == 0, stop=k == KD - 1)
            last.then_inc(f_done, 1)

            def accumulate(n0, held, before=None):
                for kp in range(4):
                    pe.wait_ge(mov_lo, n0 + (kp + 1))
                    for k2 in range(2):
                        k = 2 * kp + k2
                        for i in range(NT):
                            if k == 0 and before is not None:
                                before(i)
                            last = split_mm(ps[i][:, :], [h[:, k, held[1] + P * i:held[1] + P * (i + 1)] for h in held[0]],
                                            [mov[kp % 2][n][:, k2, :] for n in range(2)], k == 0, k == KD - 1)
                            if k == KD - 1:
                                last.then_inc(acc_done, 1)
                    if kp < 3:
                        last.then_inc(mov_used, 1)

            accumulate(0, (hnT, META))
            with pe.Fori(1, 4) as c:
                def freed(i):
                    if i % 2 == 0:
                        pe.wait_ge(acc_ev_a, c * 2 + (i // 2 - 1))
                    else:
                        pe.wait_ge(acc_ev_v, c * 2 + (i // 2 - 1))

                accumulate(c * 4, (hnT, META), freed)
            for k in range(KD):
                for j in range(3):
                    last = mm(ps[6][32 * j:32 * j + META, :], metaT[:, k, :], land_b[j][:, k, :],
                              start=k == 0, stop=k == KD - 1)
            last.then_inc(meta_done, 1)
            pe.wait_ge(logf_ok, 1)
            for i in range(NT):
                dst = ps[5][:, HEADS * i:HEADS * (i + 1)]
                mm(dst, ones[0:META, :], fx[0:META, NT, :], start=True, stop=False)
                for j in range(i):
                    mm(dst, ones, fx[:, j, :], start=False, stop=False)
                mm(dst, tri, fx[:, i, :], start=False, stop=True)
            for i in range(NT):
                dst = ps[7][0:HEADS, P * i:P * (i + 1)]
                mm(dst, fx[0:META, NT, :], ones[0:META, :], start=True, stop=False)
                for j in range(i):
                    mm(dst, fx[:, j, :], ones, start=False, stop=False)
                mm(dst, fx[:, i, :], tri, start=False, stop=True)
            mm(ps[4][0:HEADS, 0:META], fx[0:META, NT, :], cst[0:META, C_TRI:C_TRI + META],
               start=True, stop=True).then_inc(fc_done, 1)
            pe.wait_ge(ld_pool, 32)
            pe.wait_ge(meta_ev, 1)
            pe.wait_ge(acc_ev_a, 8)
            pe.wait_ge(acc_ev_v, 8)
            for g in range(NB):
                cols = slice(P * g, P * (g + 1))
                for i in range(NT):
                    dst = ps[g][:, P * i:P * (i + 1)]
                    mm(dst, raw[:, CP, i, cols], band[:, 0, g, :], start=True, stop=False)
                    if i:
                        last = mm(dst, raw[:, CP, i - 1, cols], band[:, 1, g, :], start=False, stop=True)
                    else:
                        last = mm(dst, rawm[:, CP, cols], band[0:META, 2, g, :], start=False, stop=True)
                last.then_inc(mix_done, 1)
            for g in range(NB):
                pe.wait_ge(mix_ev, g + 1)
                mm(ps[g][:, :], wpool[:, g, :], mixT[:, g, :], start=True, stop=True).then_inc(pool_done, 1)
            pe.wait_ge(pool_ev, NB)

            def raw_scores(i):
                for a in range(2):
                    rows = slice(DH * a, DH * (a + 1))
                    last = mm(ps[2 + a][:, 0:P * (i + 1)], QT[rows, P * i:P * (i + 1)],
                              KT[rows, META:META + P * (i + 1)], start=True, stop=True)
                last.then_inc(s_done, 1)

            with pe.Fori(0, PAIRS) as p:
                pe.wait_ge(qk_n, p + 1)
                for i in range(NT):
                    tp(ps[7][:, P * i:P * (i + 1)], qn[:, i, :], ident)
                    tp(ps[5][:, P * i:P * (i + 1)], kn[:, i, :], ident)
                tp(ps[4][:, 0:META], knm[:, :], ident[0:META, 0:META]).then_inc(qk_t, 1)
                pe.wait_ge(q_ev, p + 1)
                pe.wait_ge(k_ev, p + 1)
                raw_scores(0)
                for i in range(NT):
                    for a in range(2):
                        rows = slice(DH * a, DH * (a + 1))
                        last = mm(ps[(4, 7)[a]][:, META * i:META * (i + 1)], QT[rows, P * i:P * (i + 1)],
                                  KT[rows, 0:META], start=True, stop=True)
                last.then_inc(sm_done, 1)
                for i in range(NT):
                    if i < NT - 1:
                        pe.wait_ge(s_read, p * NT + (i + 1))
                        raw_scores(i + 1)
                    pe.wait_ge(e_done, p * NT + (i + 1))
                    for a in range(2):
                        for j in range(i + 1):
                            tp(ps[(1, 5)[a]][:, P * j:P * (j + 1)],
                               probs[:, i % 2, a, META + P * j:META + P * (j + 1)], ident)
                    for a in range(2):
                        last = tp(ps[6][0:META, P * a:P * (a + 1)], probs[:, i % 2, a, 0:META], ident)
                    last.then_inc(pt_done, 1)
                    pe.wait_ge(sta_lo, p * NT + (i + 1))
                    if i > 0:
                        pe.wait_ge(g_ev, p * NT + i)
                    b = i % 2
                    for k in range(KD):
                        last = split_mm(ps[0][:, :], [sta[b][n][:, k, :] for n in range(2)],
                                        [h[:, k, META:L] for h in hnT], k == 0, k == KD - 1)
                    last.then_inc(g_done, 1)
                    pe.wait_ge(pt_ev_a, p * NT + (i + 1))
                    pe.wait_ge(pt_ev_v, p * NT + (i + 1))
                    for a in range(2):
                        dst = ps[6][:, 2 * P + DH * a:2 * P + DH * (a + 1)]
                        cols = bass.ds(p * P + DH * a, DH)
                        for j in range(i + 1):
                            mm(dst, pT[:, a, P * j:P * (j + 1)], raw[:, CV, j, cols], start=j == 0, stop=False)
                        last = mm(dst, pTm[:, a, :], rawm[:, CV, cols], start=False, stop=True)
                    last.then_inc(pv_done, 1)
                    pe.wait_ge(o_ev, p * NT + (i + 1))
                    tp(ps[7][:, P * i:P * (i + 1)], oN[:, :], ident).then_inc(ot_done, 1)

            pe.wait_ge(br_lo, 1)

            def up(c0, first):
                for b in range(2):
                    pe.wait_ge(sta_lo, c0 + (2 * KD + b + 1))
                    if not first:
                        pe.wait_ge(up_read, c0 + (b - 1))
                    for br in range(2):
                        for k in range(4):
                            last = split_mm(ps[2 * br + b][:, :], [sta[b][n][:, 4 * br + k, :] for n in range(2)],
                                            [h[:, 4 * br + k, :] for h in brT], k == 0, k == 3)
                    last.then_inc(up_done, 1)

            up(0, True)
            with pe.Fori(1, KD // 2) as q:
                up(q * 2, False)
            pe.wait_ge(mg_lo, KD)
            accumulate(N_MOV_B, (mgT, 0))
            accumulate(N_MOV_B + 4, (mgT, 0), lambda i: pe.wait_ge(h2_ok, i + 1))
            def logits(i):
                pe.wait_ge(t2_ev, 2 * i + 2)
                for k in range(KD):
                    last = mm(ps[4][:, N_RT * i:N_RT * (i + 1)], hn2T[:, i % 2, k, :], w_rt[:, k, :],
                              start=k == 0, stop=k == KD - 1)
                last.then_inc(lg_done, 1)

            for i in range(NT):
                pe.wait_ge(hn2_ok, i + 1)
                for half in range(2):
                    n = 2 * i + half
                    if n >= 4:
                        pe.wait_ge(t2_ev, n - 3)
                    for j in range(4):
                        k = 4 * half + j
                        last = tp(ps[n % 4][:, P * j:P * (j + 1)], hn2[:, i % 2, P * k:P * (k + 1)], ident)
                    last.then_inc(t2_done, 1)
                if i:
                    logits(i - 1)
            logits(NT - 1)
            pe.wait_ge(ch_ok, 1)
            for i in range(NT):
                dst = ps[5][:, EXPERTS * i:EXPERTS * (i + 1)]
                for j in range(i):
                    mm(dst, ones, chosen[:, j, :], start=j == 0, stop=False)
                mm(dst, tri_strict, chosen[:, i, :], start=i == 0, stop=True)
            for i in range(NT):
                last = mm(ps[6][:, 0:EXPERTS], ones, chosen[:, i, :], start=i == 0, stop=i == NT - 1)
            last.then_inc(cnt_done, 1)

            def table():
                for ik in range(2 * NT):
                    last = mm(ps[7][:, 0:3 * EXPERTS], rank1[:, ik, :],
                              vals[:, ik, :, :].rearrange("p v e -> p (v e)"), start=ik == 0, stop=ik == 2 * NT - 1)
                last.then_inc(tab_done, 1)

            pe.wait_ge(tab_in, 1)
            table()

            def turn_rows(s, b, gathers):
                pe.wait_ge(ga[s], gathers)
                xr = xg[s][:, :].rearrange("p (q c) -> p c q", c=4)
                for c in range(4):
                    last = tp(ps[b][:, P * c:P * (c + 1)], xr[:, c, :], ident)
                last.then_inc(t_done, 1)

            def up_products(s, b, e, loads):
                pe.wait_ge(t_ev, e + 1)
                pe.wait_ge(ld_up[s], loads)
                for c in range(4):
                    for h in range(2):
                        held = xT[b][:, P * c + CAP * h:P * c + CAP * (h + 1)]
                        for fh in range(2):
                            k = F * c + P * fh
                            last = mm(ps[2 + b][CAP * fh:CAP * (fh + 1), 0:2 * P].rearrange("p (w f) -> p w f", w=2),
                                      held, w13[s][:, :, h, k:k + P],
                                      start=c == 0 and h == 0, stop=c == 3 and h == 1)
                last.then_inc(up2_done, 1)

            def round_(r16, e0, first=False, last_round=False):
                for s in range(SLOTS):
                    b = s % 2
                    if not (last_round and s == SLOTS - 1):
                        up_products((s + 1) % SLOTS, 1 - b, e0 + (s + 1), r16 * 2 + (32 if s < SLOTS - 1 else 64))
                    pe.wait_ge(hh_ok, e0 + (s + 1))
                    tp(ps[4 + b][:, 0:P], hh[b][:, :], ident).then_inc(ht_done, 1)
                    if not (last_round and s >= SLOTS - 2):
                        turn_rows((s + 2) % SLOTS, b, r16 + (16 if s < SLOTS - 2 else 32))
                    pe.wait_ge(ht_ev, e0 + (s + 1))
                    pe.wait_ge(ld_dn[s], r16 + 16)
                    if not (first and s < 2):
                        pe.wait_ge(y_ev, e0 + (s - 1))
                    for j in range(2):
                        for dh in range(2):
                            last = mm(ps[6 + b][CAP * dh:CAP * (dh + 1), :], hhT[b][:, CAP * j:CAP * (j + 1)],
                                      w2s[s][:, j, 512 * dh:512 * (dh + 1)], start=j == 0, stop=j == 1)
                    last.then_inc(dn_done, 1)

            turn_rows(0, 0, 16)
            up_products(0, 0, 0, 32)
            turn_rows(1, 1, 16)
            round_(0, 0, first=True)
            with pe.Fori(1, ROUNDS - 1) as r:
                round_(r * 16, r * SLOTS)
            round_(16 * (ROUNDS - 1), SLOTS * (ROUNDS - 1), last_round=True)
            pe.wait_ge(cnt_ok, 1)
            fullest = pe.value_load(cmaxi[0:1, 0:1], min_val=0, max_val=SEQ)
            with pe.Fori(1, BLOCKS) as blk:
                with pe.If(fullest > blk * CAP):
                    pe.wait_ge(tab_in, blk + 1)
                    pe.wait_ge(y_ev, blk * EXPERTS)
                    table()
                    r16 = blk * (16 * ROUNDS)
                    turn_rows(0, 0, r16 + 16)
                    up_products(0, 0, blk * EXPERTS, r16 * 2 + 32)
                    turn_rows(1, 1, r16 + 16)
                    with pe.Fori(0, ROUNDS - 1) as r:
                        round_(r16 + r * 16, blk * EXPERTS + r * SLOTS)
                    round_(r16 + 16 * (ROUNDS - 1), blk * EXPERTS + SLOTS * (ROUNDS - 1), last_round=True)


_INS = ["x", "meta_tokens", "norm_mix_g", "w_in", "b_forget", "q_norm_g", "k_norm_g", "w_up_attn", "w_pool",
        "pool_scale", "w_up_pool", "w_out", "norm_ffn_g", "w_group", "b_group", "w_router", "b_router", "w1", "w3", "w2"]


def kernel(**inputs):
    import numpy as np
    import concourse.bacc as bacc
    from concourse.bass_utils import run_bass_kernel_spmd

    nc = bacc.Bacc("TRN2", target_bir_lowering=False, num_devices=1)
    arrays, args = {}, []
    given = {name: np.ascontiguousarray(inputs[name]) for name in _INS}
    given.update(constants())
    for name, a in given.items():
        arrays[f"in_{name}"] = a
        args.append(nc.dram_tensor(f"in_{name}", a.shape, mybir.dt.from_np(a.dtype), kind="ExternalInput").ap())
    args.append(nc.dram_tensor("out_0", (1, SEQ, D), F32, kind="ExternalOutput").ap())
    program(nc, *args)
    r = run_bass_kernel_spmd(nc, [arrays], core_ids=[0])
    return r.results[0]["out_0"]
```

```python
import concourse.bass as bass
from concourse import mybir

F32 = mybir.dt.float32
F32R = mybir.dt.float32r
I32 = mybir.dt.int32
U32 = mybir.dt.uint32
ALU = mybir.AluOpType
ACT = mybir.ActivationFunctionType
AX = mybir.AxisListType

P = 128
D = 1024
KD = D // P
SEQ = 512
NT = SEQ // P
META = 16
L = META + SEQ
HEADS, DH = 8, 64
PAIRS = HEADS // 2
AW = HEADS * DH
NG, NE = 4, 8
EXPERTS = NG * NE
F = 256
CAP = 64
BLOCKS = SEQ // CAP
WINDOWS = (2, 4, 8, 16)
EPS = 1e-6
SKIP = 65536.0
Q_OFF, K_OFF, V_OFF = 0, AW, 2 * AW
F_OFF = 3 * AW
P_OFF = F_OFF + HEADS
G_OFF = P_OFF + AW
CP, CV, CK, CQ = range(4)
ORDER = (CK, CQ, CP, CV)
COLUMNS = (P_OFF, V_OFF, K_OFF, Q_OFF)
SLOTS = 4
ROUNDS = EXPERTS // SLOTS
BRANCH_K = (4, 5, 6, 7, 0, 1, 2, 3)

C_ID, C_TRI, C_TRS, C_ONE, C_MASK, C_SLOT = (P * i for i in range(6))
C_I8 = 6 * P
C_VA = C_I8 + NE
C_VB = C_VA + 2 * NT
C_HALF = C_VB + 2 * NT
C_END = C_HALF + 1
NB = len(WINDOWS)
HALF_L = L // 2


def constants():
    import numpy as np

    i = np.arange(P)
    c = np.zeros((P, C_END), np.float32)
    c[:, C_ID:C_ID + P] = i[:, None] == i[None, :]
    c[:, C_TRI:C_TRI + P] = i[:, None] <= i[None, :]
    c[:, C_TRS:C_TRS + P] = i[:, None] < i[None, :]
    c[:, C_ONE:C_ONE + P] = 1
    c[:, C_MASK:C_MASK + P] = np.where(i[None, :] <= i[:, None], 0.0, -1e30)
    c[:, C_SLOT:C_SLOT + P] = i[None, :] % CAP
    c[:, C_I8:C_I8 + NE] = np.arange(NE)
    for t in range(NT):
        for k in range(2):
            c[:, C_VA + 2 * t + k] = 2 * (P * t + i) + 1
            c[:, C_VB + 2 * t + k] = 2 * (P * t + i + SEQ * k) + 1
    c[:, C_HALF] = np.where(i < CAP, -1, 0)
    b = np.zeros((P, 3, NB, P), np.float32)
    for g, w in enumerate(WINDOWS):
        ago = i[None, :] - i[:, None]
        b[:, 0, g] = ((ago >= 0) & (ago < w)) / w - (ago == 0)
        b[:, 1, g] = (ago + P < w) / w
        b[:META, 2, g] = (ago[:META] + META < w) / w
    return {"consts": c, "bands": b.reshape(P, 3 * NB * P)}


class Chain:

    def __init__(self, eng, sem):
        self.eng, self.sem, self.base, self.k = eng, sem, 0, 0

    def __call__(self, ins):
        ins.then_inc(self.sem, 1)
        self.k += 1
        self.eng.wait_ge(self.sem, self.base + self.k)

    def settle(self, base):
        self.base, self.k = base, 0


def program(nc, x, meta_tokens, norm_mix_g, w_in, b_forget, q_norm_g, k_norm_g, w_up_attn, w_pool,
            pool_scale, w_up_pool, w_out, norm_ffn_g, w_group, b_group, w_router, b_router, w1, w3, w2,
            consts, bands, out):
    frames = x[0].rearrange("(i p) d -> i p d", p=P)
    out_rows = out[0].rearrange("(i p) d -> i p d", p=P)
    win = w_in[0].rearrange("(k p) n -> p k n", p=P)
    wua = w_up_attn[0].rearrange("(k p) n -> p k n", p=P)
    wup = w_up_pool[0].rearrange("(k p) n -> p k n", p=P)
    wout = w_out[0].rearrange("(k p) n -> p k n", p=P)
    w1e = w1[0].rearrange("g e (h p c) f -> (g e) p h (c f)", h=2, c=4)
    w3e = w3[0].rearrange("g e (h p c) f -> (g e) p h (c f)", h=2, c=4)
    w2e = w2[0].rearrange("g e (j p) d -> (g e) p j d", p=P)
    hn2_rows = nc.dram_tensor("hn2_rows", [2 * SEQ, D // 2], F32).ap()
    y_rows = nc.dram_tensor("y_rows", [4 * SEQ, D // 2], F32).ap()
    nf_rows = nc.dram_tensor("nf_rows", [HEADS, L], F32).ap()
    nf_pairs = nf_rows.rearrange("(q a) s -> q (a s)", a=2)

    BASE = 16512
    KB = 1024

    def sb(name, shape, at, dt=F32):
        return nc.alloc_sbuf_tensor_at(name, shape, dt, offset=BASE + int(at * KB))

    cst = sb("cst", [P, C_END], 0)
    ident = cst[:, C_ID:C_ID + P]
    tri = cst[:, C_TRI:C_TRI + P]
    tri_strict = cst[:, C_TRS:C_TRS + P]
    ones = cst[:, C_ONE:C_ONE + P]
    small = [3.25]

    def keep(name, shape, dt=F32):
        n = 1
        for s in shape[1:]:
            n *= s
        t = sb(name, shape, small[0], dt)
        small[0] += -(-n * 4 // 32) * 32 / KB
        assert small[0] <= 11
        return t

    w_rt = keep("w_rt", [P, KD, NG + EXPERTS])
    bias_rt = keep("bias_rt", [P, NG + EXPERTS])
    bias_f = keep("bias_f", [HEADS, 1])
    gain_q = keep("gain_q", [P, 1])
    gain_k = keep("gain_k", [P, 1])
    scale_pool = keep("scale_pool", [P, NB])
    ss = keep("ss", [P, NT + 1])
    ss2 = keep("ss2", [P, 2, NT])
    table_in = keep("table_in", [P, 1])
    table_out = keep("table_out", [P, 1])
    rstd = keep("rstd", [P, NT + 1])
    nw1 = keep("nw1", [P, NT + 1])
    nw3 = keep("nw3", [P, NT + 1])
    metaT = keep("metaT", [P, KD, META])
    ssh = keep("ssh", [P, 2, NT + 1, HEADS])
    rsh = keep("rsh", [P, 2, NT + 1, HEADS])
    nh1 = keep("nh1", [P, 2, NT + 1, HEADS])
    nh2 = keep("nh2", [P, 2, NT + 1, HEADS])
    fcum = keep("fcum", [P, NT, HEADS])
    mx = keep("mx", [P, 2])
    nmx = keep("nmx", [P, 2])
    rs = keep("rs", [P, 2, 2])
    rinv = keep("rinv", [P, 2])

    mov = [[sb(f"mov{b}{n}", [P, 2, 512], 11 + 8 * b + 4 * h, F32R) for h, n in enumerate(("hi", "lo"))]
           for b in range(2)]
    sta = [[sb(f"sta{b}{n}", [P, KD, P], 11 + 8 * b + 4 * h, F32R) for h, n in enumerate(("hi", "lo"))]
           for b in range(2)]
    xin = sb("xin", [P, NT, D], 27)
    gain_mix = sb("gain_mix", [P, D], 43)
    meta_in = sb("meta_in", [META, D], 116)
    junk = sb("junk", [P, D], 124)
    last_x = sb("last_x", [P, D], 128)
    meta_x = sb("meta_x", [META, D], 132)
    band = sb("band", [P, 3, NB, P], 27)
    mixT = sb("mixT", [P, NB, SEQ], 33)
    wpool = sb("wpool", [P, NB, P], 41)
    sq = sb("sq", [P, NT, 512], 154)
    sqm = sb("sqm", [META, 512], 36)
    fx = sb("fx", [HEADS, L], 158)
    nfT = sb("nfT", [HEADS, L], 43)
    fa = sb("fa", [HEADS, L], 45.25)
    fsum = sb("fsum", [HEADS, L], 47.5)
    wf = sb("wf", [P, KD, P], 202)
    wf_hi = sb("wf_hi", [P, KD, P], 194, F32R)
    wf_lo = sb("wf_lo", [P, KD, P], 198, F32R)
    qn = sb("qn", [P, NT, P], 27)
    kn = sb("kn", [P, NT, P], 29)
    knm = sb("knm", [META, P], 31)
    QT = sb("QT", [P, SEQ], 31.5)
    KT = sb("KT", [P, L], 33.5)
    sc = sb("sc", [P, 2, L], 35.75)
    pT = sb("pT", [P, 2, SEQ], 40)
    pTm = sb("pTm", [META, 2, P], 44)
    oN = sb("oN", [P, P], 45)
    probs = sb("probs", [P, 2, 2, L], 194)
    nfb = sb("nfb", [P, 2, L], 202.5)
    land_b = [sb(f"land_b{c}", [P, KD, 512], at) for c, at in enumerate((50, 66, 162, 178))]
    land_s = [sb(f"land_s{b}", [P, KD, 256], 50 + 8 * b) for b in range(2)]
    land_e = [sb("land_e0", [P, KD, 512], 66), sb("land_e1", [P, KD, 512], 50)]
    hnT = [sb(f"hnT_{n}", [P, KD, L], 82 + 17 * h, F32R) for h, n in enumerate(("hi", "lo"))]
    brT = [sb(f"brT_{n}", [P, KD, SEQ], 82 + 16 * h, F32R) for h, n in enumerate(("hi", "lo"))]
    raw = sb("raw", [P, 4, NT, 512], 116)
    poolT = sb("poolT", [P, NB, SEQ], 116)
    rawm = sb("rawm", [META, 3, 512], 148)
    oT = sb("oT", [P, PAIRS, SEQ], 154)
    gates = sb("gates", [P, 2 * KD, SEQ], 162)
    mgT = [sb(f"mgT_{n}", [P, KD, SEQ], 124 + 16 * h, F32R) for h, n in enumerate(("hi", "lo"))]
    mg = [sb(f"mg{b}", [P, SEQ], 27 + 4 * b) for b in range(2)]
    mg2 = [sb(f"mg2{b}", [P, SEQ], 29 + 4 * b) for b in range(2)]
    h2 = sb("h2", [P, NT, D], 27)
    gain_ffn = sb("gain_ffn", [P, D], 43)
    hn2 = sb("hn2", [P, NT, D], 11)
    hn2T = [sb(f"hn2T{i}", [P, KD, P], at) for i, at in enumerate((148, 152, 106.5, 110.5))]
    junk2 = sb("junk2", [P, 512], 156)
    rt = [114.5]

    def route(name, shape, dt=F32):
        n = 1
        for s in shape[1:]:
            n *= s
        t = sb(name, shape, rt[0], dt)
        rt[0] += -(-n * 4 // 32) * 32 / KB
        assert rt[0] <= 124
        return t

    lg = route("lg", [P, NT, NG + EXPERTS])
    gl8 = route("gl8", [P, NT, 8])
    top = route("top", [P, NT, 8])
    topi = route("topi", [P, NT, 8], U32)
    idf = route("idf", [P, NT, 2])
    gex = route("gex", [P, NT, NG])
    gtop = route("gtop", [P, NT])
    ohg = route("ohg", [P, NT, NG])
    esel = route("esel", [P, NT, NE])
    p2 = route("p2", [P, NT])
    r2 = route("r2", [P, NT])
    gate2 = route("gate2", [P, NT, 2])
    oh8 = route("oh8", [P, NT, 2, NE])
    chosen = route("chosen", [P, NT, EXPERTS])
    rank = route("rank", [P, 2 * NT])
    cmax = route("cmax", [P, 1])
    cmaxi = route("cmaxi", [P, 1], I32)
    skip = route("skip", [P, 2, EXPERTS])
    cand = route("cand", [P, NT * EXPERTS])
    idx = route("idx", [P, 2, EXPERTS], U32)
    gslot = route("gslot", [P, EXPERTS])
    pick = sb("pick", [P, 2 * NT, EXPERTS], 74)
    pickc = sb("pickc", [P, 2 * NT, EXPERTS], 75)
    vals = sb("vals", [P, 2 * NT, 3, EXPERTS], 76)
    rank1 = sb("rank1", [P, 2 * NT, P], 43)
    xg = [sb(f"xg{s}", [P, 512], 11 + 2 * s) for s in range(SLOTS)]
    xT = [sb(f"xT{b}", [P, 512], 19 + 2 * b) for b in range(2)]
    ye = [sb(f"ye{s}", [P, 512], 106.5 + 2 * s) for s in range(SLOTS)]
    hh = [sb(f"hh{b}", [P, P], 23 + b / 2) for b in range(2)]
    hhT = [sb(f"hhT{b}", [P, P], 24 + b / 2) for b in range(2)]
    ex = [sb(f"ex{b}", [P, P], 25 + b / 2) for b in range(2)]
    ixg = [sb(f"ixg{s}", [P, 1], 26 + s / 32, U32) for s in range(SLOTS)]
    ixs = [sb(f"ixs{s}", [P, 1], 26.125 + s / 32, U32) for s in range(SLOTS)]
    landed_flag = sb("landed_flag", [P, 1], 26.375)
    gcol = [sb(f"gcol{b}", [P, 1], 26.25 + b / 32) for b in range(2)]
    wslot_at = (82, 159.75, 183.75, 50, 124)
    w13 = [sb(f"w13_{s}", [P, 2, 2, 4 * F], at) for s, at in enumerate(wslot_at)]
    w2s = [sb(f"w2s_{s}", [P, 2, D], at + 16) for s, at in enumerate(wslot_at)]
    yfin = sb("yfin", [P, 2, 2, D], 82)

    ps = [nc.alloc_psum_tensor(f"ps{b}", [P, 512], F32) for b in range(8)]

    def sem(name):
        return nc.alloc_semaphore(name)

    ld_x = [sem(f"ld_x{i}") for i in range(NT + 1)]
    ld_first = sem("ld_first")
    wf_zero, ld_wf = sem("wf_zero"), sem("ld_wf")
    ld_small = sem("ld_small")
    ld_b = [sem(f"ld_b{c}") for c in range(4)]
    ld_pool = sem("ld_pool")
    ld_s = [sem(f"ld_s{b}") for b in range(2)]
    ld_nf = sem("ld_nf")
    ld_nfb = sem("ld_nfb")
    ld_e = [sem(f"ld_e{b}") for b in range(2)]
    ld_h2 = sem("ld_h2")
    ld_gf = sem("ld_gf")
    ld_up = [sem(f"ld_up{s}") for s in range(SLOTS + 1)]
    ld_dn = [sem(f"ld_dn{s}") for s in range(SLOTS + 1)]
    ld_y = [sem(f"ld_y{b}") for b in range(2)]
    ld_half = sem("ld_half")
    st_hn2 = sem("st_hn2")
    st_out = sem("st_out")
    chain_v, chain_c, chain_e, chain_t = (sem(f"chain_{n}") for n in "vcet")
    chain_a, chain_g = sem("chain_a"), sem("chain_g")
    sq_sum = sem("sq_sum")
    var_ok = sem("var_ok")
    rs_est = sem("rs_est")
    rstd_ok, gained, hn_ok_a = (sem(n) for n in ("rstd_ok", "gained", "hn_ok_a"))
    hn_ok = sem("hn_ok")
    tp_done = sem("tp_done")
    hi_ok = sem("hi_ok")
    lo_ok = sem("lo_ok")
    wf_h, wf_l = sem("wf_h"), sem("wf_l")
    f_done, fx_ok, fe_ok, fsum_ok = sem("f_done"), sem("fx_ok"), sem("fe_ok"), sem("fsum_ok")
    mov_hi, mov_lo, mov_used = sem("mov_hi"), sem("mov_lo"), sem("mov_used")
    acc_done = sem("acc_done")
    acc_ev_a, acc_ev_v = sem("acc_ev_a"), sem("acc_ev_v")
    meta_done, meta_ev = sem("meta_done"), sem("meta_ev")
    fc_done, fc_read, nf_ok = sem("fc_done"), sem("fc_read"), sem("nf_ok")
    mix_done, mix_ev, pool_done, pool_ev = sem("mix_done"), sem("mix_ev"), sem("pool_done"), sem("pool_ev")
    qk_n = sem("qk_n")
    qk_t = sem("qk_t")
    q_ev, k_ev = sem("q_ev"), sem("k_ev")
    s_last = sem("s_last")
    s_done = sem("s_done")
    s_read = sem("s_read")
    e_done = sem("e_done")
    pt_done, pt_ev_a, pt_ev_v = sem("pt_done"), sem("pt_ev_a"), sem("pt_ev_v")
    pv_done, o_ev, ot_done, ot_ev = sem("pv_done"), sem("o_ev"), sem("ot_done"), sem("ot_ev")
    sta_hi, sta_lo = sem("sta_hi"), sem("sta_lo")
    g_done, g_ev, g_ok = sem("g_done"), sem("g_ev"), sem("g_ok")
    br_hi, br_lo = sem("br_hi"), sem("br_lo")
    up_done, up_read, mg_hi, mg_lo = sem("up_done"), sem("up_read"), sem("mg_hi"), sem("mg_lo")
    h2_ok = sem("h2_ok")
    hn2_ok, t2_done, t2_ev, lg_done = (sem(n) for n in ("hn2_ok", "t2_done", "t2_ev", "lg_done"))
    ge_in, ge_out, pe_in, pe_out = (sem(n) for n in ("ge_in", "ge_out", "pe_in", "pe_out"))
    ch_ok, before_done, cnt_done, cnt_ok = (sem(n) for n in ("ch_ok", "before_done", "cnt_done", "cnt_ok"))
    tab_in, tab_done, tab_ok = sem("tab_in"), sem("tab_done"), sem("tab_ok")
    xg_zero = sem("xg_zero")
    ga = [sem(f"ga{s}") for s in range(SLOTS)]
    sca = [sem(f"sca{s}") for s in range(SLOTS)]
    t_done, t_ev = sem("t_done"), sem("t_ev")
    up2_done, e2_done, hh_ok = sem("up2_done"), sem("e2_done"), sem("hh_ok")
    ht_done, ht_ev = sem("ht_done"), sem("ht_ev")
    dn_done, y_ev = sem("dn_done"), sem("y_ev")
    yf_ok = sem("yf_ok")
    passed = sem("passed")
    all_landed = sem("all_landed")

    def apart(eng):
        eng.sem_inc(passed, 1)

    def bc(ap, shape):
        return ap.to_broadcast(shape)

    N_SMALL = 10
    N_MOV_B = 4 * 4
    N_STA = 2 * KD + KD
    N_RT = NG + EXPERTS
    PAIR_STEPS = 3 * NT + NT
    EXPERT_STEPS = 2

    with nc.Block() as block:

        @block.sync
        def _(sp):
            for i in range(2):
                sp.dma_start(xin[:, i, :], frames[i]).then_inc(ld_x[i], 16)
            sp.dma_start(gain_mix[:, :], norm_mix_g.to_broadcast([P, D])).then_inc(ld_first, 16)
            sp.dma_start(cst[:, :], consts).then_inc(ld_first, 16)
            for i in range(2, NT):
                sp.dma_start(xin[:, i, :], frames[i]).then_inc(ld_x[i], 16)
            sp.dma_start(meta_in[:, :], meta_tokens).then_inc(ld_x[NT], 16)
            sp.wait_ge(wf_zero, 1)
            with nc.allow_non_contiguous_dma(reason="small weights, once"):
                sp.dma_start(wf[:, :, 0:HEADS], win[:, :, F_OFF:F_OFF + HEADS]).then_inc(ld_wf, 16)
                sp.dma_start(land_b[0][:, :, :], win[:, :, COLUMNS[ORDER[0]]:COLUMNS[ORDER[0]] + 512]).then_inc(ld_b[0], 16)
                small_loads = (
                    (bias_f[:, :], b_forget.rearrange("a h -> h a")),
                    (gain_q[0:DH, :], q_norm_g.rearrange("a d -> d a")),
                    (gain_q[DH:P, :], q_norm_g.rearrange("a d -> d a")),
                    (gain_k[0:DH, :], k_norm_g.rearrange("a d -> d a")),
                    (gain_k[DH:P, :], k_norm_g.rearrange("a d -> d a")),
                    (scale_pool[:, :], pool_scale[0].rearrange("(g p) -> p g", p=P)),
                    (w_rt[:, :, 0:NG], w_group[0].rearrange("(k p) n -> p k n", p=P)),
                    (w_rt[:, :, NG:], w_router[0].rearrange("(k p) n -> p k n", p=P)),
                    (bias_rt[:, 0:NG], b_group.to_broadcast([P, NG])),
                    (bias_rt[:, NG:], b_router.to_broadcast([P, EXPERTS])),
                )
                assert len(small_loads) == N_SMALL
                for dst, src in small_loads:
                    sp.dma_start(dst, src).then_inc(ld_small, 16)
            for c in range(1, 4):
                off = COLUMNS[ORDER[c]]
                sp.dma_start(land_b[c][:, :, :], win[:, :, off:off + 512]).then_inc(ld_b[c], 16)
            sp.wait_ge(tp_done, 2 * NT + 1)
            sp.dma_start(band[:, :, :, :], bands.rearrange("p (a g t) -> p a g t", a=3, g=NB)).then_inc(ld_pool, 16)
            sp.dma_start(wpool[:, :, :], w_pool[0].rearrange("g c d -> c g d")).then_inc(ld_pool, 16)
            sp.wait_ge(mov_lo, 4)
            sp.wait_ge(meta_done, 1)
            for b in range(2):
                sp.dma_start(land_s[b][:, :, :], win[:, :, G_OFF + 256 * b:G_OFF + 256 * (b + 1)]).then_inc(ld_s[b], 16)
            sp.wait_ge(nf_ok, 1)
            sp.dma_start(nf_rows, nfT[:, :]).then_inc(ld_nf, 16)
            sp.wait_ge(ld_nf, 16)
            nfb_flat = nfb[:, :, :].rearrange("p a s -> p (a s)")
            sp.dma_start(nfb_flat, nf_pairs[0:1, :].to_broadcast([P, 2 * L])).then_inc(ld_nfb, 16)
            with sp.Fori(1, PAIRS) as p:
                for b in range(2):
                    sp.wait_ge(sta_lo, p * 4 + (2 * b - 2))
                    sp.dma_start(land_s[b][:, :, :],
                                 win[:, :, bass.ds(p * 512 + (G_OFF + 256 * b), 256)]).then_inc(ld_s[b], 16)
                sp.wait_ge(s_read, p * NT)
                sp.dma_start(nfb_flat, nf_pairs[bass.ds(p, 1), :].to_broadcast([P, 2 * L])).then_inc(ld_nfb, 16)
            for q in range(4):
                b = q % 2
                sp.wait_ge(sta_lo, 2 * KD - 2 + 2 * q)
                sp.dma_start(land_s[b][:, 0:4, :], wua[:, :, 256 * q:256 * (q + 1)]).then_inc(ld_half, 16)
                sp.wait_ge(ld_half, 16 * (q + 1))
                sp.dma_start(land_s[b][:, 4:8, :], wup[:, :, 256 * q:256 * (q + 1)]).then_inc(ld_s[b], 16)
                if q == 0:
                    sp.dma_start(land_e[0][:, :, :], wout[:, :, 0:512]).then_inc(ld_e[0], 16)
            sp.wait_ge(sta_lo, N_STA)
            sp.dma_start(land_e[1][:, :, :], wout[:, :, 512:1024]).then_inc(ld_e[1], 16)
            sp.wait_ge(mg_lo, KD)
            for i in range(NT):
                sp.dma_start(h2[:, i, :], frames[i]).then_inc(ld_h2, 16)
            sp.dma_start(gain_ffn[:, :], norm_ffn_g.to_broadcast([P, D])).then_inc(ld_gf, 16)

            def load_expert(e, s, used=None):
                if used is not None:
                    sp.wait_ge(up2_done, used)
                sp.dma_start(w13[s][:, 0, :, :], w1e[bass.ds(e, 1)].rearrange("o p h f -> p (o h) f")).then_inc(ld_up[s], 16)
                sp.dma_start(w13[s][:, 1, :, :], w3e[bass.ds(e, 1)].rearrange("o p h f -> p (o h) f")).then_inc(ld_up[s], 16)
                if used is not None:
                    sp.wait_ge(dn_done, used)
                sp.dma_start(w2s[s][:, :, :], w2e[bass.ds(e, 1)].rearrange("o p j d -> p (o j) d")).then_inc(ld_dn[s], 16)

            sp.wait_ge(up_done, KD)
            for s in range(3):
                load_expert(s, s)
            sp.wait_ge(acc_done, 6 * NT)
            load_expert(3, 3)
            sp.wait_ge(st_hn2, 16 * NT)
            load_expert(SLOTS, SLOTS)
            load_expert(2 * SLOTS, 0, 1)
            for s in range(1, SLOTS):
                load_expert(SLOTS + s, s, s + 1)
            for s in range(1, SLOTS):
                load_expert(2 * SLOTS + s, s, SLOTS + s + 1)

            def load_round(r, e0):
                for s in range(SLOTS):
                    load_expert(sp.snap(r * SLOTS + s, min_val=0, max_val=EXPERTS - 1), s, e0 + (s - SLOTS + 1))

            with sp.Fori(3, ROUNDS) as r:
                load_round(r, r * SLOTS)
            sp.wait_ge(cnt_ok, 1)
            fullest = sp.value_load(cmaxi[0:1, 0:1], min_val=0, max_val=SEQ)
            with sp.Fori(1, BLOCKS) as blk:
                with sp.If(fullest > blk * CAP):
                    with sp.Fori(0, ROUNDS) as r:
                        load_round(r, blk * EXPERTS + r * SLOTS)
            sp.wait_ge(all_landed, 1)
            for i in range(NT):
                b = i % 2
                if i >= 2:
                    sp.wait_ge(yf_ok, i - 1)
                for k in range(2):
                    r0 = 2 * (SEQ * k + P * i)
                    sp.dma_start(yfin[:, b, k, :],
                                 y_rows[r0:r0 + 2 * P, :].rearrange("(p h) d -> p (h d)", h=2)).then_inc(ld_y[b], 16)
            for i in range(NT):
                sp.wait_ge(yf_ok, i + 1)
                sp.dma_start(out_rows[i], h2[:, i, :]).then_inc(st_out, 16)
            sp.wait_ge(st_out, 16 * NT)

        @block.gpsimd
        def _(pool):
            pool.memset(wf[:, :, :], 0.0).then_inc(wf_zero, 1)
            pool.wait_ge(ld_first, 32)
            pool.wait_ge(ld_x[NT - 1], 16)
            pool.tensor_tensor(last_x[:, :], xin[:, NT - 1, :], gain_mix[:, :], ALU.mult).then_inc(gained, 1)
            pool.wait_ge(ld_x[NT], 16)
            pool.tensor_tensor(meta_x[:, :], meta_in[:, :], gain_mix[0:META, :], ALU.mult).then_inc(gained, 1)
            pool.wait_ge(t2_done, 2 * NT)
            pool.wait_ge(st_hn2, 16 * NT)
            for s in range(SLOTS):
                last = pool.memset(xg[s][:, :], 0.0)
            last.then_inc(xg_zero, 1)
            last_row, last_result = pool.to_reg(2 * SEQ - 1), pool.to_reg(4 * SEQ - 1)

            def gather(col, s, n, gathers=None, turned=None):
                if gathers is not None:
                    pool.wait_ge(ga[s], gathers)
                    pool.wait_ge(t_done, turned)
                    apart(pool)
                pool.tensor_copy(ixg[s][:, :], idx[:, 0, bass.ds(col, 1)]).then_inc(chain_g, 1)
                pool.wait_ge(chain_g, n)
                apart(pool)
                pool.indirect_dma_start(
                    out=xg[s][:, :], out_offset=None, in_=hn2_rows,
                    in_offset=bass.IndirectOffsetOnAxis(ap=ixg[s][:, 0:1], axis=0),
                    bounds_check=last_row, oob_is_err=False).then_inc(ga[s], 16)

            def scatter(e, col, s, n, scatters=None):
                pool.wait_ge(y_ev, e + 1)
                if scatters is not None:
                    pool.wait_ge(sca[s], scatters)
                apart(pool)
                pool.tensor_copy(ixs[s][:, :], idx[:, 1, bass.ds(col, 1)]).then_inc(chain_g, 1)
                pool.wait_ge(chain_g, n)
                apart(pool)
                pool.indirect_dma_start(
                    out=y_rows, out_offset=bass.IndirectOffsetOnAxis(ap=ixs[s][:, 0:1], axis=0),
                    in_=ye[s][:, :], in_offset=None,
                    bounds_check=last_result, oob_is_err=False).then_inc(sca[s], 16)

            def round_(r, e0, first=False, last=False):
                for s in range(SLOTS):
                    if not last:
                        gather(r * SLOTS + (SLOTS + s), s, e0 * 2 + (SLOTS + 2 * s + 1), e0 * 4 + 16, e0 + (s + 1))
                    scatter(e0 + s, r * SLOTS + s, s, e0 * 2 + (SLOTS + (s + 1 if last else 2 * s + 2)),
                            None if first else e0 * 4)

            pool.wait_ge(tab_ok, 1)
            pool.wait_ge(xg_zero, 1)
            for s in range(SLOTS):
                gather(s, s, s + 1)
            round_(0, 0, first=True)
            with pool.Fori(1, ROUNDS - 1) as r:
                round_(r, r * SLOTS)
            round_(ROUNDS - 1, (ROUNDS - 1) * SLOTS, last=True)
            for s in range(SLOTS):
                pool.wait_ge(sca[s], 16 * ROUNDS)
            pool.wait_ge(cnt_ok, 1)
            fullest = pool.value_load(cmaxi[0:1, 0:1], min_val=0, max_val=SEQ)
            with pool.Fori(1, BLOCKS) as blk:
                with pool.If(fullest > blk * CAP):
                    e0 = blk * EXPERTS
                    pool.wait_ge(tab_ok, blk + 1)
                    for s in range(SLOTS):
                        gather(s, s, e0 * 2 + (s + 1), e0 * 4, e0)
                    with pool.Fori(0, ROUNDS - 1) as r:
                        round_(r, blk * EXPERTS + r * SLOTS)
                    round_(ROUNDS - 1, e0 + (ROUNDS - 1) * SLOTS, last=True)
                    for s in range(SLOTS):
                        pool.wait_ge(sca[s], e0 * 4 + 16 * ROUNDS)
            pool.memset(landed_flag[:, :], 0.0).then_inc(all_landed, 1)

        @block.scalar
        def _(act):
            link = Chain(act, chain_a)

            def estimate(dst, src):
                act.activation(dst, src, ACT.Sqrt).then_inc(rs_est, 1)

            def load_table(function):
                link(act.activation(table_out[:, :], table_in[:, :], function))

            def squares(src, dst, sem, linked):
                act.wait_ge(sem, 16)
                n = src.shape[0]
                ins = act.activation(junk[0:n, :], src, ACT.Square, accum_out=dst)
                if linked:
                    link(ins)
                else:
                    ins.then_inc(sq_sum, 1)

            act.wait_ge(var_ok, 1)
            load_table(ACT.Sqrt)
            squares(xin[:, 0, :], ss[:, 0:1], ld_x[0], False)
            act.wait_ge(var_ok, 2)
            estimate(rstd[:, 0:1], nw1[:, 0:1])
            for i in range(1, NT):
                squares(xin[:, i, :], ss[:, i:i + 1], ld_x[i], True)
            squares(meta_in[:, :], ss[0:META, NT:NT + 1], ld_x[NT], False)
            act.wait_ge(var_ok, 3)
            estimate(rstd[:, 1:], nw1[:, 1:])
            act.wait_ge(ld_wf, 16)
            act.activation(wf_hi[:, :, :], wf[:, :, :], ACT.Copy).then_inc(wf_h, 1)
            act.wait_ge(rstd_ok, 1)
            act.wait_ge(gained, 2)
            act.activation(last_x[:, :], last_x[:, :], ACT.Copy, scale=rstd[:, NT - 1:NT]).then_inc(hn_ok_a, 1)
            act.activation(meta_x[:, :], meta_x[:, :], ACT.Copy, scale=rstd[0:META, NT:NT + 1]).then_inc(hn_ok_a, 1)
            for n in range(2 * NT):
                i, half = n // 2, n % 2
                act.wait_ge(tp_done, n + 1)
                act.activation(hnT[0][:, 4 * half:4 * half + 4, META + P * i:META + P * (i + 1)],
                               ps[n][:, :].rearrange("p (k t) -> p k t", k=4), ACT.Copy).then_inc(hi_ok, 1)
            act.wait_ge(tp_done, 2 * NT + 1)
            act.activation(hnT[0][:, :, 0:META], ps[0][:, 0:KD * META].rearrange("p (k t) -> p k t", k=KD),
                           ACT.Copy).then_inc(hi_ok, 1)

            def move_hi(n, src):
                if n >= 2:
                    c, kp = divmod(n - 2, 4)
                    if kp < 3:
                        act.wait_ge(mov_used, 3 * c + kp + 1)
                    else:
                        act.wait_ge(acc_done, NT * (c + 1))
                act.activation(mov[n % 2][0][:, :, :], src, ACT.Copy).then_inc(mov_hi, 1)

            def evacuate(c):
                for i in (0, 2):
                    act.wait_ge(acc_done, NT * c + i + 1)
                    act.activation(raw[:, ORDER[c], i, :], ps[i][:, :], ACT.Copy).then_inc(acc_ev_a, 1)

            for c in range(4):
                act.wait_ge(ld_b[c], 16)
                for kp in range(4):
                    move_hi(4 * c + kp, land_b[c][:, 2 * kp:2 * kp + 2, :])
                    if kp == 0 and c > 0:
                        evacuate(c - 1)
                if c == 0:
                    act.wait_ge(fx_ok, 1)
                    link(act.activation(fa[:, :], fa[:, :], ACT.Exp))
                    act.activation(fa[:, :], fa[:, :], ACT.Ln, bias=1.0).then_inc(fe_ok, 1)
                if c == 1:
                    act.wait_ge(meta_done, 1)
                    for j in range(3):
                        last = act.activation(rawm[:, j, :], ps[6][32 * j:32 * j + META, :], ACT.Copy)
                    last.then_inc(meta_ev, 1)
                    act.wait_ge(acc_ev_v, 2)
                    act.wait_ge(acc_ev_a, 2)
                    act.wait_ge(meta_ev, 1)
                    act.wait_ge(fsum_ok, 1)
                    act.activation(sqm[:, :], rawm[:, CK, :], ACT.Square)
                    act.activation(sq[:, :, :], raw[:, CK, :, :], ACT.Square).then_inc(sq_sum, 1)
                if c == 2:
                    act.wait_ge(acc_ev_v, 4)
                    act.wait_ge(acc_ev_a, 4)
                    act.wait_ge(var_ok, 4)
                    act.activation(sq[:, :, :], raw[:, CQ, :, :], ACT.Square).then_inc(sq_sum, 1)
                if c == 3:
                    act.wait_ge(var_ok, 5)
                    estimate(rsh[:, :, :, :], nh1[:, :, :, :])
            evacuate(3)
            act.wait_ge(acc_done, 4 * NT)
            act.wait_ge(ld_s[0], 16)
            act.activation(sta[0][0][:, :, :], land_s[0][:, :, 0:P], ACT.Copy).then_inc(sta_hi, 1)

            def exps(n, i):
                w = META + P * (i + 1)
                act.wait_ge(s_read, n)
                for a in range(2):
                    last = act.activation(probs[:, i % 2, a, 0:w], sc[:, a, 0:w], ACT.Exp,
                                          bias=nmx[:, a:a + 1], accum_out=rs[:, i % 2, a:a + 1])
                last.then_inc(e_done, 1)

            act.sem_inc(g_ev, 1)

            def split_hi(p, j):
                b, s = j % 2, j // 2 % 2
                if b == 0:
                    act.wait_ge(ld_s[s], p * 16 + (32 if j == NT else 16))
                act.activation(sta[b][0][:, :, :], land_s[s][:, :, P * b:P * (b + 1)], ACT.Copy).then_inc(sta_hi, 1)

            def gate_out(p, j):
                act.wait_ge(g_done, p * NT + (j + 1))
                act.activation(gates[:, bass.ds(p * NT + j, 1), :].rearrange("p o t -> p (o t)"), ps[0][:, :],
                               ACT.Copy).then_inc(g_ev, 1)

            def turned_out(p, i):
                act.wait_ge(pt_done, p * NT + (i + 1))
                act.activation(pT[:, 0, 0:P * (i + 1)], ps[1][:, 0:P * (i + 1)], ACT.Copy)
                act.activation(pTm[:, :, :].rearrange("p a t -> p (a t)"), ps[6][0:META, 0:2 * P],
                               ACT.Copy).then_inc(pt_ev_a, 1)

            with act.Fori(0, PAIRS) as p:
                split_hi(p, 1)
                act.wait_ge(qk_t, p + 1)
                act.activation(QT[:, :], ps[7][:, :], ACT.Copy, scale=gain_q[:, 0:1]).then_inc(q_ev, 1)
                gate_out(p, 0)
                split_hi(p, 2)
                exps(p * NT + 1, 0)
                turned_out(p, 0)
                gate_out(p, 1)
                exps(p * NT + 2, 1)
                split_hi(p, 3)
                turned_out(p, 1)
                exps(p * NT + 3, 2)
                gate_out(p, 2)
                split_hi(p, 4)
                turned_out(p, 2)
                exps(p * NT + 4, 3)
                turned_out(p, 3)
                gate_out(p, 3)
            for k in BRANCH_K:
                if k == BRANCH_K[4]:
                    act.wait_ge(ot_ev, PAIRS)
                act.activation(brT[0][:, k, :], poolT[:, k - 4, :] if k >= 4 else oT[:, k, :], ACT.Copy).then_inc(br_hi, 1)
            for c in range(KD):
                n = 2 * KD + c + 1
                b, s = n % 2, n // 2 % 2
                if n < N_STA:
                    if b == 0:
                        act.wait_ge(ld_s[s], 16 * (PAIRS + 1 + (n - 2 * KD) // 4))
                    if c >= 1:
                        act.wait_ge(up_done, c)
                    act.activation(sta[b][0][:, :, :], land_s[s][:, :, P * b:P * (b + 1)], ACT.Copy).then_inc(sta_hi, 1)
                if c == KD - 1:
                    act.wait_ge(up_done, c)
                    act.wait_ge(ld_e[0], 16)
                    move_hi(N_MOV_B, land_e[0][:, 0:2, :])
                act.activation(gates[:, c, :], gates[:, c, :], ACT.Sigmoid)
                act.activation(gates[:, KD + c, :], gates[:, KD + c, :], ACT.Sigmoid).then_inc(g_ok, 1)
                act.wait_ge(up_read, c + 1)
                act.activation(mgT[0][:, c, :], mg[c % 2][:, :], ACT.Copy).then_inc(mg_hi, 1)
            act.wait_ge(up_done, KD)
            for c in range(2):
                act.wait_ge(ld_e[c], 16)
                for kp in range(1 - c, 4):
                    move_hi(N_MOV_B + 4 * c + kp, land_e[c][:, 2 * kp:2 * kp + 2, :])
            load_table(ACT.Sqrt)
            for c in range(2):
                for i in range(NT):
                    act.wait_ge(h2_ok, NT * c + i + 1)
                    ins = act.activation(junk2[:, :], h2[:, i, 512 * c:512 * (c + 1)], ACT.Square,
                                         accum_out=ss2[:, c, i:i + 1])
                    if c == 1 and i >= NT - 2:
                        ins.then_inc(sq_sum, 1)
                        if i == NT - 2:
                            act.wait_ge(sq_sum, 5)
                            act.wait_ge(var_ok, 6)
                            estimate(rstd[:, 0:NT - 1], nw1[:, 0:NT - 1])
                    else:
                        link(ins)
            act.wait_ge(var_ok, 7)
            estimate(rstd[:, NT - 1:NT], nw1[:, NT - 1:NT])
            for n in range(2 * NT):
                i = n // 2
                if n % 2 == 0:
                    act.wait_ge(hn2_ok, i + 1)
                    act.dma_start(hn2_rows[2 * P * i:2 * P * (i + 1), :].rearrange("(p h) d -> p (h d)", h=2),
                                  hn2[:, i, :]).then_inc(st_hn2, 16)
                act.wait_ge(t2_done, n + 1)
                act.activation(hn2T[i][:, 4 * (n % 2):4 * (n % 2) + 4, :].rearrange("p k t -> p (k t)"),
                               ps[n % 4][:, :], ACT.Copy).then_inc(t2_ev, 1)
            load_table(ACT.Exp)
            act.wait_ge(ge_in, 1)
            act.activation(gex[:, :, :], gex[:, :, :], ACT.Exp).then_inc(ge_out, 1)
            act.wait_ge(pe_in, 1)
            act.activation(p2[:, :], p2[:, :], ACT.Exp).then_inc(pe_out, 1)
            load_table(ACT.Sigmoid)

            def x_ev(e, b):
                act.wait_ge(t_done, e + 1)
                act.activation(xT[b][:, :], ps[b][:, :], ACT.Copy).then_inc(t_ev, 1)

            def sigmoid(e, b):
                act.wait_ge(up2_done, e + 1)
                act.activation(ex[b][:, :], ps[2 + b][:, 0:P], ACT.Sigmoid).then_inc(e2_done, 1)

            def round_(e0, first=False, last=False):
                for s in range(SLOTS):
                    b = s % 2
                    if not (last and s == SLOTS - 1):
                        sigmoid(e0 + (s + 1), 1 - b)
                    if not (last and s >= SLOTS - 2):
                        x_ev(e0 + (s + 2), b)
                    act.wait_ge(dn_done, e0 + (s + 1))
                    if not first:
                        act.wait_ge(sca[s], e0 * 4)
                    act.activation(ye[s][:, :], ps[6 + b][:, :], ACT.Copy).then_inc(y_ev, 1)

            def first_two(e0):
                x_ev(e0, 0)
                sigmoid(e0, 0)
                x_ev(e0 + 1, 1)

            first_two(0)
            round_(0, first=True)
            with act.Fori(1, ROUNDS - 1) as r:
                round_(r * SLOTS)
            round_(SLOTS * (ROUNDS - 1), last=True)
            act.wait_ge(cnt_ok, 1)
            fullest = act.value_load(cmaxi[0:1, 0:1], min_val=0, max_val=SEQ)
            with act.Fori(1, BLOCKS) as blk:
                with act.If(fullest > blk * CAP):
                    first_two(blk * EXPERTS)
                    with act.Fori(0, ROUNDS - 1) as r:
                        round_(blk * EXPERTS + r * SLOTS)
                    round_(blk * EXPERTS + SLOTS * (ROUNDS - 1), last=True)

        @block.vector
        def _(dve):
            link = Chain(dve, chain_v)
            tt, ts, stt = dve.tensor_tensor, dve.tensor_scalar, dve.scalar_tensor_tensor

            def refine(y, v, t):
                link(dve.reciprocal(y, y))
                link(tt(t, y, y, ALU.mult))
                link(tt(t, t, v, ALU.mult))
                link(ts(t, t, -0.5, 1.5, ALU.mult, ALU.add))
                link(tt(y, y, t, ALU.mult))

            dve.memset(table_in[:, :], 1.0)
            dve.memset(ss[:, :], 1.0).then_inc(var_ok, 1)
            link(dve.memset(ssh[:, :, :, :], 1.0))
            for g, cols in enumerate((slice(0, 1), slice(1, NT + 1))):
                dve.wait_ge(sq_sum, g + 1)
                ts(nw1[:, cols], ss[:, cols], 1.0 / D, EPS, ALU.mult, ALU.add).then_inc(var_ok, 1)
                dve.wait_ge(rs_est, g + 1)
                refine(rstd[:, cols], nw1[:, cols], nw3[:, cols])
                if g == 0:
                    dve.wait_ge(ld_first, 32)
                else:
                    dve.sem_inc(rstd_ok, 1)
                for i in (0,) if g == 0 else (1, 2):
                    stt(xin[:, i, :], xin[:, i, :], rstd[:, i:i + 1], gain_mix[:, :], ALU.mult, ALU.mult).then_inc(hn_ok, 1)
                if g == 1:
                    dve.wait_ge(wf_h, 1)
                    tt(wf_lo[:, :, :], wf[:, :, :], wf_hi[:, :, :].bitcast(F32), ALU.subtract).then_inc(wf_l, 1)
            for n in range(2 * NT):
                i, half = n // 2, n % 2
                at = (slice(None), slice(4 * half, 4 * half + 4), slice(META + P * i, META + P * (i + 1)))
                dve.wait_ge(hi_ok, n + 1)
                tt(hnT[1][at], ps[n][:, :].rearrange("p (k t) -> p k t", k=4), hnT[0][at].bitcast(F32),
                   ALU.subtract).then_inc(lo_ok, 1)
            dve.wait_ge(hi_ok, 2 * NT + 1)
            mps = ps[0][:, 0:KD * META].rearrange("p (k t) -> p k t", k=KD)
            tt(hnT[1][:, :, 0:META], mps, hnT[0][:, :, 0:META].bitcast(F32), ALU.subtract)
            dve.tensor_copy(metaT[:, :, :], mps).then_inc(lo_ok, 1)

            def move_lo(n, src):
                dve.wait_ge(mov_hi, n + 1)
                tt(mov[n % 2][1][:, :, :], src, mov[n % 2][0][:, :, :].bitcast(F32), ALU.subtract).then_inc(mov_lo, 1)

            def evacuate(c):
                for i in (1, 3):
                    dve.wait_ge(acc_done, NT * c + i + 1)
                    dve.tensor_copy(raw[:, ORDER[c], i, :], ps[i][:, :]).then_inc(acc_ev_v, 1)

            by_head = sq[:, :, :].rearrange("p i (h d) -> p (i h) d", d=DH)
            for c in range(4):
                for kp in range(4):
                    move_lo(4 * c + kp, land_b[c][:, 2 * kp:2 * kp + 2, :])
                    if kp == 0 and c > 0:
                        evacuate(c - 1)
                    if kp == 1 and c == 0:
                        dve.wait_ge(f_done, 1)
                        dve.wait_ge(ld_small, 16 * N_SMALL)
                        for n, b in enumerate((5, 7)):
                            last = ts(fx[:, HALF_L * n:HALF_L * (n + 1)], ps[b][0:HEADS, 0:HALF_L], bias_f[:, 0:1], None, ALU.add)
                        link(last)
                        link(ts(fa[:, :], fx[:, :], -1.0, None, ALU.mult))
                        tt(fa[:, :], fa[:, :], fx[:, :], ALU.min).then_inc(fx_ok, 1)
                        link(ts(fx[:, :], fx[:, :], 0.0, None, ALU.min))
                if c == 0:
                    dve.wait_ge(fe_ok, 1)
                    link(tt(fx[:, :], fx[:, :], fa[:, :], ALU.subtract))
                    dve.tensor_tensor_scan(fsum[:, :], bc(ones[0:HEADS, 0:1], [HEADS, L]), fx[:, :], 0.0,
                                           ALU.mult, ALU.add).then_inc(fsum_ok, 1)
                    dve.wait_ge(fsum_ok, 1)
                    ts(nfT[:, :], fsum[:, :], -1.0, None, ALU.mult).then_inc(nf_ok, 1)
                    ts(gain_q[:, :], gain_q[:, :], DH ** -0.5, None, ALU.mult)
                if c == 1:
                    dve.wait_ge(sq_sum, 3)
                    dve.reduce_sum(ssh[0:META, 1, NT, :], sqm[:, :].rearrange("p (h d) -> p h d", h=HEADS), axis=AX.X)
                    dve.reduce_sum(ssh[:, 1, 0:NT, :].rearrange("p i h -> p (i h)"), by_head, axis=AX.X).then_inc(var_ok, 1)
                if c == 2:
                    dve.wait_ge(sq_sum, 4)
                    link(dve.reduce_sum(ssh[:, 0, 0:NT, :].rearrange("p i h -> p (i h)"), by_head, axis=AX.X))
                    ts(nh1[:, :, :, :], ssh[:, :, :, :], 1.0 / DH, EPS, ALU.mult, ALU.add).then_inc(var_ok, 1)
                if c == 3:
                    dve.wait_ge(rs_est, 3)
                    refine(rsh[:, :, :, :], nh1[:, :, :, :], nh2[:, :, :, :])
            evacuate(3)
            dve.wait_ge(fc_done, 1)
            dve.tensor_copy(fcum[:, :, :].rearrange("p i h -> p (i h)"), ps[7][:, 0:NT * HEADS]).then_inc(fc_read, 1)
            for g in range(NB):
                dve.wait_ge(mix_done, g + 1)
                dve.tensor_copy(mixT[:, g, :], ps[4 + g][:, :]).then_inc(mix_ev, 1)
            dve.wait_ge(sta_hi, 1)
            tt(sta[0][1][:, :, :], land_s[0][:, :, 0:P], sta[0][0][:, :, :].bitcast(F32), ALU.subtract).then_inc(sta_lo, 1)
            for g in range(NB):
                dve.wait_ge(pool_done, g + 1)
                ts(poolT[:, g, :], ps[g][:, :], scale_pool[:, g:g + 1], None, ALU.mult).then_inc(pool_ev, 1)

            pair = Chain(dve, chain_c)

            def scores(p, n, i):
                w = META + P * (i + 1)
                dve.wait_ge(s_done, n)
                if i > 0:
                    dve.wait_ge(e_done, n - 1)
                for a in range(2):
                    fc = fcum[:, i, bass.ds(p * 2 + a, 1)]
                    m = min(w, 512)
                    last = stt(sc[:, a, 0:m], ps[2 + a][:, 0:m], fc, nfb[:, a, 0:m], ALU.add, ALU.add)
                    if w > m:
                        last = stt(sc[:, a, m:w], ps[4][:, META * (a + 1):META * (a + 2)], fc, nfb[:, a, m:w],
                                   ALU.add, ALU.add)
                pair(last)
                diag = sc[:, :, META + P * i:META + P * (i + 1)]
                pair(tt(diag, diag, bc(cst[:, C_MASK:C_MASK + P].unsqueeze(1), [P, 2, P]), ALU.add))
                pair(dve.reduce_max(mx[:, :], sc[:, :, 0:w], axis=AX.X))
                ts(nmx[:, :], mx[:, :], -1.0, None, ALU.mult).then_inc(s_read, 1)

            def split_lo(p, j):
                b = j % 2
                dve.wait_ge(sta_hi, p * NT + (j + 1))
                tt(sta[b][1][:, :, :], land_s[j // 2 % 2][:, :, P * b:P * (b + 1)],
                   sta[b][0][:, :, :].bitcast(F32), ALU.subtract).then_inc(sta_lo, 1)

            def turned_out(p, i):
                dve.wait_ge(pt_done, p * NT + (i + 1))
                dve.tensor_copy(pT[:, 1, 0:P * (i + 1)], ps[5][:, 0:P * (i + 1)]).then_inc(pt_ev_v, 1)

            def attended(p, i):
                pair(dve.reciprocal(rinv[:, :], rs[:, i % 2, :]))
                dve.wait_ge(pv_done, p * NT + (i + 1))
                tt(oN[:, :].rearrange("p (a d) -> p a d", a=2), ps[6][:, 2 * P:3 * P].rearrange("p (a d) -> p a d", a=2),
                   bc(rinv[:, :].unsqueeze(2), [P, 2, DH]), ALU.mult).then_inc(o_ev, 1)

            with dve.Fori(0, PAIRS) as p:
                pair.settle(p * PAIR_STEPS)
                for dst, c, j in ((qn, CQ, 0), (kn, CK, 1)):
                    for a in range(2):
                        tt(dst[:, :, DH * a:DH * (a + 1)], raw[:, c, :, bass.ds(p * P + DH * a, DH)],
                           bc(rsh[:, j, 0:NT, bass.ds(p * 2 + a, 1)], [P, NT, DH]), ALU.mult)
                for a in range(2):
                    last = tt(knm[:, DH * a:DH * (a + 1)], rawm[:, CK, bass.ds(p * P + DH * a, DH)],
                              bc(rsh[0:META, 1, NT, bass.ds(p * 2 + a, 1)], [META, DH]), ALU.mult)
                last.then_inc(qk_n, 1)
                split_lo(p, 1)
                dve.wait_ge(qk_t, p + 1)
                ts(KT[:, META:L], ps[5][:, :], gain_k[:, 0:1], None, ALU.mult)
                ts(KT[:, 0:META], ps[4][:, 0:META], gain_k[:, 0:1], None, ALU.mult).then_inc(k_ev, 1)
                dve.wait_ge(ld_nfb, p * 16 + 16)
                scores(p, p * NT + 1, 0)
                split_lo(p, 2)
                for i in range(NT):
                    turned_out(p, i)
                    if i < NT - 1:
                        scores(p, p * NT + (i + 2), i + 1)
                    attended(p, i)
                    if i in (0, 2):
                        split_lo(p, 3 + i // 2)
                dve.wait_ge(ot_done, p * NT + NT)
                dve.tensor_copy(oT[:, bass.ds(p, 1), :].rearrange("p o t -> p (o t)"), ps[7][:, :]).then_inc(ot_ev, 1)
                assert pair.k == PAIR_STEPS, pair.k
            for n, k in enumerate(BRANCH_K):
                dve.wait_ge(br_hi, n + 1)
                tt(brT[1][:, k, :], poolT[:, k - 4, :] if k >= 4 else oT[:, k, :], brT[0][:, k, :].bitcast(F32),
                   ALU.subtract).then_inc(br_lo, 1)
            for c in range(KD):
                n = 2 * KD + c + 1
                b = n % 2
                if n < N_STA:
                    dve.wait_ge(sta_hi, n + 1)
                    tt(sta[b][1][:, :, :], land_s[n // 2 % 2][:, :, P * b:P * (b + 1)],
                       sta[b][0][:, :, :].bitcast(F32), ALU.subtract).then_inc(sta_lo, 1)
                if c == KD - 1:
                    move_lo(N_MOV_B, land_e[0][:, 0:2, :])
                dve.wait_ge(up_done, c + 1)
                dve.wait_ge(g_ok, c + 1)
                tt(mg[c % 2][:, :], ps[c % 2][:, :], gates[:, c, :], ALU.mult)
                link(tt(mg2[c % 2][:, :], ps[2 + c % 2][:, :], gates[:, KD + c, :], ALU.mult))
                tt(mg[c % 2][:, :], mg[c % 2][:, :], mg2[c % 2][:, :], ALU.add).then_inc(up_read, 1)
                dve.wait_ge(mg_hi, c + 1)
                tt(mgT[1][:, c, :], mg[c % 2][:, :], mgT[0][:, c, :].bitcast(F32), ALU.subtract).then_inc(mg_lo, 1)
            def residual(c):
                for i in range(NT):
                    dve.wait_ge(acc_done, (4 + c) * NT + i + 1)
                    half = h2[:, i, 512 * c:512 * (c + 1)]
                    tt(half, half, ps[(4, 0)[c] + i][:, :], ALU.add).then_inc(h2_ok, 1)

            for c in range(2):
                for kp in range(1 - c, 4):
                    move_lo(N_MOV_B + 4 * c + kp, land_e[c][:, 2 * kp:2 * kp + 2, :])
                    if kp == 0 and c == 1:
                        dve.wait_ge(ld_h2, 16 * NT)
                        residual(0)
            residual(1)
            def norm_rows(i):
                stt(hn2[:, i, :], h2[:, i, :], rstd[:, i:i + 1], gain_ffn[:, :], ALU.mult, ALU.mult).then_inc(hn2_ok, 1)

            dve.wait_ge(ld_gf, 16)
            for g, cols in enumerate((slice(0, NT - 1), slice(NT - 1, NT))):
                dve.wait_ge(sq_sum, 5 + g)
                link(tt(ss[:, cols], ss2[:, 0, cols], ss2[:, 1, cols], ALU.add))
                ts(nw1[:, cols], ss[:, cols], 1.0 / D, EPS, ALU.mult, ALU.add).then_inc(var_ok, 1)
                dve.wait_ge(rs_est, 4 + g)
                refine(rstd[:, cols], nw1[:, cols], nw3[:, cols])
                if g == 0:
                    norm_rows(0)
            for i in range(1, NT):
                norm_rows(i)
            link(dve.memset(gl8[:, :, :], -3e38))
            dve.wait_ge(lg_done, NT)
            link(tt(lg[:, :, :], ps[4][:, 0:NT * N_RT].rearrange("p (i n) -> p i n", i=NT),
                    bc(bias_rt[:, :].unsqueeze(1), [P, NT, N_RT]), ALU.add))
            link(dve.tensor_copy(gl8[:, :, 0:NG], lg[:, :, 0:NG]))

            def top8(src):
                for i in range(NT):
                    last = dve.max(top[:, i, :], src[:, i, :])
                link(last)
                for i in range(NT):
                    last = dve.max_index(topi[:, i, :], top[:, i, :], src[:, i, :])
                link(last)

            top8(gl8)
            tt(gex[:, :, :], lg[:, :, 0:NG], bc(top[:, :, 0:1], [P, NT, NG]), ALU.subtract).then_inc(ge_in, 1)
            link(dve.tensor_copy(idf[:, :, 0:1], topi[:, :, 0:1]))
            link(tt(ohg[:, :, :], bc(cst[:, C_I8:C_I8 + NG].unsqueeze(1), [P, NT, NG]), bc(idf[:, :, 0:1], [P, NT, NG]),
                    ALU.is_equal))
            link(tt(cand[:, :].rearrange("p (i g e) -> p i g e", i=NT, g=NG),
                    lg[:, :, NG:].rearrange("p i (g e) -> p i g e", g=NG),
                    bc(ohg[:, :, :].unsqueeze(3), [P, NT, NG, NE]), ALU.mult))
            link(dve.reduce_sum(esel[:, :, :], cand[:, :].rearrange("p (i g e) -> p i e g", i=NT, g=NG), axis=AX.X))
            top8(esel)
            tt(p2[:, :], top[:, :, 1], top[:, :, 0], ALU.subtract).then_inc(pe_in, 1)
            link(dve.tensor_copy(idf[:, :, :], topi[:, :, 0:2]))
            link(tt(oh8[:, :, :, :], bc(cst[:, C_I8:C_I8 + NE].unsqueeze(1).unsqueeze(1), [P, NT, 2, NE]),
                    bc(idf[:, :, :].unsqueeze(3), [P, NT, 2, NE]), ALU.is_equal))
            pk = pick[:, :, :].rearrange("p (i k) (g e) -> p i k g e", k=2, g=NG)
            for k in range(2):
                last = tt(pk[:, :, k, :, :], bc(ohg[:, :, :].unsqueeze(3), [P, NT, NG, NE]),
                          bc(oh8[:, :, k, :].unsqueeze(2), [P, NT, NG, NE]), ALU.mult)
            link(last)
            pki = pick[:, :, :].rearrange("p (i k) e -> p i k e", k=2)
            tt(chosen[:, :, :], pki[:, :, 0, :], pki[:, :, 1, :], ALU.add).then_inc(ch_ok, 1)
            dve.wait_ge(ge_out, 1)
            link(dve.reduce_sum(gtop[:, :], gex[:, :, :], axis=AX.X))
            dve.wait_ge(pe_out, 1)
            link(ts(r2[:, :], p2[:, :], 1.0, None, ALU.add))
            link(tt(r2[:, :], r2[:, :], gtop[:, :], ALU.mult))
            link(dve.reciprocal(gate2[:, :, 0], r2[:, :]))
            link(tt(gate2[:, :, 1], gate2[:, :, 0], p2[:, :], ALU.mult))
            for v, val in enumerate((cst[:, C_VA:C_VA + 2 * NT], cst[:, C_VB:C_VB + 2 * NT],
                                     gate2[:, :, :].rearrange("p i k -> p (i k)"))):
                last = tt(vals[:, :, v, :], pick[:, :, :], bc(val.unsqueeze(2), [P, 2 * NT, EXPERTS]), ALU.mult)
            link(last)
            dve.wait_ge(before_done, 1)
            before = ps[5][:, 0:NT * EXPERTS].rearrange("p (i e) -> p i e", i=NT)
            pci = pickc[:, :, :].rearrange("p (i k) e -> p i k e", k=2)
            for k in range(2):
                last = tt(pci[:, :, k, :], pki[:, :, k, :], before, ALU.mult)
            link(last)
            link(dve.reduce_sum(rank[:, :], pickc[:, :, :], axis=AX.X))

            def make_tables(n, step):
                for h in range(2):
                    ik = slice(NT * h, NT * (h + 1))
                    tt(rank1[:, ik, :], bc(cst[:, C_SLOT:C_SLOT + P].unsqueeze(1), [P, NT, P]),
                       bc(rank[:, ik].unsqueeze(2), [P, NT, P]), ALU.is_equal).then_inc(tab_in, 1)
                dve.wait_ge(tab_done, n)
                tab = ps[7][:, 0:2 * EXPERTS]
                flat = skip[:, :, :].rearrange("p v e -> p (v e)")
                step(ts(flat, tab, 0.0, SKIP, ALU.is_equal, ALU.mult))
                dve.tensor_copy(gslot[:, :], ps[7][:, 2 * EXPERTS:3 * EXPERTS])
                stt(idx[:, :, :].rearrange("p v e -> p (v e)"), tab, cst[:, C_HALF:C_HALF + 1], flat,
                    ALU.add, ALU.add).then_inc(tab_ok, 1)

            make_tables(1, link)
            dve.wait_ge(cnt_done, 1)
            link(dve.reduce_max(cmax[:, :], ps[6][:, 0:EXPERTS], axis=AX.X))
            dve.tensor_copy(cmaxi[:, :], cmax[:, :]).then_inc(cnt_ok, 1)
            dve.wait_ge(tab_ok, 1)
            dve.wait_ge(xg_zero, 1)

            turn = Chain(dve, chain_e)

            def round_(r, e0):
                turn.settle(e0 * EXPERT_STEPS)
                for s in range(SLOTS):
                    b = s % 2
                    turn(dve.tensor_copy(gcol[b][:, :], gslot[:, bass.ds(r * SLOTS + s, 1)]))
                    dve.wait_ge(e2_done, e0 + (s + 1))
                    turn(stt(hh[b][:, :], ps[2 + b][:, 0:P], gcol[b][:, 0:1], ex[b][:, :], ALU.mult, ALU.mult))
                    tt(hh[b][:, :], hh[b][:, :], ps[2 + b][:, P:2 * P], ALU.mult).then_inc(hh_ok, 1)
                    dve.wait_ge(ht_done, e0 + (s + 1))
                    dve.tensor_copy(hhT[b][:, :], ps[4 + b][:, 0:P]).then_inc(ht_ev, 1)
                assert turn.k == EXPERT_STEPS * SLOTS

            with dve.Fori(0, ROUNDS) as r:
                round_(r, r * SLOTS)
            dve.wait_ge(cnt_ok, 1)
            fullest = dve.value_load(cmaxi[0:1, 0:1], min_val=0, max_val=SEQ)
            fill = Chain(dve, chain_t)
            with dve.Fori(1, BLOCKS) as blk:
                with dve.If(fullest > blk * CAP):
                    fill.settle(blk * 2 - 2)
                    fill(ts(rank[:, :], rank[:, :], float(-CAP), None, ALU.add))
                    for s in range(SLOTS):
                        dve.wait_ge(sca[s], blk * (16 * ROUNDS))
                    make_tables(blk + 1, fill)
                    dve.wait_ge(tab_ok, blk + 1)
                    apart(dve)
                    with dve.Fori(0, ROUNDS) as r:
                        round_(r, blk * EXPERTS + r * SLOTS)
            for i in range(NT):
                b = i % 2
                dve.wait_ge(ld_y[b], 32 * (i // 2 + 1))
                link(tt(h2[:, i, :], h2[:, i, :], yfin[:, b, 0, :], ALU.add))
                tt(h2[:, i, :], h2[:, i, :], yfin[:, b, 1, :], ALU.add).then_inc(yf_ok, 1)

        @block.tensor
        def _(pe):
            mm, tp = pe.matmul, pe.transpose

            def split_mm(dst, held, moved, first, final):
                for n, (u, v) in enumerate(((0, 0), (0, 1), (1, 0))):
                    last = mm(dst, held[u], moved[v], start=first and n == 0, stop=final and n == 2)
                return last

            pe.wait_ge(ld_first, 32)
            for n in range(2 * NT):
                i, half = n // 2, n % 2
                if i < NT - 1:
                    pe.wait_ge(hn_ok, i + 1)
                else:
                    pe.wait_ge(hn_ok_a, 1)
                src = xin[:, i, :] if i < NT - 1 else last_x[:, :]
                for j in range(4):
                    k = 4 * half + j
                    last = tp(ps[n][:, P * j:P * (j + 1)], src[:, P * k:P * (k + 1)], ident)
                last.then_inc(tp_done, 1)
            pe.wait_ge(hn_ok_a, 2)
            pe.wait_ge(lo_ok, 1)
            for k in range(KD):
                last = tp(ps[0][:, META * k:META * (k + 1)], meta_x[:, P * k:P * (k + 1)], ident[0:META, 0:META])
            last.then_inc(tp_done, 1)
            pe.wait_ge(lo_ok, 2 * NT + 1)
            pe.wait_ge(wf_l, 1)
            for k in range(KD):
                for n, b in enumerate((5, 7)):
                    last = split_mm(ps[b][:, 0:HALF_L], (wf_hi[:, k, :], wf_lo[:, k, :]),
                                    [h[:, k, HALF_L * n:HALF_L * (n + 1)] for h in hnT], k == 0, k == KD - 1)
            last.then_inc(f_done, 1)

            def accumulate(n0, held, bank0, before=None, ready=None):
                for kp in range(4):
                    pe.wait_ge(mov_lo, n0 + (kp + 1))
                    steps = [(k2, i) for k2 in range(2) for i in range(NT)]
                    for k2, i in steps if kp < 3 else sorted(steps, key=lambda step: step[1]):
                        k = 2 * kp + k2
                        if ready is not None and i == 0:
                            ready(k)
                        if k == 0 and before is not None:
                            before(i)
                        last = split_mm(ps[bank0 + i][:, :],
                                        [h[:, k, held[1] + P * i:held[1] + P * (i + 1)] for h in held[0]],
                                        [mov[kp % 2][n][:, k2, :] for n in range(2)], k == 0, k == KD - 1)
                        if k == KD - 1:
                            last.then_inc(acc_done, 1)
                    if kp < 3:
                        last.then_inc(mov_used, 1)

            accumulate(0, (hnT, META), 0)
            pe.wait_ge(ld_b[ORDER.index(CP)], 16)
            pe.wait_ge(ld_b[ORDER.index(CV)], 16)
            for k in range(KD):
                for j in range(3):
                    last = mm(ps[6][32 * j:32 * j + META, :], metaT[:, k, :], land_b[ORDER.index(j)][:, k, :],
                              start=k == 0, stop=k == KD - 1)
            last.then_inc(meta_done, 1)
            with pe.Fori(1, 4) as c:
                def freed(i):
                    if i % 2 == 0:
                        pe.wait_ge(acc_ev_a, c * 2 + (i // 2 - 1))
                    else:
                        pe.wait_ge(acc_ev_v, c * 2 + (i // 2 - 1))

                accumulate(c * 4, (hnT, META), 0, freed)
            pe.wait_ge(fsum_ok, 1)
            for i in range(NT):
                last = tp(ps[7][:, HEADS * i:HEADS * (i + 1)], fsum[:, META + P * i:META + P * (i + 1)],
                          ident[0:HEADS, 0:HEADS])
            last.then_inc(fc_done, 1)
            pe.wait_ge(ld_pool, 32)
            pe.wait_ge(meta_ev, 1)
            pe.wait_ge(acc_ev_a, 6)
            pe.wait_ge(acc_ev_v, 6)
            for g in range(NB):
                if g == NB - 1:
                    pe.wait_ge(fc_read, 1)
                cols = slice(P * g, P * (g + 1))
                for i in range(NT):
                    dst = ps[4 + g][:, P * i:P * (i + 1)]
                    mm(dst, raw[:, CP, i, cols], band[:, 0, g, :], start=True, stop=False)
                    if i:
                        last = mm(dst, raw[:, CP, i - 1, cols], band[:, 1, g, :], start=False, stop=True)
                    else:
                        last = mm(dst, rawm[:, CP, cols], band[0:META, 2, g, :], start=False, stop=True)
                last.then_inc(mix_done, 1)
            pe.wait_ge(acc_ev_a, 8)
            pe.wait_ge(acc_ev_v, 8)
            for g in range(NB):
                pe.wait_ge(mix_ev, g + 1)
                mm(ps[g][:, :], wpool[:, g, :], mixT[:, g, :], start=True, stop=True).then_inc(pool_done, 1)
            pe.wait_ge(pool_ev, NB)

            def raw_scores(i, a, c0, c1, dst):
                rows = slice(DH * a, DH * (a + 1))
                return mm(dst, QT[rows, P * i:P * (i + 1)], KT[rows, c0:c1], start=True, stop=True)

            def tile_scores(i):
                w = META + P * (i + 1)
                m = min(w, 512)
                for a in range(2):
                    last = raw_scores(i, a, 0, m, ps[2 + a][:, 0:m])
                if w > m:
                    raw_scores(i, 0, m, w, ps[4][:, META:2 * META]).then_inc(s_last, 1)
                else:
                    last.then_inc(s_done, 1)

            def turn_probs(i):
                for a in range(2):
                    for j in range(i + 1):
                        tp(ps[(1, 5)[a]][:, P * j:P * (j + 1)],
                           probs[:, i % 2, a, META + P * j:META + P * (j + 1)], ident)
                for a in range(2):
                    last = tp(ps[6][0:META, P * a:P * (a + 1)], probs[:, i % 2, a, 0:META], ident)
                last.then_inc(pt_done, 1)

            def gate_work(p, u0, n):
                for u in range(u0, u0 + n):
                    j, k = divmod(u, KD)
                    if k == 0:
                        pe.wait_ge(sta_lo, p * NT + (j + 1))
                        pe.wait_ge(g_ev, p * NT + (j + 1))
                    last = split_mm(ps[0][:, :], [sta[j % 2][m][:, k, :] for m in range(2)],
                                    [h[:, k, META:L] for h in hnT], k == 0, k == KD - 1)
                    if k == KD - 1:
                        last.then_inc(g_done, 1)
                return u0 + n

            AFTER_TURN, AFTER_PV = (2, 3, 3, 1), (3, 2, 3, 1)
            with pe.Fori(0, PAIRS) as p:
                u = gate_work(p, 0, 4)
                pe.wait_ge(qk_n, p + 1)
                for i in range(NT):
                    tp(ps[7][:, P * i:P * (i + 1)], qn[:, i, :], ident)
                    tp(ps[5][:, P * i:P * (i + 1)], kn[:, i, :], ident)
                tp(ps[4][:, 0:META], knm[:, :], ident[0:META, 0:META]).then_inc(qk_t, 1)
                u = gate_work(p, u, 4)
                pe.wait_ge(q_ev, p + 1)
                pe.wait_ge(k_ev, p + 1)
                tile_scores(0)
                u = gate_work(p, u, 6)
                for i in range(NT):
                    if i < NT - 1:
                        pe.wait_ge(s_read, p * NT + (i + 1))
                        tile_scores(i + 1)
                    pe.wait_ge(e_done, p * NT + (i + 1))
                    turn_probs(i)
                    if i == NT - 2:
                        pe.wait_ge(s_last, p + 1)
                        raw_scores(NT - 1, 1, 512, L, ps[4][:, 2 * META:3 * META]).then_inc(s_done, 1)
                    u = gate_work(p, u, AFTER_TURN[i])
                    pe.wait_ge(pt_ev_a, p * NT + (i + 1))
                    pe.wait_ge(pt_ev_v, p * NT + (i + 1))
                    for a in range(2):
                        dst = ps[6][:, 2 * P + DH * a:2 * P + DH * (a + 1)]
                        cols = bass.ds(p * P + DH * a, DH)
                        for j in range(i + 1):
                            mm(dst, pT[:, a, P * j:P * (j + 1)], raw[:, CV, j, cols], start=j == 0, stop=False)
                        last = mm(dst, pTm[:, a, :], rawm[:, CV, cols], start=False, stop=True)
                    last.then_inc(pv_done, 1)
                    u = gate_work(p, u, AFTER_PV[i])
                    pe.wait_ge(o_ev, p * NT + (i + 1))
                    tp(ps[7][:, P * i:P * (i + 1)], oN[:, :], ident).then_inc(ot_done, 1)
                assert u == NT * KD

            def up(c0, first):
                for b in range(2):
                    pe.wait_ge(sta_lo, c0 + (2 * KD + b + 1))
                    if not first:
                        pe.wait_ge(up_read, c0 + (b - 1))
                    for n, k in enumerate(BRANCH_K):
                        if first and b == 0:
                            pe.wait_ge(br_lo, n + 1)
                        last = split_mm(ps[2 * (k // 4) + b][:, :], [sta[b][m][:, k, :] for m in range(2)],
                                        [h[:, k, :] for h in brT], k % 4 == 0, k % 4 == 3)
                    last.then_inc(up_done, 1)

            up(0, True)
            with pe.Fori(1, KD // 2) as q:
                up(q * 2, False)
            accumulate(N_MOV_B, (mgT, 0), 4, ready=lambda k: pe.wait_ge(mg_lo, k + 1))
            accumulate(N_MOV_B + 4, (mgT, 0), 0)
            def logits(i):
                pe.wait_ge(t2_ev, 2 * i + 2)
                for k in range(KD):
                    last = mm(ps[4][:, N_RT * i:N_RT * (i + 1)], hn2T[i][:, k, :], w_rt[:, k, :],
                              start=k == 0, stop=k == KD - 1)
                last.then_inc(lg_done, 1)

            for i in range(NT):
                pe.wait_ge(hn2_ok, i + 1)
                for half in range(2):
                    n = 2 * i + half
                    if n >= 4:
                        pe.wait_ge(t2_ev, n - 3)
                    for j in range(4):
                        k = 4 * half + j
                        last = tp(ps[n % 4][:, P * j:P * (j + 1)], hn2[:, i, P * k:P * (k + 1)], ident)
                    last.then_inc(t2_done, 1)
                if i:
                    logits(i - 1)
            logits(NT - 1)
            pe.wait_ge(ch_ok, 1)
            before = ps[5][:, 0:NT * EXPERTS].rearrange("p (i e) -> p i e", i=NT)
            mm(before, tri_strict, chosen[:, :, :], start=True, stop=False)
            for j in range(NT - 1):
                last = mm(before[:, j + 1:NT, :], ones, bc(chosen[:, j:j + 1, :], [P, NT - 1 - j, EXPERTS]),
                          start=False, stop=j == NT - 2)
            last.then_inc(before_done, 1)
            for i in range(NT):
                last = mm(ps[6][:, 0:EXPERTS], ones, chosen[:, i, :], start=i == 0, stop=i == NT - 1)
            last.then_inc(cnt_done, 1)

            def table(n):
                for ik in range(2 * NT):
                    if ik % NT == 0:
                        pe.wait_ge(tab_in, n * 2 + (1 + ik // NT))
                    last = mm(ps[7][:, 0:3 * EXPERTS], rank1[:, ik, :],
                              vals[:, ik, :, :].rearrange("p v e -> p (v e)"), start=ik == 0, stop=ik == 2 * NT - 1)
                last.then_inc(tab_done, 1)

            table(0)

            def turn_rows(s, b, gathers):
                pe.wait_ge(ga[s], gathers)
                xr = xg[s][:, :].rearrange("p (q c) -> p c q", c=4)
                for c in range(4):
                    last = tp(ps[b][:, P * c:P * (c + 1)], xr[:, c, :], ident)
                last.then_inc(t_done, 1)

            def loaded(s, r16):
                return 16 if s == SLOTS else r16 if s == 0 and not (isinstance(r16, int) and r16 == 0) else r16 + 16

            def up_products(s, b, e, r16):
                pe.wait_ge(t_ev, e + 1)
                pe.wait_ge(ld_up[s], loaded(s, r16) * 2)
                for c in range(4):
                    for h in range(2):
                        held = xT[b][:, P * c + CAP * h:P * c + CAP * (h + 1)]
                        for fh in range(2):
                            k = F * c + P * fh
                            last = mm(ps[2 + b][CAP * fh:CAP * (fh + 1), 0:2 * P].rearrange("p (w f) -> p w f", w=2),
                                      held, w13[s][:, :, h, k:k + P],
                                      start=c == 0 and h == 0, stop=c == 3 and h == 1)
                last.then_inc(up2_done, 1)

            def round_(r16, e0, first=False, last_round=False, slot0=0):
                for s in range(SLOTS):
                    b = s % 2
                    if not (last_round and s == SLOTS - 1):
                        up_products(s + 1 if s < SLOTS - 1 else SLOTS if first else 0, 1 - b, e0 + (s + 1),
                                    r16 if s < SLOTS - 1 else r16 + 16)
                    pe.wait_ge(hh_ok, e0 + (s + 1))
                    tp(ps[4 + b][:, 0:P], hh[b][:, :], ident).then_inc(ht_done, 1)
                    if not (last_round and s >= SLOTS - 2):
                        turn_rows((s + 2) % SLOTS, b, r16 + (16 if s < SLOTS - 2 else 32))
                    pe.wait_ge(ht_ev, e0 + (s + 1))
                    w = slot0 if s == 0 else s
                    pe.wait_ge(ld_dn[w], loaded(w, r16))
                    if not (first and s < 2):
                        pe.wait_ge(y_ev, e0 + (s - 1))
                    for j in range(2):
                        for dh in range(2):
                            last = mm(ps[6 + b][CAP * dh:CAP * (dh + 1), :], hhT[b][:, CAP * j:CAP * (j + 1)],
                                      w2s[w][:, j, 512 * dh:512 * (dh + 1)], start=j == 0, stop=j == 1)
                    last.then_inc(dn_done, 1)

            turn_rows(0, 0, 16)
            up_products(0, 0, 0, 0)
            turn_rows(1, 1, 16)
            round_(0, 0, first=True)
            round_(16, SLOTS, slot0=SLOTS)
            with pe.Fori(2, ROUNDS - 1) as r:
                round_(r * 16, r * SLOTS)
            round_(16 * (ROUNDS - 1), SLOTS * (ROUNDS - 1), last_round=True)
            pe.wait_ge(cnt_ok, 1)
            fullest = pe.value_load(cmaxi[0:1, 0:1], min_val=0, max_val=SEQ)
            with pe.Fori(1, BLOCKS) as blk:
                with pe.If(fullest > blk * CAP):
                    pe.wait_ge(y_ev, blk * EXPERTS)
                    table(blk)
                    r16 = blk * (16 * ROUNDS)
                    turn_rows(0, 0, r16 + 16)
                    up_products(0, 0, blk * EXPERTS, r16)
                    turn_rows(1, 1, r16 + 16)
                    with pe.Fori(0, ROUNDS - 1) as r:
                        round_(r16 + r * 16, blk * EXPERTS + r * SLOTS)
                    round_(r16 + 16 * (ROUNDS - 1), blk * EXPERTS + SLOTS * (ROUNDS - 1), last_round=True)


_INS = ["x", "meta_tokens", "norm_mix_g", "w_in", "b_forget", "q_norm_g", "k_norm_g", "w_up_attn", "w_pool",
        "pool_scale", "w_up_pool", "w_out", "norm_ffn_g", "w_group", "b_group", "w_router", "b_router", "w1", "w3", "w2"]


def kernel(**inputs):
    import numpy as np
    import concourse.bacc as bacc
    from concourse.bass_utils import run_bass_kernel_spmd

    nc = bacc.Bacc("TRN2", target_bir_lowering=False, num_devices=1)
    arrays, args = {}, []
    given = {name: np.ascontiguousarray(inputs[name]) for name in _INS}
    given.update(constants())
    for name, a in given.items():
        arrays[f"in_{name}"] = a
        args.append(nc.dram_tensor(f"in_{name}", a.shape, mybir.dt.from_np(a.dtype), kind="ExternalInput").ap())
    args.append(nc.dram_tensor("out_0", (1, SEQ, D), F32, kind="ExternalOutput").ap())
    program(nc, *args)
    r = run_bass_kernel_spmd(nc, [arrays], core_ids=[0])
    return r.results[0]["out_0"]
```

```python
import concourse.bass as bass
from concourse import mybir

F32 = mybir.dt.float32
F32R = mybir.dt.float32r
I32 = mybir.dt.int32
U32 = mybir.dt.uint32
ALU = mybir.AluOpType
ACT = mybir.ActivationFunctionType
AX = mybir.AxisListType

P = 128
D = 1024
KD = D // P
SEQ = 512
NT = SEQ // P
META = 16
L = META + SEQ
HEADS, DH = 8, 64
PAIRS = HEADS // 2
AW = HEADS * DH
NG, NE = 4, 8
EXPERTS = NG * NE
F = 256
CAP = 64
BLOCKS = SEQ // CAP
WINDOWS = (2, 4, 8, 16)
EPS = 1e-6
SKIP = 65536.0
Q_OFF, K_OFF, V_OFF = 0, AW, 2 * AW
F_OFF = 3 * AW
P_OFF = F_OFF + HEADS
G_OFF = P_OFF + AW
CP, CV, CK, CQ = range(4)
ORDER = (CK, CQ, CP, CV)
COLUMNS = (P_OFF, V_OFF, K_OFF, Q_OFF)
SLOTS = 4
ROUNDS = EXPERTS // SLOTS
BRANCH_K = (4, 5, 6, 7, 0, 1, 2, 3)

C_ID, C_TRS, C_ONE, C_MASK, C_SLOT = (P * i for i in range(5))
C_I8 = 5 * P
C_VA = C_I8 + NE
C_VB = C_VA + 2 * NT
C_HALF = C_VB + 2 * NT
C_FOLD = C_HALF + 1
C_END = C_FOLD + NG + EXPERTS
NB = len(WINDOWS)
HALF_L = L // 2


def constants():
    import numpy as np

    i = np.arange(P)
    c = np.zeros((P, C_END), np.float32)
    c[:, C_ID:C_ID + P] = i[:, None] == i[None, :]
    c[:, C_TRS:C_TRS + P] = i[:, None] < i[None, :]
    c[:, C_ONE:C_ONE + P] = 1
    c[:, C_MASK:C_MASK + P] = np.where(i[None, :] <= i[:, None], 0.0, -1e30)
    c[:, C_SLOT:C_SLOT + P] = i[None, :] % CAP
    c[:, C_I8:C_I8 + NE] = np.arange(NE)
    for t in range(NT):
        for k in range(2):
            c[:, C_VA + 2 * t + k] = 2 * (P * t + i) + 1
            c[:, C_VB + 2 * t + k] = 2 * (P * t + i + SEQ * k) + 1
    c[:, C_HALF] = np.where(i < CAP, -1, 0)
    c[:, C_FOLD:C_END] = i[:, None] % (P // 2) == np.arange(NG + EXPERTS)[None, :]
    b = np.zeros((P, 3, NB, P), np.float32)
    for g, w in enumerate(WINDOWS):
        ago = i[None, :] - i[:, None]
        b[:, 0, g] = ((ago >= 0) & (ago < w)) / w - (ago == 0)
        b[:, 1, g] = (ago + P < w) / w
        b[:META, 2, g] = (ago[:META] + META < w) / w
    return {"consts": c, "bands": b.reshape(P, 3 * NB * P)}


class Chain:

    def __init__(self, eng, sem):
        self.eng, self.sem, self.base, self.k = eng, sem, 0, 0

    def __call__(self, ins):
        ins.then_inc(self.sem, 1)
        self.k += 1
        self.eng.wait_ge(self.sem, self.base + self.k)

    def settle(self, base):
        self.base, self.k = base, 0


def program(nc, x, meta_tokens, norm_mix_g, w_in, b_forget, q_norm_g, k_norm_g, w_up_attn, w_pool,
            pool_scale, w_up_pool, w_out, norm_ffn_g, w_group, b_group, w_router, b_router, w1, w3, w2,
            consts, bands, out):
    frames = x[0].rearrange("(i p) d -> i p d", p=P)
    out_rows = out[0].rearrange("(i p) d -> i p d", p=P)
    win = w_in[0].rearrange("(k p) n -> p k n", p=P)
    wua = w_up_attn[0].rearrange("(k p) n -> p k n", p=P)
    wup = w_up_pool[0].rearrange("(k p) n -> p k n", p=P)
    wout = w_out[0].rearrange("(k p) n -> p k n", p=P)
    w1e = w1[0].rearrange("g e (h p c) f -> (g e) p h (c f)", h=2, c=4)
    w3e = w3[0].rearrange("g e (h p c) f -> (g e) p h (c f)", h=2, c=4)
    w2e = w2[0].rearrange("g e (j p) d -> (g e) p j d", p=P)
    hn2_rows = nc.dram_tensor("hn2_rows", [2 * SEQ, D // 2], F32).ap()
    y_rows = nc.dram_tensor("y_rows", [4 * SEQ, D // 2], F32).ap()
    nf_rows = nc.dram_tensor("nf_rows", [HEADS, L], F32).ap()
    nf_pairs = nf_rows.rearrange("(q a) s -> q (a s)", a=2)

    BASE = 16512
    KB = 1024

    def sb(name, shape, at, dt=F32):
        return nc.alloc_sbuf_tensor_at(name, shape, dt, offset=BASE + int(at * KB))

    cst = sb("cst", [P, C_END], 0)
    ident = cst[:, C_ID:C_ID + P]
    tri_strict = cst[:, C_TRS:C_TRS + P]
    ones = cst[:, C_ONE:C_ONE + P]
    fold = cst[:, C_FOLD:C_END]
    small = [3.4375]

    def keep(name, shape, dt=F32):
        n = 1
        for s in shape[1:]:
            n *= s
        t = sb(name, shape, small[0], dt)
        small[0] += -(-n * 4 // 32) * 32 / KB
        assert small[0] <= 11
        return t

    w_rt = keep("w_rt", [P, KD, NG + EXPERTS])
    bias_rt = keep("bias_rt", [P, NG + EXPERTS])
    bias_f = keep("bias_f", [HEADS, 1])
    gain_q = keep("gain_q", [P, 1])
    gain_k = keep("gain_k", [P, 1])
    scale_pool = keep("scale_pool", [P, NB])
    ss = keep("ss", [P, NT + 1])
    ss2 = keep("ss2", [P, 2, NT])
    table_in = keep("table_in", [P, 1])
    table_out = keep("table_out", [P, 1])
    rstd = keep("rstd", [P, NT + 1])
    nw1 = keep("nw1", [P, NT + 1])
    nw3 = keep("nw3", [P, NT + 1])
    metaT = keep("metaT", [P, KD, META])
    ssh = keep("ssh", [P, 2, NT + 1, HEADS])
    rsh = keep("rsh", [P, 2, NT + 1, HEADS])
    nh1 = keep("nh1", [P, 2, NT + 1, HEADS])
    nh2 = keep("nh2", [P, 2, NT + 1, HEADS])
    fcum = keep("fcum", [P, NT, HEADS])
    mx = keep("mx", [P, 2])
    nmx = keep("nmx", [P, 2])
    rs = keep("rs", [P, 2, 2])
    rinv = keep("rinv", [P, 2])

    mov = [[sb(f"mov{b}{n}", [P, 2, 512], 11 + 8 * b + 4 * h, F32R) for h, n in enumerate(("hi", "lo"))]
           for b in range(2)]
    sta = [[sb(f"sta{b}{n}", [P, KD, P], 11 + 8 * b + 4 * h, F32R) for h, n in enumerate(("hi", "lo"))]
           for b in range(2)]
    xin = sb("xin", [P, NT, D], 27)
    gain_mix = sb("gain_mix", [P, D], 43)
    meta_in = sb("meta_in", [META, D], 116)
    junk = sb("junk", [P, D], 124)
    last_x = sb("last_x", [P, D], 128)
    meta_x = sb("meta_x", [META, D], 132)
    band = sb("band", [P, 3, NB, P], 27)
    mixT = sb("mixT", [P, NB, SEQ], 33)
    wpool = sb("wpool", [P, NB, P], 41)
    sq = sb("sq", [P, NT, 512], 154)
    sqm = sb("sqm", [META, 512], 36)
    fx = sb("fx", [HEADS, L], 158)
    nfT = sb("nfT", [HEADS, L], 43)
    fa = sb("fa", [HEADS, L], 45.25)
    fsum = sb("fsum", [HEADS, L], 47.5)
    wf = sb("wf", [P, KD, P], 202)
    wf_hi = sb("wf_hi", [P, KD, P], 194, F32R)
    wf_lo = sb("wf_lo", [P, KD, P], 198, F32R)
    qn = sb("qn", [P, NT, P], 27)
    kn = sb("kn", [P, NT, P], 29)
    knm = sb("knm", [META, P], 31)
    QT = sb("QT", [P, SEQ], 31.5)
    KT = sb("KT", [P, L], 33.5)
    sc = sb("sc", [P, 2, L], 35.75)
    pT = sb("pT", [P, 2, SEQ], 40)
    pTm = sb("pTm", [META, 2, P], 44)
    vN = sb("vN", [P, NT, P], 47)
    vNm = sb("vNm", [META, P], 49)
    probs = sb("probs", [P, 2, 2, L], 194)
    nfb = sb("nfb", [P, 2, L], 202.5)
    land_b = [sb(f"land_b{c}", [P, KD, 512], at) for c, at in enumerate((50, 66, 162, 178))]
    land_s = [sb(f"land_s{b}", [P, KD, 256], 50 + 8 * b) for b in range(2)]
    land_e = [sb("land_e0", [P, KD, 512], 66), sb("land_e1", [P, KD, 512], 50)]
    hnT = [sb(f"hnT_{n}", [P, KD, L], 82 + 17 * h, F32R) for h, n in enumerate(("hi", "lo"))]
    brT = [sb(f"brT_{n}", [P, KD, SEQ], 82 + 16 * h, F32R) for h, n in enumerate(("hi", "lo"))]
    raw = sb("raw", [P, 4, NT, 512], 116)
    poolT = sb("poolT", [P, NB, SEQ], 116)
    rawm = sb("rawm", [META, 3, 512], 148)
    oT = sb("oT", [P, PAIRS, SEQ], 154)
    gates = sb("gates", [P, 2 * KD, SEQ], 162)
    mgT = [sb(f"mgT_{n}", [P, KD, SEQ], 124 + 16 * h, F32R) for h, n in enumerate(("hi", "lo"))]
    mg = [sb(f"mg{b}", [P, SEQ], 27 + 4 * b) for b in range(2)]
    mg2 = [sb(f"mg2{b}", [P, SEQ], 29 + 4 * b) for b in range(2)]
    h2 = sb("h2", [P, NT, D], 27)
    gain_ffn = sb("gain_ffn", [P, D], 43)
    hn2 = sb("hn2", [P, NT, D], 11)
    hn2T = [sb(f"hn2T{i}", [P, KD, P], at) for i, at in enumerate((148, 152, 106.5, 110.5))]
    junk2 = sb("junk2", [P, 512], 156)
    rt = [114.5]

    def route(name, shape, dt=F32):
        n = 1
        for s in shape[1:]:
            n *= s
        t = sb(name, shape, rt[0], dt)
        rt[0] += -(-n * 4 // 32) * 32 / KB
        assert rt[0] <= 124
        return t

    lg = route("lg", [P, NT, NG + EXPERTS])
    gl8 = route("gl8", [P, NT, 8])
    top = route("top", [P, NT, 8])
    topi = route("topi", [P, NT, 8], U32)
    idf = route("idf", [P, NT, 2])
    gex = route("gex", [P, NT, NG])
    gtop = route("gtop", [P, NT])
    ohg = route("ohg", [P, NT, NG])
    esel = route("esel", [P, NT, NE])
    p2 = route("p2", [P, NT])
    r2 = route("r2", [P, NT])
    gate2 = route("gate2", [P, NT, 2])
    oh8 = route("oh8", [P, NT, 2, NE])
    chosen = route("chosen", [P, NT, EXPERTS], F32R)
    rank = route("rank", [P, 2 * NT])
    cmax = route("cmax", [P, 1])
    cmaxi = route("cmaxi", [P, 1], I32)
    skip = route("skip", [P, 2, EXPERTS])
    cand = route("cand", [P, NT * EXPERTS])
    idx = route("idx", [P, 2, EXPERTS], U32)
    gslot = route("gslot", [P, EXPERTS])
    pick = sb("pick", [P, 2 * NT, EXPERTS], 74)
    pickc = sb("pickc", [P, 2 * NT, EXPERTS], 75)
    vals = sb("vals", [P, 2 * NT, 4, EXPERTS], 76, F32R)
    wide = sb("wide", [P, 2 * NT, EXPERTS], 80)
    rank1 = sb("rank1", [P, 2 * NT, P], 43, F32R)
    tri_r = sb("tri_r", [P, P], 47, F32R)
    ones_r = sb("ones_r", [P, P], 47.5, F32R)
    lgT = sb("lgT", [P, SEQ], 48)
    xg = [sb(f"xg{s}", [P, 512], 11 + 2 * s) for s in range(SLOTS)]
    xT = [sb(f"xT{b}", [P, 512], 19 + 2 * b) for b in range(2)]
    ye = [sb(f"ye{s}", [P, 512], 106.5 + 2 * s) for s in range(SLOTS)]
    hh = [sb(f"hh{b}", [P, P], 23 + b / 2) for b in range(2)]
    hhT = [sb(f"hhT{b}", [P, P], 24 + b / 2) for b in range(2)]
    ex = [sb(f"ex{b}", [P, P], 25 + b / 2) for b in range(2)]
    ixg = [sb(f"ixg{s}", [P, 1], 26 + s / 32, U32) for s in range(SLOTS)]
    ixs = [sb(f"ixs{s}", [P, 1], 26.125 + s / 32, U32) for s in range(SLOTS)]
    landed_flag = sb("landed_flag", [P, 1], 26.375)
    gcol = [sb(f"gcol{b}", [P, 1], 26.25 + b / 32) for b in range(2)]
    wslot_at = (82, 159.75, 183.75, 50, 124)
    w13 = [sb(f"w13_{s}", [P, 2, 2, 4 * F], at) for s, at in enumerate(wslot_at)]
    w2s = [sb(f"w2s_{s}", [P, 2, D], at + 16) for s, at in enumerate(wslot_at)]
    yfin = sb("yfin", [P, NT, 2, D], 82)

    ps = [nc.alloc_psum_tensor(f"ps{b}", [P, 512], F32) for b in range(8)]

    def sem(name):
        return nc.alloc_semaphore(name)

    ld_x = [sem(f"ld_x{i}") for i in range(NT + 1)]
    ld_first = sem("ld_first")
    wf_zero, ld_wf = sem("wf_zero"), sem("ld_wf")
    ld_small = sem("ld_small")
    ld_b = [sem(f"ld_b{c}") for c in range(4)]
    ld_pool = sem("ld_pool")
    ld_s = [sem(f"ld_s{b}") for b in range(2)]
    ld_nf = sem("ld_nf")
    ld_nfb = sem("ld_nfb")
    ld_e = [sem(f"ld_e{b}") for b in range(2)]
    ld_h2 = sem("ld_h2")
    ld_gf = sem("ld_gf")
    ld_up = [sem(f"ld_up{s}") for s in range(SLOTS + 1)]
    ld_dn = [sem(f"ld_dn{s}") for s in range(SLOTS + 1)]
    ld_y = [[sem(f"ld_y{i}_{k}") for k in range(2)] for i in range(NT)]
    ld_half = sem("ld_half")
    st_hn2 = sem("st_hn2")
    st_out = sem("st_out")
    chain_v, chain_c, chain_e, chain_t = (sem(f"chain_{n}") for n in "vcet")
    chain_a, chain_g = sem("chain_a"), sem("chain_g")
    sq_sum = sem("sq_sum")
    var_ok = sem("var_ok")
    rs_est = sem("rs_est")
    rstd_ok, gained, hn_ok_a = (sem(n) for n in ("rstd_ok", "gained", "hn_ok_a"))
    hn_ok = sem("hn_ok")
    tp_done = sem("tp_done")
    hi_ok = sem("hi_ok")
    lo_ok = sem("lo_ok")
    wf_h, wf_l = sem("wf_h"), sem("wf_l")
    f_done, fx_ok, fe_ok, fsum_ok = sem("f_done"), sem("fx_ok"), sem("fe_ok"), sem("fsum_ok")
    mov_hi, mov_lo, mov_used = sem("mov_hi"), sem("mov_lo"), sem("mov_used")
    acc_done = sem("acc_done")
    acc_ev_a, acc_ev_v = sem("acc_ev_a"), sem("acc_ev_v")
    meta_done, meta_ev = sem("meta_done"), sem("meta_ev")
    fc_done, fc_read, nf_ok = sem("fc_done"), sem("fc_read"), sem("nf_ok")
    mix_done, mix_ev, pool_done, pool_ev = sem("mix_done"), sem("mix_ev"), sem("pool_done"), sem("pool_ev")
    qk_n = sem("qk_n")
    qk_t = sem("qk_t")
    q_ev, k_ev = sem("q_ev"), sem("k_ev")
    s_last = sem("s_last")
    s_done = sem("s_done")
    s_read = sem("s_read")
    e_done = sem("e_done")
    pt_done, pt_ev_a, pt_ev_v = sem("pt_done"), sem("pt_ev_a"), sem("pt_ev_v")
    pr_ok = sem("pr_ok")
    v_ok = sem("v_ok")
    pv_done, ot_ev = sem("pv_done"), sem("ot_ev")
    sta_hi, sta_lo = sem("sta_hi"), sem("sta_lo")
    g_done, g_ev, g_ok = sem("g_done"), sem("g_ev"), sem("g_ok")
    br_hi, br_lo = sem("br_hi"), sem("br_lo")
    up_done, up_read, mg_hi, mg_lo = sem("up_done"), sem("up_read"), sem("mg_hi"), sem("mg_lo")
    h2_ok = sem("h2_ok")
    hn2_ok, t2_done, t2_ev, lg_done = (sem(n) for n in ("hn2_ok", "t2_done", "t2_ev", "lg_done"))
    flat_ok, lgT_zero, lg_ev, folded = (sem(n) for n in ("flat_ok", "lgT_zero", "lg_ev", "folded"))
    ge_in, ge_out, pe_in, pe_out = (sem(n) for n in ("ge_in", "ge_out", "pe_in", "pe_out"))
    ch_ok, before_done, cnt_done, cnt_ok = (sem(n) for n in ("ch_ok", "before_done", "cnt_done", "cnt_ok"))
    tab_in, weights_in, tab_done, tab_ok = (sem(n) for n in ("tab_in", "weights_in", "tab_done", "tab_ok"))
    xg_zero = sem("xg_zero")
    ga = [sem(f"ga{s}") for s in range(SLOTS)]
    sca = [sem(f"sca{s}") for s in range(SLOTS)]
    t_done, t_ev = sem("t_done"), sem("t_ev")
    up2_done, e2_done, hh_ok = sem("up2_done"), sem("e2_done"), sem("hh_ok")
    ht_done, ht_ev = sem("ht_done"), sem("ht_ev")
    dn_done, y_ev = sem("dn_done"), sem("y_ev")
    yf_ok = sem("yf_ok")
    passed = sem("passed")
    all_landed = sem("all_landed")

    def apart(eng):
        eng.sem_inc(passed, 1)

    def bc(ap, shape):
        return ap.to_broadcast(shape)

    N_SMALL = 10
    N_MOV_B = 4 * 4
    N_STA = 2 * KD + KD
    N_RT = NG + EXPERTS
    PAIR_STEPS = 3 * NT + NT
    EXPERT_STEPS = 2

    with nc.Block() as block:

        @block.sync
        def _(sp):
            for i in range(2):
                sp.dma_start(xin[:, i, :], frames[i]).then_inc(ld_x[i], 16)
            sp.dma_start(gain_mix[:, :], norm_mix_g.to_broadcast([P, D])).then_inc(ld_first, 16)
            sp.dma_start(cst[:, :], consts).then_inc(ld_first, 16)
            for i in range(2, NT):
                sp.dma_start(xin[:, i, :], frames[i]).then_inc(ld_x[i], 16)
            sp.dma_start(meta_in[:, :], meta_tokens).then_inc(ld_x[NT], 16)
            sp.wait_ge(wf_zero, 1)
            with nc.allow_non_contiguous_dma(reason="small weights, once"):
                sp.dma_start(wf[:, :, 0:HEADS], win[:, :, F_OFF:F_OFF + HEADS]).then_inc(ld_wf, 16)
                sp.dma_start(land_b[0][:, :, :], win[:, :, COLUMNS[ORDER[0]]:COLUMNS[ORDER[0]] + 512]).then_inc(ld_b[0], 16)
                small_loads = (
                    (bias_f[:, :], b_forget.rearrange("a h -> h a")),
                    (gain_q[0:DH, :], q_norm_g.rearrange("a d -> d a")),
                    (gain_q[DH:P, :], q_norm_g.rearrange("a d -> d a")),
                    (gain_k[0:DH, :], k_norm_g.rearrange("a d -> d a")),
                    (gain_k[DH:P, :], k_norm_g.rearrange("a d -> d a")),
                    (scale_pool[:, :], pool_scale[0].rearrange("(g p) -> p g", p=P)),
                    (w_rt[:, :, 0:NG], w_group[0].rearrange("(k p) n -> p k n", p=P)),
                    (w_rt[:, :, NG:], w_router[0].rearrange("(k p) n -> p k n", p=P)),
                    (bias_rt[:, 0:NG], b_group.to_broadcast([P, NG])),
                    (bias_rt[:, NG:], b_router.to_broadcast([P, EXPERTS])),
                )
                assert len(small_loads) == N_SMALL
                for dst, src in small_loads:
                    sp.dma_start(dst, src).then_inc(ld_small, 16)
            for c in range(1, 4):
                off = COLUMNS[ORDER[c]]
                sp.dma_start(land_b[c][:, :, :], win[:, :, off:off + 512]).then_inc(ld_b[c], 16)
            sp.wait_ge(tp_done, 2 * NT + 1)
            sp.dma_start(band[:, :, :, :], bands.rearrange("p (a g t) -> p a g t", a=3, g=NB)).then_inc(ld_pool, 16)
            sp.dma_start(wpool[:, :, :], w_pool[0].rearrange("g c d -> c g d")).then_inc(ld_pool, 16)
            sp.wait_ge(mov_lo, 4)
            sp.wait_ge(meta_done, 1)
            for b in range(2):
                sp.dma_start(land_s[b][:, :, :], win[:, :, G_OFF + 256 * b:G_OFF + 256 * (b + 1)]).then_inc(ld_s[b], 16)
            sp.wait_ge(nf_ok, 1)
            sp.dma_start(nf_rows, nfT[:, :]).then_inc(ld_nf, 16)
            sp.wait_ge(ld_nf, 16)
            nfb_flat = nfb[:, :, :].rearrange("p a s -> p (a s)")
            sp.dma_start(nfb_flat, nf_pairs[0:1, :].to_broadcast([P, 2 * L])).then_inc(ld_nfb, 16)
            with sp.Fori(1, PAIRS) as p:
                for b in range(2):
                    sp.wait_ge(sta_lo, p * 4 + (2 * b - 2))
                    sp.dma_start(land_s[b][:, :, :],
                                 win[:, :, bass.ds(p * 512 + (G_OFF + 256 * b), 256)]).then_inc(ld_s[b], 16)
                sp.wait_ge(s_read, p * NT)
                sp.dma_start(nfb_flat, nf_pairs[bass.ds(p, 1), :].to_broadcast([P, 2 * L])).then_inc(ld_nfb, 16)
            for q in range(4):
                b = q % 2
                sp.wait_ge(sta_lo, 2 * KD - 2 + 2 * q)
                sp.dma_start(land_s[b][:, 0:4, :], wua[:, :, 256 * q:256 * (q + 1)]).then_inc(ld_half, 16)
                sp.wait_ge(ld_half, 16 * (q + 1))
                sp.dma_start(land_s[b][:, 4:8, :], wup[:, :, 256 * q:256 * (q + 1)]).then_inc(ld_s[b], 16)
                if q == 0:
                    sp.dma_start(land_e[0][:, :, :], wout[:, :, 0:512]).then_inc(ld_e[0], 16)
            sp.wait_ge(sta_lo, N_STA)
            sp.dma_start(land_e[1][:, :, :], wout[:, :, 512:1024]).then_inc(ld_e[1], 16)
            sp.wait_ge(mg_lo, KD)
            for i in range(NT):
                sp.dma_start(h2[:, i, :], frames[i]).then_inc(ld_h2, 16)
            sp.dma_start(gain_ffn[:, :], norm_ffn_g.to_broadcast([P, D])).then_inc(ld_gf, 16)

            def load_expert(e, s, used=None):
                if used is not None:
                    sp.wait_ge(up2_done, used)
                sp.dma_start(w13[s][:, 0, :, :], w1e[bass.ds(e, 1)].rearrange("o p h f -> p (o h) f")).then_inc(ld_up[s], 16)
                sp.dma_start(w13[s][:, 1, :, :], w3e[bass.ds(e, 1)].rearrange("o p h f -> p (o h) f")).then_inc(ld_up[s], 16)
                if used is not None:
                    sp.wait_ge(dn_done, used)
                sp.dma_start(w2s[s][:, :, :], w2e[bass.ds(e, 1)].rearrange("o p j d -> p (o j) d")).then_inc(ld_dn[s], 16)

            sp.wait_ge(up_done, KD)
            for s in range(3):
                load_expert(s, s)
            sp.wait_ge(mov_lo, N_MOV_B + 8)
            load_expert(3, 3)
            sp.wait_ge(st_hn2, 16 * NT)
            load_expert(SLOTS, SLOTS)
            load_expert(2 * SLOTS, 0, 1)
            for s in range(1, SLOTS):
                load_expert(SLOTS + s, s, s + 1)
            for s in range(1, SLOTS):
                load_expert(2 * SLOTS + s, s, SLOTS + s + 1)

            def load_round(r, e0):
                for s in range(SLOTS):
                    load_expert(sp.snap(r * SLOTS + s, min_val=0, max_val=EXPERTS - 1), s, e0 + (s - SLOTS + 1))

            with sp.Fori(3, ROUNDS) as r:
                load_round(r, r * SLOTS)
            sp.wait_ge(cnt_ok, 1)
            fullest = sp.value_load(cmaxi[0:1, 0:1], min_val=0, max_val=SEQ)
            with sp.If(fullest > CAP):
                with sp.Fori(1, BLOCKS) as blk:
                    with sp.If(fullest > blk * CAP):
                        with sp.Fori(0, ROUNDS) as r:
                            load_round(r, blk * EXPERTS + r * SLOTS)
            sp.wait_ge(all_landed, 1)
            for i in range(NT):
                for k in range(2):
                    r0 = 2 * (SEQ * k + P * i)
                    sp.dma_start(yfin[:, i, k, :],
                                 y_rows[r0:r0 + 2 * P, :].rearrange("(p h) d -> p (h d)", h=2)).then_inc(ld_y[i][k], 16)
            for i in range(NT):
                sp.wait_ge(yf_ok, i + 1)
                sp.dma_start(out_rows[i], h2[:, i, :]).then_inc(st_out, 16)
            sp.wait_ge(st_out, 16 * NT)

        @block.gpsimd
        def _(pool):
            pool.memset(wf[:, :, :], 0.0).then_inc(wf_zero, 1)
            pool.wait_ge(ld_first, 32)
            pool.wait_ge(ld_x[NT - 1], 16)
            pool.tensor_tensor(last_x[:, :], xin[:, NT - 1, :], gain_mix[:, :], ALU.mult).then_inc(gained, 1)
            pool.wait_ge(ld_x[NT], 16)
            pool.tensor_tensor(meta_x[:, :], meta_in[:, :], gain_mix[0:META, :], ALU.mult).then_inc(gained, 1)
            pool.wait_ge(wf_h, 1)
            pool.tensor_tensor(wf_lo[:, :, :], wf[:, :, :], wf_hi[:, :, :].bitcast(F32), ALU.subtract).then_inc(wf_l, 1)

            def pair_v(cols):
                pool.tensor_copy(vN[:, :, :], raw[:, CV, :, cols])
                pool.tensor_copy(vNm[:, :], rawm[:, CV, cols]).then_inc(v_ok, 1)

            pool.wait_ge(acc_ev_a, 8)
            pool.wait_ge(acc_ev_v, 8)
            pool.wait_ge(meta_ev, 1)
            pool.wait_ge(fc_done, 1)
            pair_v(slice(0, P))
            with pool.Fori(1, PAIRS) as p:
                pool.wait_ge(pv_done, p * NT)
                apart(pool)
                pair_v(bass.ds(p * P, P))
            pool.wait_ge(pv_done, PAIRS * NT)
            pool.memset(lgT[:, :], 0.0).then_inc(lgT_zero, 1)
            pool.wait_ge(t2_done, 2 * NT)
            pool.wait_ge(st_hn2, 16 * NT)
            for s in range(SLOTS):
                last = pool.memset(xg[s][:, :], 0.0)
            last.then_inc(xg_zero, 1)
            last_row, last_result = pool.to_reg(2 * SEQ - 1), pool.to_reg(4 * SEQ - 1)

            def gather(col, s, n, gathers=None, turned=None):
                if gathers is not None:
                    pool.wait_ge(ga[s], gathers)
                    pool.wait_ge(t_done, turned)
                    apart(pool)
                pool.tensor_copy(ixg[s][:, :], idx[:, 0, bass.ds(col, 1)]).then_inc(chain_g, 1)
                pool.wait_ge(chain_g, n)
                apart(pool)
                pool.indirect_dma_start(
                    out=xg[s][:, :], out_offset=None, in_=hn2_rows,
                    in_offset=bass.IndirectOffsetOnAxis(ap=ixg[s][:, 0:1], axis=0),
                    bounds_check=last_row, oob_is_err=False).then_inc(ga[s], 16)

            def scatter(e, col, s, n, scatters=None):
                pool.wait_ge(y_ev, e + 1)
                if scatters is not None:
                    pool.wait_ge(sca[s], scatters)
                apart(pool)
                pool.tensor_copy(ixs[s][:, :], idx[:, 1, bass.ds(col, 1)]).then_inc(chain_g, 1)
                pool.wait_ge(chain_g, n)
                apart(pool)
                pool.indirect_dma_start(
                    out=y_rows, out_offset=bass.IndirectOffsetOnAxis(ap=ixs[s][:, 0:1], axis=0),
                    in_=ye[s][:, :], in_offset=None,
                    bounds_check=last_result, oob_is_err=False).then_inc(sca[s], 16)

            def round_(r, e0, first=False, left=2):
                n = e0 * 2 + (SLOTS + (0 if left == 0 else 1))
                for s in range(SLOTS):
                    if left == 2 or left == 1 and s < SLOTS - 1:
                        n += 1
                        gather(r * SLOTS + (SLOTS + 1 + s), (s + 1) % SLOTS, n,
                               e0 * 4 + (16 if s < SLOTS - 1 else 32), e0 + (s + 2))
                    n += 1
                    scatter(e0 + s, r * SLOTS + s, s, n, None if first else e0 * 4)

            def last_rounds(e0):
                for left in (1, 0):
                    round_(ROUNDS - 1 - left, e0 + (ROUNDS - 1 - left) * SLOTS, left=left)

            pool.wait_ge(tab_ok, 1)
            pool.wait_ge(xg_zero, 1)
            for s in range(SLOTS):
                gather(s, s, s + 1)
            gather(SLOTS, 0, SLOTS + 1, 16, 1)
            round_(0, 0, first=True)
            with pool.Fori(1, ROUNDS - 2) as r:
                round_(r, r * SLOTS)
            last_rounds(0)
            for s in range(SLOTS):
                pool.wait_ge(sca[s], 16 * ROUNDS)
            pool.wait_ge(cnt_ok, 1)
            fullest = pool.value_load(cmaxi[0:1, 0:1], min_val=0, max_val=SEQ)
            with pool.If(fullest > CAP):
                with pool.Fori(1, BLOCKS) as blk:
                    with pool.If(fullest > blk * CAP):
                        e0 = blk * EXPERTS
                        pool.wait_ge(tab_ok, blk + 1)
                        for s in range(SLOTS):
                            gather(s, s, e0 * 2 + (s + 1), e0 * 4, e0)
                        gather(SLOTS, 0, e0 * 2 + (SLOTS + 1), e0 * 4 + 16, e0 + 1)
                        with pool.Fori(0, ROUNDS - 2) as r:
                            round_(r, blk * EXPERTS + r * SLOTS)
                        last_rounds(e0)
                        for s in range(SLOTS):
                            pool.wait_ge(sca[s], e0 * 4 + 16 * ROUNDS)
            pool.memset(landed_flag[:, :], 0.0).then_inc(all_landed, 1)

        @block.scalar
        def _(act):
            link = Chain(act, chain_a)

            def estimate(dst, src):
                act.activation(dst, src, ACT.Sqrt).then_inc(rs_est, 1)

            def load_table(function):
                link(act.activation(table_out[:, :], table_in[:, :], function))

            def squares(src, dst, sem, linked):
                act.wait_ge(sem, 16)
                n = src.shape[0]
                ins = act.activation(junk[0:n, :], src, ACT.Square, accum_out=dst)
                if linked:
                    link(ins)
                else:
                    ins.then_inc(sq_sum, 1)

            act.wait_ge(var_ok, 1)
            load_table(ACT.Sqrt)
            squares(xin[:, 0, :], ss[:, 0:1], ld_x[0], True)
            squares(xin[:, 1, :], ss[:, 1:2], ld_x[1], False)
            act.wait_ge(var_ok, 2)
            estimate(rstd[:, 0:2], nw1[:, 0:2])
            for i in range(2, NT):
                squares(xin[:, i, :], ss[:, i:i + 1], ld_x[i], True)
            squares(meta_in[:, :], ss[0:META, NT:NT + 1], ld_x[NT], False)
            act.wait_ge(var_ok, 3)
            estimate(rstd[:, 2:], nw1[:, 2:])
            act.wait_ge(ld_wf, 16)
            act.activation(wf_hi[:, :, :], wf[:, :, :], ACT.Copy).then_inc(wf_h, 1)
            for n in range(2 * NT):
                i, half = n // 2, n % 2
                if n == 4:
                    act.wait_ge(rstd_ok, 1)
                    act.wait_ge(gained, 2)
                    act.activation(last_x[:, :], last_x[:, :], ACT.Copy, scale=rstd[:, NT - 1:NT]).then_inc(hn_ok_a, 1)
                    act.activation(meta_x[:, :], meta_x[:, :], ACT.Copy,
                                   scale=rstd[0:META, NT:NT + 1]).then_inc(hn_ok_a, 1)
                act.wait_ge(tp_done, n + 1)
                act.activation(hnT[0][:, 4 * half:4 * half + 4, META + P * i:META + P * (i + 1)],
                               ps[n][:, :].rearrange("p (k t) -> p k t", k=4), ACT.Copy).then_inc(hi_ok, 1)
            act.wait_ge(tp_done, 2 * NT + 1)
            act.activation(hnT[0][:, :, 0:META], ps[0][:, 0:KD * META].rearrange("p (k t) -> p k t", k=KD),
                           ACT.Copy).then_inc(hi_ok, 1)

            def move_hi(n, src):
                if n >= 2:
                    c, kp = divmod(n - 2, 4)
                    if kp < 3:
                        act.wait_ge(mov_used, 3 * c + kp + 1)
                    else:
                        act.wait_ge(acc_done, NT * (c + 1))
                act.activation(mov[n % 2][0][:, :, :], src, ACT.Copy).then_inc(mov_hi, 1)

            def evacuate(c):
                for i in (0, 2):
                    act.wait_ge(acc_done, NT * c + i + 1)
                    act.activation(raw[:, ORDER[c], i, :], ps[i][:, :], ACT.Copy).then_inc(acc_ev_a, 1)

            for c in range(4):
                act.wait_ge(ld_b[c], 16)
                for kp in range(4):
                    move_hi(4 * c + kp, land_b[c][:, 2 * kp:2 * kp + 2, :])
                    if kp == 0 and c > 0:
                        evacuate(c - 1)
                if c == 0:
                    act.wait_ge(fx_ok, 1)
                    link(act.activation(fa[:, :], fa[:, :], ACT.Exp))
                    act.activation(fa[:, :], fa[:, :], ACT.Ln, bias=1.0).then_inc(fe_ok, 1)
                if c == 1:
                    act.wait_ge(meta_done, 1)
                    for j in range(3):
                        last = act.activation(rawm[:, j, :], ps[6][32 * j:32 * j + META, :], ACT.Copy)
                    last.then_inc(meta_ev, 1)
                    act.wait_ge(acc_ev_v, 2)
                    act.wait_ge(acc_ev_a, 2)
                    act.wait_ge(meta_ev, 1)
                    act.wait_ge(fsum_ok, 1)
                    act.activation(sqm[:, :], rawm[:, CK, :], ACT.Square)
                    act.activation(sq[:, :, :], raw[:, CK, :, :], ACT.Square).then_inc(sq_sum, 1)
                if c == 2:
                    act.wait_ge(acc_ev_v, 4)
                    act.wait_ge(acc_ev_a, 4)
                    act.wait_ge(var_ok, 4)
                    act.activation(sq[:, :, :], raw[:, CQ, :, :], ACT.Square).then_inc(sq_sum, 1)
                if c == 3:
                    act.wait_ge(var_ok, 5)
                    estimate(rsh[:, :, :, :], nh1[:, :, :, :])
            evacuate(3)
            act.wait_ge(acc_done, 4 * NT)
            act.wait_ge(ld_s[0], 16)
            act.activation(sta[0][0][:, :, :], land_s[0][:, :, 0:P], ACT.Copy).then_inc(sta_hi, 1)

            def exps(n, i):
                w = META + P * (i + 1)
                act.wait_ge(s_read, n)
                for a in range(2):
                    last = act.activation(probs[:, i % 2, a, 0:w], sc[:, a, 0:w], ACT.Exp,
                                          bias=nmx[:, a:a + 1], accum_out=rs[:, i % 2, a:a + 1])
                last.then_inc(e_done, 1)

            act.sem_inc(g_ev, 2)

            def split_hi(p, j):
                b, s = j % 2, j // 2 % 2
                if b == 0:
                    act.wait_ge(ld_s[s], p * 16 + (32 if j == NT else 16))
                act.activation(sta[b][0][:, :, :], land_s[s][:, :, P * b:P * (b + 1)], ACT.Copy).then_inc(sta_hi, 1)

            def gate_out(p, j):
                act.wait_ge(g_done, p * NT + (j + 1))
                act.activation(gates[:, bass.ds(p * NT + j, 1), :].rearrange("p o t -> p (o t)"),
                               ps[4 * (j % 2)][:, :], ACT.Copy).then_inc(g_ev, 1)

            def turned_out(p, i):
                act.wait_ge(pt_done, p * NT + (i + 1))
                act.activation(pT[:, 0, 0:P * (i + 1)], ps[1][:, 0:P * (i + 1)], ACT.Copy)
                act.activation(pTm[:, :, :].rearrange("p a t -> p (a t)"), ps[6][0:META, 0:2 * P],
                               ACT.Copy).then_inc(pt_ev_a, 1)

            with act.Fori(0, PAIRS) as p:
                split_hi(p, 1)
                act.wait_ge(qk_t, p + 1)
                act.activation(QT[:, :], ps[7][:, :], ACT.Copy, scale=gain_q[:, 0:1]).then_inc(q_ev, 1)
                exps(p * NT + 1, 0)
                gate_out(p, 0)
                split_hi(p, 2)
                turned_out(p, 0)
                exps(p * NT + 2, 1)
                gate_out(p, 1)
                split_hi(p, 3)
                turned_out(p, 1)
                exps(p * NT + 3, 2)
                turned_out(p, 2)
                gate_out(p, 2)
                split_hi(p, 4)
                exps(p * NT + 4, 3)
                turned_out(p, 3)
                gate_out(p, 3)
            for k in BRANCH_K:
                if k == BRANCH_K[4]:
                    act.wait_ge(ot_ev, PAIRS)
                act.activation(brT[0][:, k, :], poolT[:, k - 4, :] if k >= 4 else oT[:, k, :], ACT.Copy).then_inc(br_hi, 1)
            for c in range(KD):
                n = 2 * KD + c + 1
                b, s = n % 2, n // 2 % 2
                if n < N_STA:
                    if b == 0:
                        act.wait_ge(ld_s[s], 16 * (PAIRS + 1 + (n - 2 * KD) // 4))
                    if c >= 1:
                        act.wait_ge(up_done, c)
                    act.activation(sta[b][0][:, :, :], land_s[s][:, :, P * b:P * (b + 1)], ACT.Copy).then_inc(sta_hi, 1)
                if c == KD - 1:
                    act.wait_ge(up_done, c)
                    act.wait_ge(ld_e[0], 16)
                    move_hi(N_MOV_B, land_e[0][:, 0:2, :])
                act.activation(gates[:, c, :], gates[:, c, :], ACT.Sigmoid)
                act.activation(gates[:, KD + c, :], gates[:, KD + c, :], ACT.Sigmoid).then_inc(g_ok, 1)
                act.wait_ge(up_read, c + 1)
                act.activation(mgT[0][:, c, :], mg[c % 2][:, :], ACT.Copy).then_inc(mg_hi, 1)
            act.wait_ge(up_done, KD)
            for c in range(2):
                act.wait_ge(ld_e[c], 16)
                for kp in range(1 - c, 4):
                    move_hi(N_MOV_B + 4 * c + kp, land_e[c][:, 2 * kp:2 * kp + 2, :])
            act.activation(tri_r[:, :], tri_strict, ACT.Copy)
            act.activation(ones_r[:, :], ones, ACT.Copy).then_inc(flat_ok, 1)
            load_table(ACT.Sqrt)
            for c in range(2):
                for i in range(NT):
                    act.wait_ge(h2_ok, NT * c + i + 1)
                    ins = act.activation(junk2[:, :], h2[:, i, 512 * c:512 * (c + 1)], ACT.Square,
                                         accum_out=ss2[:, c, i:i + 1])
                    if c == 1 and i % 2 == 1:
                        ins.then_inc(sq_sum, 1)
                        if i == 1:
                            act.wait_ge(sq_sum, 5)
                    else:
                        link(ins)
                    if c == 1 and i == 2:
                        act.wait_ge(var_ok, 6)
                        estimate(rstd[:, 0:2], nw1[:, 0:2])
            act.wait_ge(var_ok, 7)
            estimate(rstd[:, 2:NT], nw1[:, 2:NT])
            def logits_out(i):
                act.wait_ge(lg_done, i + 1)
                act.wait_ge(lgT_zero, 1)
                for h in range(2):
                    rows, cols = slice(P // 2 * h, P // 2 * h + N_RT), slice(P * i, P * (i + 1))
                    last = act.activation(lgT[rows, cols], ps[4 + 2 * (i % 2)][rows, 0:P], ACT.Copy)
                last.then_inc(lg_ev, 1)

            for n in range(2 * NT):
                i = n // 2
                if n % 2 == 0:
                    act.wait_ge(hn2_ok, 2 * i + 2)
                    act.dma_start(hn2_rows[2 * P * i:2 * P * (i + 1), :].rearrange("(p h) d -> p (h d)", h=2),
                                  hn2[:, i, :]).then_inc(st_hn2, 16)
                act.wait_ge(t2_done, n + 1)
                act.activation(hn2T[i][:, 4 * (n % 2):4 * (n % 2) + 4, :].rearrange("p k t -> p (k t)"),
                               ps[n % 4][:, :], ACT.Copy).then_inc(t2_ev, 1)
                if n % 2 == 1 and i > 0:
                    logits_out(i - 1)
            logits_out(NT - 1)
            load_table(ACT.Exp)
            act.wait_ge(ge_in, 1)
            act.activation(gex[:, :, :], gex[:, :, :], ACT.Exp).then_inc(ge_out, 1)
            act.wait_ge(pe_in, 1)
            act.activation(p2[:, :], p2[:, :], ACT.Exp).then_inc(pe_out, 1)
            load_table(ACT.Sigmoid)

            def x_ev(e, b):
                act.wait_ge(t_done, e + 1)
                act.activation(xT[b][:, :], ps[b][:, :], ACT.Copy).then_inc(t_ev, 1)

            def sigmoid(e, b):
                act.wait_ge(up2_done, e + 1)
                act.activation(ex[b][:, :], ps[2 + b][:, 0:P], ACT.Sigmoid).then_inc(e2_done, 1)

            def round_(e0, first=False, last=False):
                for s in range(SLOTS):
                    b = s % 2
                    if not (last and s == SLOTS - 1):
                        sigmoid(e0 + (s + 1), 1 - b)
                    act.wait_ge(dn_done, e0 + (s + 1))
                    if not first:
                        act.wait_ge(sca[s], e0 * 4)
                    act.activation(ye[s][:, :], ps[6 + b][:, :], ACT.Copy).then_inc(y_ev, 1)
                    if not (last and s >= SLOTS - 2):
                        x_ev(e0 + (s + 2), b)

            def first_two(e0):
                x_ev(e0, 0)
                sigmoid(e0, 0)
                x_ev(e0 + 1, 1)

            first_two(0)
            round_(0, first=True)
            with act.Fori(1, ROUNDS - 1) as r:
                round_(r * SLOTS)
            round_(SLOTS * (ROUNDS - 1), last=True)
            act.wait_ge(cnt_ok, 1)
            fullest = act.value_load(cmaxi[0:1, 0:1], min_val=0, max_val=SEQ)
            with act.If(fullest > CAP):
                with act.Fori(1, BLOCKS) as blk:
                    with act.If(fullest > blk * CAP):
                        first_two(blk * EXPERTS)
                        with act.Fori(0, ROUNDS - 1) as r:
                            round_(blk * EXPERTS + r * SLOTS)
                        round_(blk * EXPERTS + SLOTS * (ROUNDS - 1), last=True)

        @block.vector
        def _(dve):
            link = Chain(dve, chain_v)
            tt, ts, stt = dve.tensor_tensor, dve.tensor_scalar, dve.scalar_tensor_tensor

            def refine(y, v, t):
                link(dve.reciprocal(y, y))
                link(tt(t, y, y, ALU.mult))
                link(tt(t, t, v, ALU.mult))
                link(ts(t, t, -0.5, 1.5, ALU.mult, ALU.add))
                link(tt(y, y, t, ALU.mult))

            dve.memset(table_in[:, :], 1.0)
            dve.memset(ss[:, :], 1.0).then_inc(var_ok, 1)
            link(dve.memset(ssh[:, :, :, :], 1.0))
            for g, cols in enumerate((slice(0, 2), slice(2, NT + 1))):
                dve.wait_ge(sq_sum, g + 1)
                ts(nw1[:, cols], ss[:, cols], 1.0 / D, EPS, ALU.mult, ALU.add).then_inc(var_ok, 1)
                dve.wait_ge(rs_est, g + 1)
                refine(rstd[:, cols], nw1[:, cols], nw3[:, cols])
                if g == 0:
                    dve.wait_ge(ld_first, 32)
                else:
                    dve.sem_inc(rstd_ok, 1)
                for i in (0, 1) if g == 0 else (2,):
                    stt(xin[:, i, :], xin[:, i, :], rstd[:, i:i + 1], gain_mix[:, :], ALU.mult, ALU.mult).then_inc(hn_ok, 1)
            for n in range(2 * NT):
                i, half = n // 2, n % 2
                at = (slice(None), slice(4 * half, 4 * half + 4), slice(META + P * i, META + P * (i + 1)))
                dve.wait_ge(hi_ok, n + 1)
                tt(hnT[1][at], ps[n][:, :].rearrange("p (k t) -> p k t", k=4), hnT[0][at].bitcast(F32),
                   ALU.subtract).then_inc(lo_ok, 1)
            dve.wait_ge(hi_ok, 2 * NT + 1)
            mps = ps[0][:, 0:KD * META].rearrange("p (k t) -> p k t", k=KD)
            tt(hnT[1][:, :, 0:META], mps, hnT[0][:, :, 0:META].bitcast(F32), ALU.subtract)
            dve.tensor_copy(metaT[:, :, :], mps).then_inc(lo_ok, 1)

            def move_lo(n, src):
                dve.wait_ge(mov_hi, n + 1)
                tt(mov[n % 2][1][:, :, :], src, mov[n % 2][0][:, :, :].bitcast(F32), ALU.subtract).then_inc(mov_lo, 1)

            def evacuate(c):
                for i in (1, 3):
                    dve.wait_ge(acc_done, NT * c + i + 1)
                    dve.tensor_copy(raw[:, ORDER[c], i, :], ps[i][:, :]).then_inc(acc_ev_v, 1)

            by_head = sq[:, :, :].rearrange("p i (h d) -> p (i h) d", d=DH)
            for c in range(4):
                for kp in range(4):
                    move_lo(4 * c + kp, land_b[c][:, 2 * kp:2 * kp + 2, :])
                    if kp == 0 and c > 0:
                        evacuate(c - 1)
                    if kp == 1 and c == 0:
                        dve.wait_ge(f_done, 1)
                        dve.wait_ge(ld_small, 16 * N_SMALL)
                        for n, b in enumerate((5, 7)):
                            last = ts(fx[:, HALF_L * n:HALF_L * (n + 1)], ps[b][0:HEADS, 0:HALF_L], bias_f[:, 0:1], None, ALU.add)
                        link(last)
                        link(ts(fa[:, :], fx[:, :], -1.0, None, ALU.mult))
                        tt(fa[:, :], fa[:, :], fx[:, :], ALU.min).then_inc(fx_ok, 1)
                        link(ts(fx[:, :], fx[:, :], 0.0, None, ALU.min))
                if c == 0:
                    dve.wait_ge(fe_ok, 1)
                    link(tt(fx[:, :], fx[:, :], fa[:, :], ALU.subtract))
                    dve.tensor_tensor_scan(fsum[:, :], bc(ones[0:HEADS, 0:1], [HEADS, L]), fx[:, :], 0.0,
                                           ALU.mult, ALU.add).then_inc(fsum_ok, 1)
                    dve.wait_ge(fsum_ok, 1)
                    ts(nfT[:, :], fsum[:, :], -1.0, None, ALU.mult).then_inc(nf_ok, 1)
                    ts(gain_q[:, :], gain_q[:, :], DH ** -0.5, None, ALU.mult)
                if c == 1:
                    dve.wait_ge(sq_sum, 3)
                    dve.reduce_sum(ssh[0:META, 1, NT, :], sqm[:, :].rearrange("p (h d) -> p h d", h=HEADS), axis=AX.X)
                    dve.reduce_sum(ssh[:, 1, 0:NT, :].rearrange("p i h -> p (i h)"), by_head, axis=AX.X).then_inc(var_ok, 1)
                if c == 2:
                    dve.wait_ge(sq_sum, 4)
                    link(dve.reduce_sum(ssh[:, 0, 0:NT, :].rearrange("p i h -> p (i h)"), by_head, axis=AX.X))
                    ts(nh1[:, :, :, :], ssh[:, :, :, :], 1.0 / DH, EPS, ALU.mult, ALU.add).then_inc(var_ok, 1)
                if c == 3:
                    dve.wait_ge(rs_est, 3)
                    refine(rsh[:, :, :, :], nh1[:, :, :, :], nh2[:, :, :, :])
            evacuate(3)
            dve.wait_ge(fc_done, 1)
            dve.tensor_copy(fcum[:, :, :].rearrange("p i h -> p (i h)"), ps[7][:, 0:NT * HEADS]).then_inc(fc_read, 1)
            for g in range(NB):
                dve.wait_ge(mix_done, g + 1)
                dve.tensor_copy(mixT[:, g, :], ps[4 + g][:, :]).then_inc(mix_ev, 1)
            dve.wait_ge(sta_hi, 1)
            tt(sta[0][1][:, :, :], land_s[0][:, :, 0:P], sta[0][0][:, :, :].bitcast(F32), ALU.subtract).then_inc(sta_lo, 1)
            for g in range(NB):
                dve.wait_ge(pool_done, g + 1)
                ts(poolT[:, g, :], ps[g][:, :], scale_pool[:, g:g + 1], None, ALU.mult).then_inc(pool_ev, 1)

            pair = Chain(dve, chain_c)

            def scores(p, n, i):
                w = META + P * (i + 1)
                dve.wait_ge(s_done, n)
                for a in range(2):
                    fc = fcum[:, i, bass.ds(p * 2 + a, 1)]
                    m = min(w, 512)
                    last = stt(sc[:, a, 0:m], ps[2 + a][:, 0:m], fc, nfb[:, a, 0:m], ALU.add, ALU.add)
                    if w > m:
                        if a == 0:
                            dve.wait_ge(pt_ev_a, p * NT + i)
                        last = stt(sc[:, a, m:w], ps[6][:, 256 + META * a:256 + META * (a + 1)], fc, nfb[:, a, m:w],
                                   ALU.add, ALU.add)
                pair(last)
                diag = sc[:, :, META + P * i:META + P * (i + 1)]
                pair(tt(diag, diag, bc(cst[:, C_MASK:C_MASK + P].unsqueeze(1), [P, 2, P]), ALU.add))
                pair(dve.reduce_max(mx[:, :], sc[:, :, 0:w], axis=AX.X))
                ts(nmx[:, :], mx[:, :], -1.0, None, ALU.mult).then_inc(s_read, 1)

            def split_lo(p, j):
                b = j % 2
                dve.wait_ge(sta_hi, p * NT + (j + 1))
                tt(sta[b][1][:, :, :], land_s[j // 2 % 2][:, :, P * b:P * (b + 1)],
                   sta[b][0][:, :, :].bitcast(F32), ALU.subtract).then_inc(sta_lo, 1)

            def turned_out(p, i):
                dve.wait_ge(pt_done, p * NT + (i + 1))
                dve.tensor_copy(pT[:, 1, 0:P * (i + 1)], ps[5][:, 0:P * (i + 1)]).then_inc(pt_ev_v, 1)

            def normalise(p, i):
                dve.wait_ge(e_done, p * NT + (i + 1))
                pair(dve.reciprocal(rinv[:, :], rs[:, i % 2, :]))
                for a in range(2):
                    row = probs[:, i % 2, a, 0:META + P * (i + 1)]
                    last = ts(row, row, rinv[:, a:a + 1], None, ALU.mult)
                last.then_inc(pr_ok, 1)

            with dve.Fori(0, PAIRS) as p:
                pair.settle(p * PAIR_STEPS)
                for dst, c, j in ((qn, CQ, 0), (kn, CK, 1)):
                    for a in range(2):
                        tt(dst[:, :, DH * a:DH * (a + 1)], raw[:, c, :, bass.ds(p * P + DH * a, DH)],
                           bc(rsh[:, j, 0:NT, bass.ds(p * 2 + a, 1)], [P, NT, DH]), ALU.mult)
                for a in range(2):
                    last = tt(knm[:, DH * a:DH * (a + 1)], rawm[:, CK, bass.ds(p * P + DH * a, DH)],
                              bc(rsh[0:META, 1, NT, bass.ds(p * 2 + a, 1)], [META, DH]), ALU.mult)
                last.then_inc(qk_n, 1)
                split_lo(p, 1)
                dve.wait_ge(qk_t, p + 1)
                ts(KT[:, META:L], ps[5][:, :], gain_k[:, 0:1], None, ALU.mult)
                ts(KT[:, 0:META], ps[6][:, 0:META], gain_k[:, 0:1], None, ALU.mult).then_inc(k_ev, 1)
                dve.wait_ge(ld_nfb, p * 16 + 16)
                scores(p, p * NT + 1, 0)
                for i in range(NT):
                    if i >= 2:
                        split_lo(p, 1 + i)
                    normalise(p, i)
                    if i == 0:
                        split_lo(p, 2)
                    turned_out(p, i)
                    if i < NT - 1:
                        scores(p, p * NT + (i + 2), i + 1)
                dve.wait_ge(pv_done, p * NT + NT)
                dve.tensor_copy(oT[:, bass.ds(p, 1), :].rearrange("p o t -> p (o t)"), ps[7][:, :]).then_inc(ot_ev, 1)
                assert pair.k == PAIR_STEPS, pair.k
            for n, k in enumerate(BRANCH_K):
                dve.wait_ge(br_hi, n + 1)
                tt(brT[1][:, k, :], poolT[:, k - 4, :] if k >= 4 else oT[:, k, :], brT[0][:, k, :].bitcast(F32),
                   ALU.subtract).then_inc(br_lo, 1)
            for c in range(KD):
                n = 2 * KD + c + 1
                b = n % 2
                if n < N_STA:
                    dve.wait_ge(sta_hi, n + 1)
                    tt(sta[b][1][:, :, :], land_s[n // 2 % 2][:, :, P * b:P * (b + 1)],
                       sta[b][0][:, :, :].bitcast(F32), ALU.subtract).then_inc(sta_lo, 1)
                if c == KD - 1:
                    move_lo(N_MOV_B, land_e[0][:, 0:2, :])
                dve.wait_ge(up_done, c + 1)
                dve.wait_ge(g_ok, c + 1)
                tt(mg[c % 2][:, :], ps[c % 2][:, :], gates[:, c, :], ALU.mult)
                link(tt(mg2[c % 2][:, :], ps[2 + c % 2][:, :], gates[:, KD + c, :], ALU.mult))
                tt(mg[c % 2][:, :], mg[c % 2][:, :], mg2[c % 2][:, :], ALU.add).then_inc(up_read, 1)
                dve.wait_ge(mg_hi, c + 1)
                tt(mgT[1][:, c, :], mg[c % 2][:, :], mgT[0][:, c, :].bitcast(F32), ALU.subtract).then_inc(mg_lo, 1)
            def residual(c, tiles=range(NT)):
                for i in tiles:
                    dve.wait_ge(acc_done, (4 + c) * NT + i + 1)
                    half = h2[:, i, 512 * c:512 * (c + 1)]
                    tt(half, half, ps[(4, 0)[c] + i][:, :], ALU.add).then_inc(h2_ok, 1)

            for c in range(2):
                for kp in range(1 - c, 4):
                    move_lo(N_MOV_B + 4 * c + kp, land_e[c][:, 2 * kp:2 * kp + 2, :])
                    if kp == 0 and c == 1:
                        dve.wait_ge(ld_h2, 16 * NT)
                        residual(0)
            def norm_rows(i):
                for cols in (slice(0, 512), slice(512, D)):
                    stt(hn2[:, i, cols], h2[:, i, cols], rstd[:, i:i + 1], gain_ffn[:, cols],
                        ALU.mult, ALU.mult).then_inc(hn2_ok, 1)

            def norm_factors(g):
                cols = slice(2 * g, 2 * g + 2)
                dve.wait_ge(sq_sum, 5 + g)
                link(tt(ss[:, cols], ss2[:, 0, cols], ss2[:, 1, cols], ALU.add))
                ts(nw1[:, cols], ss[:, cols], 1.0 / D, EPS, ALU.mult, ALU.add).then_inc(var_ok, 1)
                dve.wait_ge(rs_est, 4 + g)
                refine(rstd[:, cols], nw1[:, cols], nw3[:, cols])

            residual(1, (0, 1, 2))
            norm_factors(0)
            residual(1, (3,))
            dve.wait_ge(ld_gf, 16)
            norm_rows(0)
            norm_factors(1)
            for i in range(1, NT):
                norm_rows(i)
            link(dve.memset(gl8[:, :, :], -3e38))
            dve.wait_ge(folded, 1)
            link(tt(lg[:, :, :], ps[5][:, 0:NT * N_RT].rearrange("p (i n) -> p i n", i=NT),
                    bc(bias_rt[:, :].unsqueeze(1), [P, NT, N_RT]), ALU.add))
            link(dve.tensor_copy(gl8[:, :, 0:NG], lg[:, :, 0:NG]))

            def top8(src):
                for i in range(NT):
                    last = dve.max(top[:, i, :], src[:, i, :])
                link(last)
                for i in range(NT):
                    last = dve.max_index(topi[:, i, :], top[:, i, :], src[:, i, :])
                link(last)

            top8(gl8)
            tt(gex[:, :, :], lg[:, :, 0:NG], bc(top[:, :, 0:1], [P, NT, NG]), ALU.subtract).then_inc(ge_in, 1)
            link(dve.tensor_copy(idf[:, :, 0:1], topi[:, :, 0:1]))
            link(tt(ohg[:, :, :], bc(cst[:, C_I8:C_I8 + NG].unsqueeze(1), [P, NT, NG]), bc(idf[:, :, 0:1], [P, NT, NG]),
                    ALU.is_equal))
            link(tt(cand[:, :].rearrange("p (i g e) -> p i g e", i=NT, g=NG),
                    lg[:, :, NG:].rearrange("p i (g e) -> p i g e", g=NG),
                    bc(ohg[:, :, :].unsqueeze(3), [P, NT, NG, NE]), ALU.mult))
            link(dve.reduce_sum(esel[:, :, :], cand[:, :].rearrange("p (i g e) -> p i e g", i=NT, g=NG), axis=AX.X))
            top8(esel)
            tt(p2[:, :], top[:, :, 1], top[:, :, 0], ALU.subtract).then_inc(pe_in, 1)
            link(dve.tensor_copy(idf[:, :, :], topi[:, :, 0:2]))
            link(tt(oh8[:, :, :, :], bc(cst[:, C_I8:C_I8 + NE].unsqueeze(1).unsqueeze(1), [P, NT, 2, NE]),
                    bc(idf[:, :, :].unsqueeze(3), [P, NT, 2, NE]), ALU.is_equal))
            pk = pick[:, :, :].rearrange("p (i k) (g e) -> p i k g e", k=2, g=NG)
            for k in range(2):
                last = tt(pk[:, :, k, :, :], bc(ohg[:, :, :].unsqueeze(3), [P, NT, NG, NE]),
                          bc(oh8[:, :, k, :].unsqueeze(2), [P, NT, NG, NE]), ALU.mult)
            link(last)
            pki = pick[:, :, :].rearrange("p (i k) e -> p i k e", k=2)
            tt(chosen[:, :, :], pki[:, :, 0, :], pki[:, :, 1, :], ALU.add).then_inc(ch_ok, 1)
            for v, at in enumerate((C_VA, C_VB)):
                last = tt(vals[:, :, v, :], pick[:, :, :],
                          bc(cst[:, at:at + 2 * NT].unsqueeze(2), [P, 2 * NT, EXPERTS]), ALU.mult)
            link(last)
            dve.wait_ge(before_done, 1)
            before = ps[0][:, 0:NT * EXPERTS].rearrange("p (i e) -> p i e", i=NT)
            pci = pickc[:, :, :].rearrange("p (i k) e -> p i k e", k=2)
            for k in range(2):
                last = tt(pci[:, :, k, :], pki[:, :, k, :], before, ALU.mult)
            link(last)
            link(dve.reduce_sum(rank[:, :], pickc[:, :, :], axis=AX.X))

            def one_hot_ranks():
                for h in range(2):
                    ik = slice(NT * h, NT * (h + 1))
                    tt(rank1[:, ik, :], bc(cst[:, C_SLOT:C_SLOT + P].unsqueeze(1), [P, NT, P]),
                       bc(rank[:, ik].unsqueeze(2), [P, NT, P]), ALU.is_equal).then_inc(tab_in, 1)

            def slot_rows(tables, step):
                dve.wait_ge(tab_done, tables)
                tab = ps[7][:, 0:2 * EXPERTS]
                flat = skip[:, :, :].rearrange("p v e -> p (v e)")
                step(ts(flat, tab, 0.0, SKIP, ALU.is_equal, ALU.mult))
                stt(idx[:, :, :].rearrange("p v e -> p (v e)"), tab, cst[:, C_HALF:C_HALF + 1], flat,
                    ALU.add, ALU.add).then_inc(tab_ok, 1)

            def slot_weights(tables, step):
                dve.wait_ge(tab_done, tables)
                step(dve.tensor_copy(gslot[:, :], ps[5][:, 0:EXPERTS]))
                step(tt(gslot[:, :], gslot[:, :], ps[5][:, EXPERTS:2 * EXPERTS], ALU.add))

            one_hot_ranks()
            dve.wait_ge(ge_out, 1)
            link(dve.reduce_sum(gtop[:, :], gex[:, :, :], axis=AX.X))
            dve.wait_ge(pe_out, 1)
            link(ts(r2[:, :], p2[:, :], 1.0, None, ALU.add))
            link(tt(r2[:, :], r2[:, :], gtop[:, :], ALU.mult))
            link(dve.reciprocal(gate2[:, :, 0], r2[:, :]))
            link(tt(gate2[:, :, 1], gate2[:, :, 0], p2[:, :], ALU.mult))
            slot_rows(1, link)
            link(tt(wide[:, :, :], pick[:, :, :], bc(gate2[:, :, :].rearrange("p i k -> p (i k)").unsqueeze(2),
                                                   [P, 2 * NT, EXPERTS]), ALU.mult))
            link(dve.tensor_copy(vals[:, :, 2, :], wide[:, :, :]))
            tt(vals[:, :, 3, :], wide[:, :, :], vals[:, :, 2, :].bitcast(F32), ALU.subtract).then_inc(weights_in, 1)
            slot_weights(2, link)
            dve.wait_ge(cnt_done, 1)
            link(dve.reduce_max(cmax[:, :], ps[6][:, 0:EXPERTS], axis=AX.X))
            dve.tensor_copy(cmaxi[:, :], cmax[:, :]).then_inc(cnt_ok, 1)
            dve.wait_ge(tab_ok, 1)
            dve.wait_ge(xg_zero, 1)

            turn = Chain(dve, chain_e)

            def round_(r, e0):
                turn.settle(e0 * EXPERT_STEPS)
                for s in range(SLOTS):
                    b = s % 2
                    turn(dve.tensor_copy(gcol[b][:, :], gslot[:, bass.ds(r * SLOTS + s, 1)]))
                    dve.wait_ge(e2_done, e0 + (s + 1))
                    turn(stt(hh[b][:, :], ps[2 + b][:, 0:P], gcol[b][:, 0:1], ex[b][:, :], ALU.mult, ALU.mult))
                    tt(hh[b][:, :], hh[b][:, :], ps[2 + b][:, P:2 * P], ALU.mult).then_inc(hh_ok, 1)
                    dve.wait_ge(ht_done, e0 + (s + 1))
                    dve.tensor_copy(hhT[b][:, :], ps[4 + b][:, 0:P]).then_inc(ht_ev, 1)
                assert turn.k == EXPERT_STEPS * SLOTS

            with dve.Fori(0, ROUNDS) as r:
                round_(r, r * SLOTS)
            dve.wait_ge(cnt_ok, 1)
            fullest = dve.value_load(cmaxi[0:1, 0:1], min_val=0, max_val=SEQ)
            fill = Chain(dve, chain_t)
            with dve.If(fullest > CAP):
                with dve.Fori(1, BLOCKS) as blk:
                    with dve.If(fullest > blk * CAP):
                        fill.settle(blk * 4 - 4)
                        fill(ts(rank[:, :], rank[:, :], float(-CAP), None, ALU.add))
                        for s in range(SLOTS):
                            dve.wait_ge(sca[s], blk * (16 * ROUNDS))
                        one_hot_ranks()
                        slot_rows(blk * 2 + 1, fill)
                        slot_weights(blk * 2 + 2, fill)
                        dve.wait_ge(tab_ok, blk + 1)
                        apart(dve)
                        with dve.Fori(0, ROUNDS) as r:
                            round_(r, blk * EXPERTS + r * SLOTS)
            for i in range(NT):
                dve.wait_ge(ld_y[i][0], 16)
                link(tt(h2[:, i, :], h2[:, i, :], yfin[:, i, 0, :], ALU.add))
                dve.wait_ge(ld_y[i][1], 16)
                tt(h2[:, i, :], h2[:, i, :], yfin[:, i, 1, :], ALU.add).then_inc(yf_ok, 1)

        @block.tensor
        def _(pe):
            mm, tp = pe.matmul, pe.transpose

            def split_mm(dst, held, moved, first, final):
                for n, (u, v) in enumerate(((0, 0), (0, 1), (1, 0))):
                    last = mm(dst, held[u], moved[v], start=first and n == 0, stop=final and n == 2)
                return last

            pe.wait_ge(ld_first, 32)
            for n in range(2 * NT):
                i, half = n // 2, n % 2
                if i < NT - 1:
                    pe.wait_ge(hn_ok, i + 1)
                else:
                    pe.wait_ge(hn_ok_a, 1)
                src = xin[:, i, :] if i < NT - 1 else last_x[:, :]
                for j in range(4):
                    k = 4 * half + j
                    last = tp(ps[n][:, P * j:P * (j + 1)], src[:, P * k:P * (k + 1)], ident)
                last.then_inc(tp_done, 1)
            pe.wait_ge(hn_ok_a, 2)
            pe.wait_ge(lo_ok, 1)
            for k in range(KD):
                last = tp(ps[0][:, META * k:META * (k + 1)], meta_x[:, P * k:P * (k + 1)], ident[0:META, 0:META])
            last.then_inc(tp_done, 1)
            pe.wait_ge(lo_ok, 2 * NT + 1)
            pe.wait_ge(wf_l, 1)
            for k in range(KD):
                for n, b in enumerate((5, 7)):
                    last = split_mm(ps[b][:, 0:HALF_L], (wf_hi[:, k, :], wf_lo[:, k, :]),
                                    [h[:, k, HALF_L * n:HALF_L * (n + 1)] for h in hnT], k == 0, k == KD - 1)
            last.then_inc(f_done, 1)

            def accumulate(n0, held, bank0, before=None, ready=None):
                for kp in range(4):
                    pe.wait_ge(mov_lo, n0 + (kp + 1))
                    steps = [(k2, i) for k2 in range(2) for i in range(NT)]
                    for k2, i in steps if kp < 3 else sorted(steps, key=lambda step: step[1]):
                        k = 2 * kp + k2
                        if ready is not None and i == 0:
                            ready(k)
                        if k == 0 and before is not None:
                            before(i)
                        last = split_mm(ps[bank0 + i][:, :],
                                        [h[:, k, held[1] + P * i:held[1] + P * (i + 1)] for h in held[0]],
                                        [mov[kp % 2][n][:, k2, :] for n in range(2)], k == 0, k == KD - 1)
                        if k == KD - 1:
                            last.then_inc(acc_done, 1)
                    if kp < 3:
                        last.then_inc(mov_used, 1)

            accumulate(0, (hnT, META), 0)
            pe.wait_ge(ld_b[ORDER.index(CP)], 16)
            pe.wait_ge(ld_b[ORDER.index(CV)], 16)
            for k in range(KD):
                for j in range(3):
                    last = mm(ps[6][32 * j:32 * j + META, :], metaT[:, k, :], land_b[ORDER.index(j)][:, k, :],
                              start=k == 0, stop=k == KD - 1)
            last.then_inc(meta_done, 1)
            with pe.Fori(1, 4) as c:
                def freed(i):
                    if i % 2 == 0:
                        pe.wait_ge(acc_ev_a, c * 2 + (i // 2 - 1))
                    else:
                        pe.wait_ge(acc_ev_v, c * 2 + (i // 2 - 1))

                accumulate(c * 4, (hnT, META), 0, freed)
            pe.wait_ge(fsum_ok, 1)
            for i in range(NT):
                last = tp(ps[7][:, HEADS * i:HEADS * (i + 1)], fsum[:, META + P * i:META + P * (i + 1)],
                          ident[0:HEADS, 0:HEADS])
            last.then_inc(fc_done, 1)
            pe.wait_ge(ld_pool, 32)
            pe.wait_ge(meta_ev, 1)
            pe.wait_ge(acc_ev_a, 6)
            pe.wait_ge(acc_ev_v, 6)
            for g in range(NB):
                if g == NB - 1:
                    pe.wait_ge(fc_read, 1)
                cols = slice(P * g, P * (g + 1))
                for i in range(NT):
                    dst = ps[4 + g][:, P * i:P * (i + 1)]
                    mm(dst, raw[:, CP, i, cols], band[:, 0, g, :], start=True, stop=False)
                    if i:
                        last = mm(dst, raw[:, CP, i - 1, cols], band[:, 1, g, :], start=False, stop=True)
                    else:
                        last = mm(dst, rawm[:, CP, cols], band[0:META, 2, g, :], start=False, stop=True)
                last.then_inc(mix_done, 1)
            pe.wait_ge(acc_ev_a, 8)
            pe.wait_ge(acc_ev_v, 8)
            for g in range(NB):
                pe.wait_ge(mix_ev, g + 1)
                mm(ps[g][:, :], wpool[:, g, :], mixT[:, g, :], start=True, stop=True).then_inc(pool_done, 1)
            pe.wait_ge(pool_ev, 1)

            def raw_scores(i, a, c0, c1, dst):
                rows = slice(DH * a, DH * (a + 1))
                return mm(dst, QT[rows, P * i:P * (i + 1)], KT[rows, c0:c1], start=True, stop=True)

            def tile_scores(i):
                w = META + P * (i + 1)
                m = min(w, 512)
                for a in range(2):
                    last = raw_scores(i, a, 0, m, ps[2 + a][:, 0:m])
                if w > m:
                    raw_scores(i, 0, m, w, ps[6][:, 256:256 + META]).then_inc(s_last, 1)
                else:
                    last.then_inc(s_done, 1)

            def turn_probs(p, i):
                for a in range(2):
                    for j in range(i + 1):
                        tp(ps[(1, 5)[a]][:, P * j:P * (j + 1)],
                           probs[:, i % 2, a, META + P * j:META + P * (j + 1)], ident)
                if i == NT - 2:
                    pe.wait_ge(s_last, p + 1)
                    raw_scores(NT - 1, 1, 512, L, ps[6][:, 256 + META:256 + 2 * META]).then_inc(s_done, 1)
                for a in range(2):
                    last = tp(ps[6][0:META, P * a:P * (a + 1)], probs[:, i % 2, a, 0:META], ident)
                last.then_inc(pt_done, 1)

            def gate_work(p, u0, n):
                for u in range(u0, u0 + n):
                    j, k = divmod(u, KD)
                    if k == 0:
                        pe.wait_ge(sta_lo, p * NT + (j + 1))
                        pe.wait_ge(g_ev, p * NT + (j + 1))
                    last = split_mm(ps[4 * (j % 2)][:, :], [sta[j % 2][m][:, k, :] for m in range(2)],
                                    [h[:, k, META:L] for h in hnT], k == 0, k == KD - 1)
                    if k == KD - 1:
                        last.then_inc(g_done, 1)
                return u0 + n

            AFTER_TURN, AFTER_PV = (5, 3, 2, 2), (1, 2, 7, 0)
            with pe.Fori(0, PAIRS) as p:
                u = gate_work(p, 0, 4)
                pe.wait_ge(qk_n, p + 1)
                for i in range(NT):
                    tp(ps[7][:, P * i:P * (i + 1)], qn[:, i, :], ident)
                    tp(ps[5][:, P * i:P * (i + 1)], kn[:, i, :], ident)
                tp(ps[6][:, 0:META], knm[:, :], ident[0:META, 0:META]).then_inc(qk_t, 1)
                u = gate_work(p, u, 2)
                pe.wait_ge(q_ev, p + 1)
                pe.wait_ge(k_ev, p + 1)
                tile_scores(0)
                u = gate_work(p, u, 4)
                for i in range(NT):
                    if i < NT - 1:
                        pe.wait_ge(s_read, p * NT + (i + 1))
                        tile_scores(i + 1)
                    pe.wait_ge(pr_ok, p * NT + (i + 1))
                    turn_probs(p, i)
                    u = gate_work(p, u, AFTER_TURN[i])
                    pe.wait_ge(pt_ev_a, p * NT + (i + 1))
                    pe.wait_ge(pt_ev_v, p * NT + (i + 1))
                    if i == 0:
                        pe.wait_ge(v_ok, p + 1)
                    for j in range(i + 2):
                        for a in range(2):
                            head = slice(DH * a, DH * (a + 1))
                            held, moved = ((vN[:, j, head], pT[:, a, P * j:P * (j + 1)]) if j <= i else
                                           (vNm[:, head], pTm[:, a, :]))
                            last = mm(ps[7][head, P * i:P * (i + 1)], held, moved, start=j == 0, stop=j == i + 1)
                    last.then_inc(pv_done, 1)
                    u = gate_work(p, u, AFTER_PV[i])
                assert u == NT * KD

            def up(c0, first):
                for b in range(2):
                    pe.wait_ge(sta_lo, c0 + (2 * KD + b + 1))
                    if not first:
                        pe.wait_ge(up_read, c0 + (b - 1))
                    for n, k in enumerate(BRANCH_K):
                        if first and b == 0:
                            pe.wait_ge(br_lo, n + 1)
                        last = split_mm(ps[2 * (k // 4) + b][:, :], [sta[b][m][:, k, :] for m in range(2)],
                                        [h[:, k, :] for h in brT], k % 4 == 0, k % 4 == 3)
                    last.then_inc(up_done, 1)

            up(0, True)
            with pe.Fori(1, KD // 2) as q:
                up(q * 2, False)
            accumulate(N_MOV_B, (mgT, 0), 4, ready=lambda k: pe.wait_ge(mg_lo, k + 1))
            accumulate(N_MOV_B + 4, (mgT, 0), 0)
            def keep_clock(n):
                for _ in range(n):
                    mm(ps[7][:, :], ident, cst[:, 0:512], start=True, stop=True)

            def logits(i):
                pe.wait_ge(t2_ev, 2 * i + 2)
                if i >= 2:
                    pe.wait_ge(lg_ev, i - 1)
                for k in range(KD):
                    h = P // 2 * (k % 2)
                    last = mm(ps[4 + 2 * (i % 2)][h:h + N_RT, 0:P], w_rt[:, k, :], hn2T[i][:, k, :],
                              start=k < 2, stop=k >= KD - 2)
                last.then_inc(lg_done, 1)

            keep_clock(3)
            for i in range(NT):
                if i == 1:
                    keep_clock(1)
                for half in range(2):
                    n = 2 * i + half
                    pe.wait_ge(hn2_ok, n + 1)
                    if n >= 4:
                        pe.wait_ge(t2_ev, n - 3)
                    for j in range(4):
                        k = 4 * half + j
                        last = tp(ps[n % 4][:, P * j:P * (j + 1)], hn2[:, i, P * k:P * (k + 1)], ident)
                    last.then_inc(t2_done, 1)
                if i:
                    logits(i - 1)
            logits(NT - 1)
            for i in range(NT):
                pe.wait_ge(lg_ev, i + 1)
                last = mm(ps[5][:, N_RT * i:N_RT * (i + 1)], lgT[:, P * i:P * (i + 1)], fold, start=True, stop=True)
            last.then_inc(folded, 1)
            keep_clock(4)
            pe.wait_ge(flat_ok, 1)
            pe.wait_ge(ch_ok, 1)
            before = ps[0][:, 0:NT * EXPERTS].rearrange("p (i e) -> p i e", i=NT)
            mm(before, tri_r[:, :], chosen[:, :, :], start=True, stop=False)
            for j in range(NT - 1):
                last = mm(before[:, j + 1:NT, :], ones_r[:, :], bc(chosen[:, j:j + 1, :], [P, NT - 1 - j, EXPERTS]),
                          start=False, stop=j == NT - 2)
            last.then_inc(before_done, 1)
            for i in range(NT):
                last = mm(ps[6][:, 0:EXPERTS], ones_r[:, :], chosen[:, i, :], start=i == 0, stop=i == NT - 1)
            last.then_inc(cnt_done, 1)

            def table(n):
                for bank, v in ((7, 0), (5, 2)):
                    if v:
                        pe.wait_ge(weights_in, 1)
                    for ik in range(2 * NT):
                        if not v and ik % NT == 0:
                            pe.wait_ge(tab_in, n * 2 + (1 + ik // NT))
                        last = mm(ps[bank][:, 0:2 * EXPERTS], rank1[:, ik, :],
                                  vals[:, ik, v:v + 2, :].rearrange("p v e -> p (v e)"), start=ik == 0, stop=ik == 2 * NT - 1)
                    last.then_inc(tab_done, 1)

            table(0)

            def turn_rows(s, b, gathers):
                pe.wait_ge(ga[s], gathers)
                xr = xg[s][:, :].rearrange("p (q c) -> p c q", c=4)
                for c in range(4):
                    last = tp(ps[b][:, P * c:P * (c + 1)], xr[:, c, :], ident)
                last.then_inc(t_done, 1)

            def loaded(s, r16):
                return 16 if s == SLOTS else r16 if s == 0 and not (isinstance(r16, int) and r16 == 0) else r16 + 16

            def up_products(s, b, e, r16):
                pe.wait_ge(t_ev, e + 1)
                pe.wait_ge(ld_up[s], loaded(s, r16) * 2)
                for c in range(4):
                    for h in range(2):
                        held = xT[b][:, P * c + CAP * h:P * c + CAP * (h + 1)]
                        for fh in range(2):
                            k = F * c + P * fh
                            last = mm(ps[2 + b][CAP * fh:CAP * (fh + 1), 0:2 * P].rearrange("p (w f) -> p w f", w=2),
                                      held, w13[s][:, :, h, k:k + P],
                                      start=c == 0 and h == 0, stop=c == 3 and h == 1)
                last.then_inc(up2_done, 1)

            def round_(r16, e0, first=False, last_round=False, slot0=0):
                for s in range(SLOTS):
                    b = s % 2
                    if not (last_round and s == SLOTS - 1):
                        up_products(s + 1 if s < SLOTS - 1 else SLOTS if first else 0, 1 - b, e0 + (s + 1),
                                    r16 if s < SLOTS - 1 else r16 + 16)
                    pe.wait_ge(hh_ok, e0 + (s + 1))
                    tp(ps[4 + b][:, 0:P], hh[b][:, :], ident).then_inc(ht_done, 1)
                    pe.wait_ge(ht_ev, e0 + (s + 1))
                    w = slot0 if s == 0 else s
                    pe.wait_ge(ld_dn[w], loaded(w, r16))
                    if not (first and s < 2):
                        pe.wait_ge(y_ev, e0 + (s - 1))
                    for j in range(2):
                        for dh in range(2):
                            last = mm(ps[6 + b][CAP * dh:CAP * (dh + 1), :], hhT[b][:, CAP * j:CAP * (j + 1)],
                                      w2s[w][:, j, 512 * dh:512 * (dh + 1)], start=j == 0, stop=j == 1)
                    last.then_inc(dn_done, 1)
                    if not (last_round and s >= SLOTS - 2):
                        turn_rows((s + 2) % SLOTS, b, r16 + (16 if s < SLOTS - 2 else 32))

            turn_rows(0, 0, 16)
            up_products(0, 0, 0, 0)
            turn_rows(1, 1, 16)
            round_(0, 0, first=True)
            round_(16, SLOTS, slot0=SLOTS)
            with pe.Fori(2, ROUNDS - 1) as r:
                round_(r * 16, r * SLOTS)
            round_(16 * (ROUNDS - 1), SLOTS * (ROUNDS - 1), last_round=True)
            pe.wait_ge(cnt_ok, 1)
            fullest = pe.value_load(cmaxi[0:1, 0:1], min_val=0, max_val=SEQ)
            with pe.If(fullest > CAP):
                with pe.Fori(1, BLOCKS) as blk:
                    with pe.If(fullest > blk * CAP):
                        pe.wait_ge(y_ev, blk * EXPERTS)
                        table(blk)
                        r16 = blk * (16 * ROUNDS)
                        turn_rows(0, 0, r16 + 16)
                        up_products(0, 0, blk * EXPERTS, r16)
                        turn_rows(1, 1, r16 + 16)
                        with pe.Fori(0, ROUNDS - 1) as r:
                            round_(r16 + r * 16, blk * EXPERTS + r * SLOTS)
                        round_(r16 + 16 * (ROUNDS - 1), blk * EXPERTS + SLOTS * (ROUNDS - 1), last_round=True)


_INS = ["x", "meta_tokens", "norm_mix_g", "w_in", "b_forget", "q_norm_g", "k_norm_g", "w_up_attn", "w_pool",
        "pool_scale", "w_up_pool", "w_out", "norm_ffn_g", "w_group", "b_group", "w_router", "b_router", "w1", "w3", "w2"]


def kernel(**inputs):
    import numpy as np
    import concourse.bacc as bacc
    from concourse.bass_utils import run_bass_kernel_spmd

    nc = bacc.Bacc("TRN2", target_bir_lowering=False, num_devices=1)
    arrays, args = {}, []
    given = {name: np.ascontiguousarray(inputs[name]) for name in _INS}
    given.update(constants())
    for name, a in given.items():
        arrays[f"in_{name}"] = a
        args.append(nc.dram_tensor(f"in_{name}", a.shape, mybir.dt.from_np(a.dtype), kind="ExternalInput").ap())
    args.append(nc.dram_tensor("out_0", (1, SEQ, D), F32, kind="ExternalOutput").ap())
    program(nc, *args)
    r = run_bass_kernel_spmd(nc, [arrays], core_ids=[0])
    return r.results[0]["out_0"]
```
